# Optimizing a Trainium2 kernel written in Bass

```python
import jax
import jax.numpy as jnp
from jax import lax
import numpy as np

D_MODEL = 1024
BATCH = 1
SEQ = 512
DEPTH = 2
DEC_BATCH = 1
DEC_SEQ = 32
PAST_LEN = 1024

CHUNK = 64
N_A_LAYERS = DEPTH // 2
N_B_LAYERS = DEPTH - N_A_LAYERS
POOL_WINDOWS = (2, 4, 8, 16)
N_POOL_GROUPS = len(POOL_WINDOWS)
POOL_GROUP_DIM = D_MODEL // N_POOL_GROUPS
POOL_BUF = max(POOL_WINDOWS) - 1
N_HEADS = 16
HEAD_DIM = D_MODEL // N_HEADS
KV_WIDTH = N_HEADS * HEAD_DIM
ATTN_SCALE = HEAD_DIM ** -0.5
QBLOCK = 128
FORGET_BIAS = 2.0
N_EXPERTS = 16
N_EXPERT_GROUPS = 4
EXPERTS_PER_GROUP = N_EXPERTS // N_EXPERT_GROUPS
TOP_K = 2
D_EXPERT = D_MODEL // 2
EPS = 1e-6
NEG_INF = -1e30

kernel_name = 'yoco_pool_fox_moe_stream_step'

def _rms_norm(x, gain):
    xf = x.astype(jnp.float32)
    y = xf * lax.rsqrt(jnp.mean(xf * xf, axis=-1, keepdims=True) + EPS)
    return (y * gain.astype(jnp.float32)).astype(x.dtype)

def _modulate(x, gain, shift, scale):
    return _rms_norm(x, gain) * (1 + scale[:, None, :]) + shift[:, None, :]

def _adaln(c, w, b, n):
    return jnp.split(jax.nn.silu(c) @ w + b, n, axis=-1)

def _pool_mixer(u, hist, start_pos, w_pool, scale):
    B, T, _ = u.shape
    ext = jnp.concatenate([hist.astype(u.dtype), u], axis=1)
    cs = jnp.cumsum(ext.astype(jnp.float32), axis=1)
    cs = jnp.pad(cs, ((0, 0), (1, 0), (0, 0)))
    end = cs[:, POOL_BUF + 1:]
    pos = start_pos + jnp.arange(T)
    means = []
    for g, w in enumerate(POOL_WINDOWS):
        sl = slice(g * POOL_GROUP_DIM, (g + 1) * POOL_GROUP_DIM)
        lo = POOL_BUF + 1 - w
        s = end[..., sl] - cs[:, lo:lo + T, sl]
        cnt = jnp.minimum(pos + 1, w).astype(jnp.float32)[None, :, None]
        means.append(s / cnt)
    pooled = jnp.stack(means, axis=2)
    diff = pooled - u.astype(jnp.float32).reshape(B, T, N_POOL_GROUPS, POOL_GROUP_DIM)
    y = jnp.einsum('btgc,gcd->btgd', diff.astype(u.dtype), w_pool).reshape(B, T, D_MODEL)
    return y * scale, ext[:, -POOL_BUF:]

def _moe(h, w_router, b_router, w_gate, w_up, w_down):
    logits = jnp.einsum('btd,de->bte', h.astype(jnp.float32), w_router.astype(jnp.float32))
    scores = jax.nn.softmax(logits, axis=-1)
    sel = scores + b_router.astype(jnp.float32)
    grouped = sel.reshape(sel.shape[:-1] + (N_EXPERT_GROUPS, EXPERTS_PER_GROUP))
    group_score = jnp.sum(lax.top_k(grouped, TOP_K)[0], axis=-1)
    best = jnp.argmax(group_score, axis=-1)
    in_group = (jnp.arange(N_EXPERTS) // EXPERTS_PER_GROUP) == best[..., None]
    masked = jnp.where(in_group, sel, -jnp.inf)
    _, idx = lax.top_k(masked, TOP_K)
    chosen = jnp.take_along_axis(scores, idx, axis=-1)
    wts = chosen / jnp.sum(chosen, axis=-1, keepdims=True)
    combine = jnp.sum(jax.nn.one_hot(idx, N_EXPERTS, dtype=jnp.float32) * wts[..., None], axis=-2)
    combine = combine.astype(h.dtype)
    y = None
    for e in range(N_EXPERTS):
        act = jax.nn.silu(h @ w_gate[e]) * (h @ w_up[e])
        term = combine[..., e:e + 1] * (act @ w_down[e])
        y = term if y is None else y + term
    return y

def _shared_kv(x, c, past, kv_ada_w, kv_ada_b, kv_norm, w_kvf, b_f, k_norm):
    B, T, _ = x.shape
    shift, scale = _adaln(c, kv_ada_w, kv_ada_b, 2)
    h = _modulate(x, kv_norm, shift, scale)
    proj = h @ w_kvf
    k = _rms_norm(proj[..., :KV_WIDTH].reshape(B, T, N_HEADS, HEAD_DIM), k_norm)
    v = proj[..., KV_WIDTH:2 * KV_WIDTH].reshape(B, T, N_HEADS, HEAD_DIM)
    logf = jax.nn.log_sigmoid((proj[..., 2 * KV_WIDTH:] + b_f).astype(jnp.float32))
    if past is None:
        f_new = jnp.cumsum(logf, axis=1)
        past_segs = []
    else:
        ck, cv, clogf = past
        P = ck.shape[1]
        f_all = jnp.cumsum(jnp.concatenate([clogf.astype(jnp.float32), logf], axis=1), axis=1)
        past_segs = [(ck, cv, f_all[:, :P], jnp.arange(P))]
        f_new = f_all[:, P:]
    return k, v, logf, f_new, past_segs

def _fox_attend(q, fq, pos_q, segments):
    fq_t = jnp.swapaxes(fq, 1, 2)[..., :, None]
    logits, vals = [], []
    for k, v, fk, pos_k in segments:
        s = jnp.einsum('bqhd,bkhd->bhqk', q, k).astype(jnp.float32) * ATTN_SCALE
        s = s + fq_t - jnp.swapaxes(fk, 1, 2)[..., None, :]
        s = jnp.where(pos_k[None, None, None, :] <= pos_q[None, None, :, None], s, NEG_INF)
        logits.append(s)
        vals.append(v)
    p = jax.nn.softmax(jnp.concatenate(logits, axis=-1), axis=-1)
    out = None
    off = 0
    for v in vals:
        n = v.shape[1]
        term = jnp.einsum('bhqk,bkhd->bqhd', p[..., off:off + n].astype(v.dtype), v)
        out = term if out is None else out + term
        off += n
    return out

def _fox_mixer(h, shared, start_pos, w_q, q_norm, w_o):
    B, T, _ = h.shape
    k, v, _, f_new, past_segs = shared
    q = _rms_norm((h @ w_q).reshape(B, T, N_HEADS, HEAD_DIM), q_norm)
    pos = start_pos + jnp.arange(T)
    outs = []
    for i in range(0, T, QBLOCK):
        e = min(i + QBLOCK, T)
        segs = past_segs + [(k[:, :e], v[:, :e], f_new[:, :e], pos[:e])]
        outs.append(_fox_attend(q[:, i:e], f_new[:, i:e], pos[i:e], segs))
    o = jnp.concatenate(outs, axis=1).reshape(B, T, KV_WIDTH)
    return o @ w_o

def _trunk(x, c, pool_hist, start_pos, past, ada_w, ada_b, norm_g, w_pool, pool_scale,
           kv_ada_w, kv_ada_b, kv_norm, w_kvf, b_f, k_norm, w_q, q_norm, w_o,
           w_router, b_router, w_gate, w_up, w_down):
    new_hist = []
    shared = None
    for layer in range(DEPTH):
        sh1, sc1, g1, sh2, sc2, g2 = _adaln(c, ada_w[layer], ada_b[layer], 6)
        if layer < N_A_LAYERS:
            h = _modulate(x, norm_g[layer, 0], sh1, sc1)
            y, hist = _pool_mixer(h, pool_hist[layer], start_pos, w_pool[layer], pool_scale[layer])
            new_hist.append(hist)
        else:
            if shared is None:
                shared = _shared_kv(x, c, past, kv_ada_w, kv_ada_b, kv_norm, w_kvf, b_f, k_norm)
            j = layer - N_A_LAYERS
            h = _modulate(x, norm_g[layer, 0], sh1, sc1)
            y = _fox_mixer(h, shared, start_pos, w_q[j], q_norm[j], w_o[j])
        x = x + g1[:, None, :] * y
        h = _modulate(x, norm_g[layer, 1], sh2, sc2)
        x = x + g2[:, None, :] * _moe(h, w_router, b_router, w_gate[layer], w_up[layer], w_down[layer])
    return x, jnp.stack(new_hist), shared[0], shared[1], shared[2]

def setup_inputs(seed: int = 0) -> dict:
    key = jax.random.key(seed)
    ks = jax.random.split(key, 32)

    def nrm(k, shape, s):
        return s * jax.random.normal(k, shape, jnp.float32)

    return {
        'x_prompt': nrm(ks[0], (BATCH, SEQ, D_MODEL), 1.0),
        'x_sample': nrm(ks[1], (DEC_BATCH, DEC_SEQ, D_MODEL), 1.0),
        'cache_pool': nrm(ks[2], (N_A_LAYERS, DEC_BATCH, POOL_BUF, D_MODEL), 1.0),
        'cache_k': nrm(ks[3], (DEC_BATCH, PAST_LEN, N_HEADS, HEAD_DIM), 1.0),
        'cache_v': nrm(ks[4], (DEC_BATCH, PAST_LEN, N_HEADS, HEAD_DIM), 1.0),
        'cache_logf': jax.nn.log_sigmoid(FORGET_BIAS + nrm(ks[5], (DEC_BATCH, PAST_LEN, N_HEADS), 0.5)),
        'c_prompt': nrm(ks[6], (BATCH, D_MODEL), 1.0),
        'c_sample': nrm(ks[7], (DEC_BATCH, D_MODEL), 1.0),
        'ada_w': nrm(ks[8], (DEPTH, D_MODEL, 6 * D_MODEL), 0.5 * D_MODEL ** -0.5),
        'ada_b': nrm(ks[9], (DEPTH, 6 * D_MODEL), 0.02),
        'norm_g': 1.0 + nrm(ks[10], (DEPTH, 2, D_MODEL), 0.02),
        'w_pool': nrm(ks[11], (N_A_LAYERS, N_POOL_GROUPS, POOL_GROUP_DIM, POOL_GROUP_DIM), POOL_GROUP_DIM ** -0.5),
        'pool_scale': 1.0 + nrm(ks[12], (N_A_LAYERS, D_MODEL), 0.1),
        'kv_ada_w': nrm(ks[13], (D_MODEL, 2 * D_MODEL), 0.5 * D_MODEL ** -0.5),
        'kv_ada_b': nrm(ks[14], (2 * D_MODEL,), 0.02),
        'kv_norm': 1.0 + nrm(ks[15], (D_MODEL,), 0.02),
        'w_kvf': nrm(ks[16], (D_MODEL, 2 * KV_WIDTH + N_HEADS), D_MODEL ** -0.5),
        'b_f': FORGET_BIAS + nrm(ks[17], (N_HEADS,), 0.5),
        'k_norm': 1.0 + nrm(ks[18], (HEAD_DIM,), 0.02),
        'w_q': nrm(ks[19], (N_B_LAYERS, D_MODEL, KV_WIDTH), D_MODEL ** -0.5),
        'q_norm': 1.0 + nrm(ks[20], (N_B_LAYERS, HEAD_DIM), 0.02),
        'w_o': nrm(ks[21], (N_B_LAYERS, KV_WIDTH, D_MODEL), KV_WIDTH ** -0.5),
        'w_router': nrm(ks[22], (D_MODEL, N_EXPERTS), D_MODEL ** -0.5),
        'b_router': nrm(ks[23], (N_EXPERTS,), 0.01),
        'w_gate': nrm(ks[24], (DEPTH, N_EXPERTS, D_MODEL, D_EXPERT), D_MODEL ** -0.5),
        'w_up': nrm(ks[25], (DEPTH, N_EXPERTS, D_MODEL, D_EXPERT), D_MODEL ** -0.5),
        'w_down': nrm(ks[26], (DEPTH, N_EXPERTS, D_EXPERT, D_MODEL), D_EXPERT ** -0.5),
    }

def reference(x_prompt, x_sample, cache_pool, cache_k, cache_v, cache_logf, c_prompt, c_sample,
              ada_w, ada_b, norm_g, w_pool, pool_scale, kv_ada_w, kv_ada_b, kv_norm, w_kvf, b_f,
              k_norm, w_q, q_norm, w_o, w_router, b_router, w_gate, w_up, w_down):
    assert x_sample.shape[1] <= CHUNK
    hist0 = jnp.zeros((N_A_LAYERS, x_prompt.shape[0], POOL_BUF, D_MODEL), x_prompt.dtype)
    y_prompt, pool_prompt, k_prompt, v_prompt, logf_prompt = _trunk(
        x_prompt, c_prompt, hist0, 0, None,
        ada_w, ada_b, norm_g, w_pool, pool_scale, kv_ada_w, kv_ada_b, kv_norm, w_kvf, b_f,
        k_norm, w_q, q_norm, w_o, w_router, b_router, w_gate, w_up, w_down)
    y_sample, pool_sample, k_sample, v_sample, logf_sample = _trunk(
        x_sample, c_sample, cache_pool, cache_k.shape[1], (cache_k, cache_v, cache_logf),
        ada_w, ada_b, norm_g, w_pool, pool_scale, kv_ada_w, kv_ada_b, kv_norm, w_kvf, b_f,
        k_norm, w_q, q_norm, w_o, w_router, b_router, w_gate, w_up, w_down)
    return (y_prompt, y_sample, pool_prompt, k_prompt, v_prompt, logf_prompt,
            pool_sample, k_sample, v_sample, logf_sample)


_drawn_inputs = setup_inputs


def setup_inputs(seed=0):
    import zlib

    import numpy as np

    out = dict(_drawn_inputs(seed))
    spreads = {}
    factors = {'cache_logf': 8.0, 'k_norm': 2.834, 'q_norm': 8.0}
    for name, (base, spread) in spreads.items():
        noise = np.random.default_rng([zlib.crc32(name.encode()), seed]).standard_normal(out[name].shape)
        drawn = base * np.exp(spread * noise) if base else spread * noise
        out[name] = jnp.asarray(drawn.astype(out[name].dtype))
    for name, factor in factors.items():
        out[name] = (out[name] * factor).astype(out[name].dtype)
    return out
```

```python
import concourse.bass as bass
from concourse import mybir
from contextlib import ExitStack



def bass_yoco_stream_step(
    nc, x_prompt, x_sample, cache_pool, cache_k, cache_v, cache_logf, c_prompt, c_sample,
    ada_w, ada_b, norm_g, w_pool, pool_scale, kv_ada_w, kv_ada_b, kv_norm, w_kvf, b_f,
    k_norm, w_q, q_norm, w_o, w_router, b_router, w_gate, w_up, w_down,
    y_prompt, y_sample, pool_prompt, k_prompt, v_prompt, logf_prompt,
    pool_sample, k_sample, v_sample, logf_sample,
):
    fp32, bf16, i32 = mybir.dt.float32, mybir.dt.bfloat16, mybir.dt.int32
    ALU, ACT, AX = mybir.AluOpType, mybir.ActivationFunctionType, mybir.AxisListType

    P = 128
    D = x_prompt.shape[2]
    SEQ, DEC = x_prompt.shape[1], x_sample.shape[1]
    PAST = cache_k.shape[1]
    NH, HD = cache_k.shape[2], cache_k.shape[3]
    NE = w_router.shape[1]
    NG, EPG = 4, 4
    DE = w_gate.shape[3]
    NPG = w_pool.shape[1]
    PGD = D // NPG
    WINDOWS = (2, 4, 8, 16)
    PBUF = cache_pool.shape[2]
    EPS, NEG = 1e-6, -1e30
    KC = D // P
    KE = DE // P
    TP = SEQ // P
    TS = TP
    NT = TP + 1
    TOK = SEQ + DEC
    NPAIR = NH // 2
    CT = PAST // P
    NF = TP + CT + 1
    SCALE = HD ** -0.5
    rows = [P] * TP + [DEC]
    col = [t * P for t in range(NT)]

    NASSIGN = 2 * TOK
    NOV = NASSIGN // P
    XROWS = NASSIGN + P
    YROWS = NE * P + NOV * P

    ada_d = nc.dram_tensor("ada_d", (2, 14 * D), fp32, kind="Internal").ap()
    xs_d = nc.dram_tensor("xs_d", (XROWS, D), fp32, kind="Internal").ap()
    ys_d = nc.dram_tensor("ys_d", (YROWS, D), fp32, kind="Internal").ap()
    f_d = nc.dram_tensor("f_d", (NF * NH, P), fp32, kind="Internal").ap()

    NADA = 28
    ada_src = []
    for grp in range(7):
        w, c0 = (ada_w[0], grp * 2048) if grp < 3 else (kv_ada_w, 0) if grp == 3 else (ada_w[1], (grp - 4) * 2048)
        v = w.rearrange("(p k) n -> p k n", k=KC)
        ada_src += [v[:, 2 * u:2 * u + 2, c0:c0 + 2048] for u in range(4)]
    kvf_v = w_kvf.rearrange("(p k) n -> p k n", k=KC)
    q_v = w_q[0].rearrange("(p k) n -> p k n", k=KC)
    o_v = w_o[0].rearrange("(p k) n -> p k n", k=KC)
    proj_src = ([kvf_v[:, :, 512 * c:512 * (c + 1)] for c in range(4)]
                + [q_v[:, :, 512 * c:512 * (c + 1)] for c in range(2)]
                + [o_v[:, :, 512 * c:512 * (c + 1)] for c in range(2)])
    wg_v = w_gate.rearrange("l e (p k) f -> (l e) p (k f)", k=KC)
    wu_v = w_up.rearrange("l e (p k) f -> (l e) p (k f)", k=KC)
    wd_v = w_down.rearrange("l e (p k) f -> (l e) p (k f)", k=KE)
    G_SLOT, U_SLOT, D_SLOT = 0, 2, 4
    NPE = NE // 2

    ada_slot = [n % 6 for n in range(NADA)]
    before0 = [ada_slot.count(s) for s in range(6)]
    before_proj = [n + NPE for n in before0]
    before1 = [n + (3, 4, 0, 0, 0, 0)[s] for s, n in enumerate(before_proj)]
    MOE_BEFORE = [before0, before1]

    ctx = ExitStack()
    with ctx:
        def sb(name, shape, dt=fp32):
            return ctx.enter_context(nc.sbuf_tensor(name, shape, dt))

        def sem(name):
            return ctx.enter_context(nc.semaphore(name))

        x = sb("x", [P, NT, D])
        h = sb("h", [P, NT, D])
        hT_raw = sb("hT_raw", [P, KC * TOK])
        ring = sb("ring", [P, 6, 4096])
        mod = sb("mod", [P, 3, 2, D])
        gainb = sb("gainb", [P, D])
        hT = hT_raw[:, :].rearrange("p (k t) -> p k t", k=KC)
        partT = hT_raw[:, 0:TOK]
        wpool = hT_raw[:, 0:2048].rearrange("p (g k n) -> p g k n", g=NPG, k=2)
        cachep = hT_raw[:, 2048:3072]
        diffT = hT_raw[:, 3072:4096].rearrange("p (c t) -> p c t", c=KC)
        cnti, wtmp = hT_raw[:, 4096:4224], hT_raw[:, 4224:4352]
        hf = h[:, :, :].rearrange("p t d -> p (t d)")
        xg = hf[:, 0:2048].rearrange("p (b n) -> p b n", b=2)
        xgT = hf[:, 2048:4096].rearrange("p (b k t) -> p b k t", b=2, k=KC)
        sg = hf[:, 4096:4608]
        hact = hf[:, 4608:5120]
        hactT = hT_raw[:, 0:512].rearrange("p (k t) -> p k t", k=KE)
        ysb = hT_raw[:, 512:2560].rearrange("p (b n) -> p b n", b=2)
        rf = ring[:, :, :].rearrange("p s n -> p (s n)")
        kk = rf[:, 8192:8192 + NT * D].rearrange("p (t d) -> p t d", t=NT)
        qq = rf[:, 13312:13312 + NT * D].rearrange("p (t d) -> p t d", t=NT)
        vv = rf[:, 18432:18432 + NT * D].rearrange("p (t d) -> p t d", t=NT)
        yg = rf[:, 8192:8192 + NT * 2 * D].rearrange("p (t r n) -> p t r n", t=NT, r=2)
        kT = hT
        qT = hf[:, 0:KC * TOK].rearrange("p (k t) -> p k t", k=KC)
        nfb = rf[:, 8192:8192 + NH * SEQ].rearrange("p (h t k) -> p h t k", h=NH, t=TP)
        oo = rf[:, 0:NT * D].rearrange("p (t d) -> p t d", t=NT)
        qz = rf[:, 5120:5120 + 2 * SEQ].rearrange("p (s t) -> p s t", s=2)
        S_sb = rf[:, 6144:8192].rearrange("p (b n) -> p b n", b=4)
        mf = mod[:, :, :, :].rearrange("p a s d -> p (a s d)")
        PT = rf[:, 23552:24576].rearrange("p (b n) -> p b n", b=2)
        ck = [v.rearrange("p (t n) -> p t n", t=CT) for v in (mf[:, 0:2048], rf[:, 16384:18432])]
        cv = [v.rearrange("p (t n) -> p t n", t=CT) for v in (mf[:, 2048:4096], rf[:, 8192:10240])]
        bias_s = [mf[:, 4096:4096 + (CT + 1) * P], rf[:, 10240:10240 + (CT + 1) * P]]
        kTc = rf[:, 11392:13440].rearrange("p (a n) -> p a n", a=2)
        SK = PAST + DEC
        Ss = rf[:, 6144:6144 + SK]
        wo_first = hf[:, 0:4096]
        PTs = rf[:, 13440:13440 + (CT + 1) * P].rearrange("p (t n) -> p t n", t=CT + 1)

        ident = sb("ident", [P, P])
        identb = sb("identb", [P, P], bf16)
        causal = sb("causal", [P, P], bf16)
        smask = sb("smask", [P, DEC])
        tri_s = sb("tri_s", [P, P])
        tri_i = sb("tri_i", [P, P])
        ones = sb("ones", [P, P])
        bands = sb("bands", [P, 3, NPG, P])
        wrf = sb("wrf", [P, KC, 2, NE])
        sel = sb("sel", [P, 2, NE])
        stage = sb("stage", [P, 2, 512])
        adab = sb("adab", [P, 2, 512])
        cs = sb("cs", [P, 2, KC])
        csl = sb("csl", [P, 2, KC])
        cT = sb("cT", [P, KC, 32])
        ssq = sb("ssq", [P, NT])
        rstd = sb("rstd", [P, NT])
        brb = sb("brb", [P, NE])
        bfb = sb("bfb", [P, NH])
        knb = sb("knb", [P, HD])
        qnb = sb("qnb", [P, HD])
        valid = sb("valid", [P, NT])
        desc4 = sb("desc4", [P, 4])
        iotae = sb("iotae", [P, NE])
        iotaj = sb("iotaj", [P, NOV])
        L = sb("L", [P, NT, NE])
        sc = sb("sc", [P, NT, NE])
        selv = sb("selv", [P, NT, NE])
        pm = sb("pm", [P, 4, NT * NG, 2])
        m4 = sb("m4", [P, 4, NT, 4])
        best = sb("best", [P, NT, NG])
        vj = sb("vj", [P, NT, EPG])
        one = sb("one", [P, 2, NT, EPG])
        oh = sb("oh", [P, 2, NT, NE])
        Mb = sb("Mb", [P, NT, NE])
        t5 = sb("t5", [P, 8, NT])
        wts = sb("wts", [P, 2, NT])
        tot = sb("tot", [P, NT, NE])
        rank = sb("rank", [P, NT, NE])
        cnt = sb("cnt", [P, NE])
        offs = sb("offs", [P, NE])
        ovc = sb("ovc", [P, NE])
        ovs = sb("ovs", [P, NE])
        e16 = sb("e16", [P, 4, NE])
        nfh = gainb[:, :].rearrange("p (s k) -> p s k", s=2)
        onesr = sb("onesr", [P, NE])
        prod = sb("prod", [P, NT, NE])
        posf = sb("posf", [P, 2, 2, NT])
        posi = sb("posi", [P, 2, 2, NT], i32)
        tabf = sb("tabf", [P, NE + 2 * NOV + 1])
        tabi = sb("tabi", [P, NE + 2 * NOV + 1], i32)
        LF = sb("LF", [P, NF, NH])
        fqs = sb("fqs", [P, 4])
        mx = sb("mx", [P, 8, 4])
        rs = sb("rs", [P, 8, 2])
        bandf = bands[:, :, :, :].rearrange("p a g n -> p (a g n)")
        Fs = bandf[:, 0:NF * NH].rearrange("p (t n) -> p t n", t=NF)
        tF = bandf[:, 256:256 + NF * NH].rearrange("p (t n) -> p t n", t=NF)
        fT = bandf[:, 512:768].rearrange("p (a n) -> p a n", a=2)
        z = bandf[:, 768:768 + NT * NH].rearrange("p (t n) -> p t n", t=NT)
        za = bandf[:, 896:896 + NT * NH].rearrange("p (t n) -> p t n", t=NT)
        ss = bandf[:, 1024:1024 + NT * NH].rearrange("p (t n) -> p t n", t=NT)
        qbs = stage[:, 1, 0:128].rearrange("p (a q) -> p a q", a=2)
        kns = stage[:, 1, 128:192].rearrange("p (a t) -> p a t", a=2)
        ind = bandf[:, 1104:1104 + 3 * NOV * NE].rearrange("p (a j e) -> p a j e", a=3, j=NOV)
        qbd = stage[:, 0, :].rearrange("p (j a q) -> p j a q", j=NPAIR, a=2)
        pb = [ctx.enter_context(nc.psum_tensor(f"pb{i}", [P, 512], fp32)) for i in range(8)]

        consts = sem("consts")
        bands_ready = sem("bands_ready")
        cachep_zero = sem("cachep_zero")
        cachep_loaded = sem("cachep_loaded")
        ident_ready = sem("ident_ready")
        slot_loaded = [sem(f"slot{i}_loaded") for i in range(6)]
        unit_used = sem("unit_used")
        x_loaded = sem("x_loaded")
        small_loaded = sem("small_loaded")
        tail_stored = sem("tail_stored")
        c_loaded = sem("c_loaded")
        c_silu = sem("c_silu")
        c_ready = sem("c_ready")
        bias_loaded = [sem(f"adab{i}_loaded") for i in range(2)]
        ada_staged = sem("ada_staged")
        ada_stored = [sem(f"ada{i}_stored") for i in range(7)]
        ab_loaded = sem("ab_loaded")
        a_ready = sem("a_ready")
        g_loaded = sem("g_loaded")
        gp_ready = sem("gp_ready")
        adab_zero = sem("adab_zero")
        qk_sq = sem("qk_sq")
        qk_ms = sem("qk_ms")
        at_nf = sem("at_nf")
        g_free = sem("g_free")
        squares = sem("squares")
        ms_ready = sem("ms_ready")
        root_ready = sem("root_ready")
        h_ready = sem("h_ready")
        mix_diff = sem("mix_diff")
        mix_diffT = sem("mix_diffT")
        mix_y = sem("mix_y")
        mix_added = sem("mix_added")
        hist_stored = sem("hist_stored")
        tr_done = sem("tr_done")
        tr_act = sem("tr_act")
        tr_dve = sem("tr_dve")
        logits_done = sem("logits_done")
        l_ready = sem("l_ready")
        exp_ready = sem("exp_ready")
        pick_ready = sem("pick_ready")
        rank_done = sem("rank_done")
        pos_ready = sem("pos_ready")
        scattered = sem("scattered")
        xg_loaded = [sem(f"xg{i}_loaded") for i in range(2)]
        y_stored = [sem(f"y{i}_stored") for i in range(2)]
        yg_loaded = [sem(f"yg{i}_loaded") for i in range(NT)]
        combined = sem("combined")
        yg_scaled = sem("yg_scaled")
        out_stored = sem("out_stored")
        chain_v = sem("chain_v")
        chain_a = sem("chain_a")
        chain_p = sem("chain_p")
        proj_done = sem("proj_done")
        proj_act = sem("proj_act")
        proj_dve = sem("proj_dve")
        f_done = sem("f_done")
        wo_loaded = sem("wo_loaded")
        part_done = sem("part_done")
        part_copied = sem("part_copied")
        f_abs = sem("f_abs")
        f_exp = sem("f_exp")
        f_1p = sem("f_1p")
        f_ln = sem("f_ln")
        lf_ready = sem("lf_ready")
        clogf_loaded = sem("clogf_loaded")
        csum_done = sem("csum_done")
        F_ready = sem("F_ready")
        fT_done = sem("fT_done")
        fT_ready = sem("fT_ready")
        f_stored = sem("f_stored")
        nfb_loaded = sem("nfb_loaded")
        kv_out = sem("kv_out")
        qk_ss = sem("qk_ss")
        qk_root = sem("qk_root")
        qk_ready = sem("qk_ready")
        at_q = sem("at_q")
        at_s = sem("at_s")
        at_add = sem("at_add")
        at_nb = sem("at_nb")
        at_exp = sem("at_exp")
        at_rinv = sem("at_rinv")
        at_t = sem("at_t")
        at_pt = sem("at_pt")
        at_pv = sem("at_pv")
        at_o = sem("at_o")
        at_chain = sem("at_chain")
        sa_loaded = [sem(f"sa{i}_loaded") for i in range(2)]
        sa_q = sem("sa_q")
        sa_kt = sem("sa_kt")
        sa_kte = sem("sa_kte")
        sa_s = sem("sa_s")
        sa_nb = sem("sa_nb")
        sa_exp = sem("sa_exp")
        sa_rinv = sem("sa_rinv")
        sa_t = sem("sa_t")
        sa_pt = sem("sa_pt")
        sa_pv = sem("sa_pv")
        sa_o = sem("sa_o")
        sa_chain = sem("sa_chain")
        passed_sp = sem("passed_sp")
        passed_dve = sem("passed_dve")
        norm_mul = sem("norm_mul")
        o_done = sem("o_done")
        o_added = sem("o_added")

        class ExpertSems:

            def __init__(self, name):
                self.tx = sem(name + "_tx")
                self.xt_act = sem(name + "_xt_act")
                self.xt_dve = sem(name + "_xt_dve")
                self.gate = sem(name + "_gate")
                self.up = sem(name + "_up")
                self.silu = sem(name + "_silu")
                self.hact = sem(name + "_hact")
                self.th = sem(name + "_th")
                self.hactT = sem(name + "_hactT")
                self.down = sem(name + "_down")
                self.ys_act = sem(name + "_ys_act")
                self.ys_dve = sem(name + "_ys_dve")

        E = ExpertSems("ex")

        ov_w = [sem(f"ov{i}_w") for i in range(2)]
        ov_x = [sem(f"ov{i}_x") for i in range(2)]
        ov_y = [sem(f"ov{i}_y") for i in range(2)]
        ov_pe = [sem(f"ov{i}_pe") for i in range(2)]
        ov_act = [sem(f"ov{i}_act") for i in range(2)]
        ov_dve = [sem(f"ov{i}_dve") for i in range(2)]

        def bc(ap, n, axis):
            a = ap.unsqueeze(axis)
            shape = list(a.shape)
            shape[axis] = n
            return a.to_broadcast(shape)

        block = ctx.enter_context(nc.Block())

        STAGES = [(0, 1, norm_g[0, 0]), (3, 4, norm_g[0, 1]), (6, 7, kv_norm), (8, 9, norm_g[1, 0]),
                  (11, 12, norm_g[1, 1])]
        GATES = [2, 5, 10, 13]
        SMALL = 16 * 7
        NORM_DONE = [NT * (m + 1) for m in range(5)]
        TRN = 2 * NT

        @block.sync
        def _(sp):
            def load(slot, src):
                dst = ring[:, slot, :]
                if len(src.shape) == 3:
                    dst = dst.rearrange("p (k n) -> p k n", k=src.shape[1])
                sp.dma_start(dst, src).then_inc(slot_loaded[slot], 16)

            sp.dma_start(cs[:, 0, :], c_prompt[0].rearrange("(p k) -> p k", k=KC)).then_inc(c_loaded, 16)
            sp.dma_start(cs[:, 1, :], c_sample[0].rearrange("(p k) -> p k", k=KC)).then_inc(c_loaded, 16)
            load(0, ada_src[0])
            load(1, ada_src[1])
            for t in range(TP):
                sp.dma_start(x[:, t, :], x_prompt[0, t * P:(t + 1) * P, :]).then_inc(x_loaded, 16)
            sp.dma_start(x[0:DEC, TS, :], x_sample[0]).then_inc(x_loaded, 16)
            for n in range(2, NADA):
                if n >= 6:
                    sp.wait_ge(unit_used, n - 5)
                if n >= 4:
                    sp.wait_ge(slot_loaded[ada_slot[n - 2]], 16 * ((n - 2) // 6 + 1))
                load(ada_slot[n], ada_src[n])

            def experts(layer):
                e0 = layer * NE

                def w(view, e):
                    return view[e0 + e] if isinstance(e, int) else \
                        view[bass.ds(e + e0, 1), :, :].rearrange("o p n -> p (o n)")

                def first(kind, e):
                    view, slot = {"g": (wg_v, G_SLOT + e), "u": (wu_v, U_SLOT + e), "d": (wd_v, D_SLOT + e)}[kind]
                    if layer == 0:
                        last = max(n for n in range(NADA) if ada_slot[n] == slot)
                        sp.wait_ge(unit_used, last + 1)
                    elif slot == 1:
                        sp.wait_ge(o_done, 2 * NT)
                    else:
                        sp.wait_ge(tr_done, 2 * NT * 6)
                    load(slot, w(view, e))

                def turn(e, par):
                    sp.wait_ge(E.gate, e + (e0 - 1))
                    load(G_SLOT + par, w(wg_v, e))
                    sp.wait_ge(E.down, 2 * e + (2 * e0 - 4))
                    load(D_SLOT + 1 - par, w(wd_v, e - 1))
                    sp.wait_ge(E.up, e + (e0 - 1))
                    load(U_SLOT + par, w(wu_v, e))

                order = ["g0", "u0", "g1", "d0", "u1"] if layer == 0 else ["g0", "u0", "d0", "u1", "g1"]
                for n, (kind, e) in enumerate(order):
                    if layer == 0 and n == 2:
                        sp.wait_ge(xg_loaded[1], 16)
                    first(kind, int(e))
                sp.wait_ge(E.gate, e0 + 1)
                load(G_SLOT, w(wg_v, 2))
                first("d", 1)
                sp.wait_ge(E.up, e0 + 1)
                load(U_SLOT, w(wu_v, 2))
                turn(3, 1)
                with sp.Fori(2, NPE) as i:
                    turn(2 * i, 0)
                    turn(2 * i + 1, 1)
                sp.wait_ge(E.down, 2 * (e0 + NE - 2))
                load(D_SLOT + 1, w(wd_v, NE - 1))
                sp.wait_ge(pos_ready, layer + 1)
                n_ov = sp.value_load(tabi[0:1, NE + 2 * NOV:NE + 2 * NOV + 1], min_val=0, max_val=NOV)
                with sp.If(n_ov > 0):
                    sp.wait_ge(E.down, 2 * (e0 + NE))
                    with sp.Fori(0, n_ov) as j:
                        e = sp.value_load(tabi[0:1, bass.ds(j + NE, 1)], min_val=0, max_val=NE - 1)
                        for view, slot in ((wg_v, G_SLOT), (wu_v, U_SLOT), (wd_v, D_SLOT)):
                            sp.dma_start(ring[:, slot, :], w(view, e)).then_inc(ov_w[layer], 16)
                        sp.wait_ge(ov_y[layer], 16 * j + 16)
                        sp.sem_inc(passed_sp, 1)

            experts(0)
            for n in range(6):
                if n < 2:
                    sp.wait_ge(E.gate, NE - 1 + n)
                else:
                    sp.wait_ge(proj_done, NT * (n - 1))
                load(n % 2, proj_src[n])
            sp.wait_ge(proj_act, 2 * NT)
            sp.wait_ge(proj_dve, 2 * NT)
            sp.dma_start(v_prompt[0].rearrange("(t p) h d -> p t (h d)", p=P), vv[:, 0:TP, :]).then_inc(kv_out, 16)
            sp.dma_start(v_sample[0].rearrange("p h d -> p (h d)"), vv[0:DEC, TS, :]).then_inc(kv_out, 16)
            sp.wait_ge(lf_ready, 1)
            sp.dma_start(logf_prompt[0].rearrange("(t p) h -> p t h", p=P), LF[:, 0:TP, :]).then_inc(kv_out, 16)
            sp.dma_start(logf_sample[0], LF[0:DEC, NF - 1, :]).then_inc(kv_out, 16)
            sp.wait_ge(qk_ready, NT)
            sp.dma_start(k_prompt[0].rearrange("(t p) h d -> p t (h d)", p=P), kk[:, 0:TP, :]).then_inc(kv_out, 16)
            sp.dma_start(k_sample[0].rearrange("p h d -> p (h d)"), kk[0:DEC, TS, :]).then_inc(kv_out, 16)
            sp.wait_ge(at_o, TP * NH)
            sp.dma_start(wo_first.rearrange("p (k n) -> p k n", k=KC), proj_src[6]).then_inc(wo_loaded, 16)
            sp.wait_ge(tr_done, 2 * NT * 6)
            load(1, proj_src[7])
            experts(1)
            for t in range(NT):
                sp.wait_ge(combined, NT + t + 1)
                dst = y_prompt[0, t * P:(t + 1) * P, :] if t < TP else y_sample[0]
                sp.dma_start(dst, x[0:rows[t], t, :]).then_inc(out_stored, 16)
            sp.wait_ge(kv_out, 16 * 6)
            sp.wait_ge(hist_stored, 32)
            sp.wait_ge(out_stored, 16 * NT)

        @block.gpsimd
        def _(pool):
            g = nc.gpsimd
            count = [0]

            def link(ins):
                count[0] += 1
                ins.then_inc(chain_p, 1)
                pool.wait_ge(chain_p, count[0])

            def fill_where(m, cmp, fill, base, pattern, cm):
                return g.affine_select(out=m, in_=m, compare_op=cmp, fill=fill, base=base,
                                       pattern=pattern, channel_multiplier=cm)

            link(g.memset(ident[:, :], 0.0))
            link(fill_where(ident[:, :], ALU.not_equal, 1.0, 0, [[-1, P]], 1))
            link(g.memset(bands[:, :, :, :], 0.0))
            for i, w in enumerate(WINDOWS):
                link(g.memset(bands[:, 0, i, :], 1.0 / w))
                link(fill_where(bands[:, 0, i, :], ALU.is_ge, 0.0, 0, [[1, P]], -1))
                link(fill_where(bands[:, 0, i, :], ALU.is_ge, 0.0, w - 1, [[-1, P]], 1))
                link(g.memset(bands[:, 2, i, :], 1.0 / w))
                link(fill_where(bands[:, 2, i, :], ALU.is_ge, 0.0, w - 1 - P, [[-1, P]], 1))
                link(g.memset(bands[:, 1, i, :], 1.0))
                link(fill_where(bands[:, 1, i, :], ALU.is_ge, 0.0, 0, [[1, P]], -1))
                link(fill_where(bands[:, 1, i, :], ALU.is_ge, 0.0, w - 1, [[-1, P]], 1))
            link(g.iota(cnti[:, :], pattern=[[1, P]], base=1, channel_multiplier=0,
                        allow_small_or_imprecise_dtypes=True))
            link(g.memset(tri_s[:, :], 1.0))
            link(g.memset(tri_i[:, :], 1.0))
            link(fill_where(tri_s[:, :], ALU.is_gt, 0.0, 0, [[1, P]], -1))
            link(fill_where(tri_i[:, :], ALU.is_ge, 0.0, 0, [[1, P]], -1))
            link(g.memset(ones[:, :], 1.0))
            link(g.memset(causal[:, :], 0.0))
            link(fill_where(causal[:, :], ALU.is_ge, NEG, 0, [[-1, P]], 1))
            link(g.memset(smask[:, :], 0.0))
            for j in range(4):
                part = smask[32 * j:32 * j + 32, :]
                link(fill_where(part, ALU.is_ge, NEG, 0, [[-1, DEC]], 1))
            link(g.memset(valid[:, :], 1.0))
            link(fill_where(valid[:, TS:TS + 1], ALU.is_ge, 0.0, DEC - 1, [[0, 1]], -1))
            link(g.iota(iotae[:, :], pattern=[[1, NE]], base=0, channel_multiplier=0,
                        allow_small_or_imprecise_dtypes=True))
            link(g.iota(iotaj[:, :], pattern=[[1, NOV]], base=0, channel_multiplier=0,
                        allow_small_or_imprecise_dtypes=True))
            link(g.iota(desc4[:, :], pattern=[[-1, 4]], base=4, channel_multiplier=0,
                        allow_small_or_imprecise_dtypes=True))
            link(g.memset(onesr[:, :], 1.0))
            g.memset(LF[:, :, :], 0.0).then_inc(consts, 1)

            def load_ab(m):
                shift, scale, gain = STAGES[m]
                if m:
                    pool.wait_ge(h_ready, NORM_DONE[m - 1])
                for v in (shift, scale):
                    pool.wait_ge(ada_stored[v // 2], 32)
                for v, a in ((scale, 0), (shift, 1)):
                    g.dma_start(mod[:, a, 0, :], ada_d[0:1, v * D:(v + 1) * D].to_broadcast([P, D])).then_inc(ab_loaded, 16)
                    g.dma_start(mod[0:DEC, a, 1, :], ada_d[1:2, v * D:(v + 1) * D].to_broadcast([DEC, D])).then_inc(ab_loaded, 16)
                if m:
                    pool.wait_ge(a_ready, m)
                if m == 1:
                    pool.wait_ge(gp_ready, 1)
                g.dma_start(gainb[:, :], gain.unsqueeze(0).to_broadcast([P, D])).then_inc(ab_loaded, 16)

            def load_g(i):
                v = GATES[i]
                pool.wait_ge(ada_stored[v // 2], 32)
                if i:
                    pool.wait_ge(g_free, i)
                g.dma_start(mod[:, 2, 0, :], ada_d[0:1, v * D:(v + 1) * D].to_broadcast([P, D])).then_inc(g_loaded, 16)
                g.dma_start(mod[0:DEC, 2, 1, :], ada_d[1:2, v * D:(v + 1) * D].to_broadcast([DEC, D])).then_inc(g_loaded, 16)

            load_ab(0)
            load_g(0)
            pool.wait_ge(a_ready, 1)
            g.dma_start(gainb[:, :], pool_scale[0:1, :].to_broadcast([P, D])).then_inc(g_loaded, 16)
            load_ab(1)
            g.dma_start(xs_d[NASSIGN:XROWS, :], x_prompt[0, 0:P, :]).then_inc(tail_stored, 16)
            for j in range(0, NOV, TP):
                n = min(TP, NOV - j) * P
                g.dma_start(ys_d[(NE + j) * P:(NE + j) * P + n, :], x_prompt[0, 0:n, :]).then_inc(tail_stored, 16)
            load_g(1)

            def dispatch(layer):
                pool.wait_ge(pos_ready, layer + 1)
                pool.wait_ge(tail_stored, 16 * (1 + (NOV + TP - 1) // TP))
                for t in range(NT):
                    for r in range(2):
                        g.indirect_dma_start(
                            out=xs_d[:, :], out_offset=bass.IndirectOffsetOnAxis(ap=posi[0:rows[t], 0, r, t:t + 1], axis=0),
                            in_=h[0:rows[t], t, :], in_offset=None).then_inc(scattered, 16)

                def load_x(i, par, e):
                    off = pool.value_load(tabi[0:1, bass.ds(e, 1)] if not isinstance(e, int) else tabi[0:1, e:e + 1],
                                          min_val=0, max_val=NASSIGN)
                    g.dma_start(xg[:, par, :], xs_d[bass.ds(off, P), :]).then_inc(xg_loaded[par], 16)

                pool.wait_ge(scattered, 16 * 2 * NT * (layer + 1))
                b = layer * NE
                load_x(0, 0, 0)
                load_x(1, 1, 1)

                def step(e, par, more):
                    if more:
                        pool.wait_ge(E.tx, 2 * e + (2 * b + 2))
                        load_x(None, par, e + 2)
                    pool.wait_ge(E.ys_act, e + (b + 1))
                    pool.wait_ge(E.ys_dve, e + (b + 1))
                    row = e * P
                    dst = ys_d[row:row + P, :] if isinstance(e, int) else ys_d[bass.ds(row, P), :]
                    g.dma_start(dst, ysb[:, par, :]).then_inc(y_stored[par], 16)

                with pool.Fori(0, NE // 2 - 1) as i:
                    for par in range(2):
                        step(2 * i + par, par, True)
                step(NE - 2, 0, False)
                step(NE - 1, 1, False)
                n_ov = pool.value_load(tabi[0:1, NE + 2 * NOV:NE + 2 * NOV + 1], min_val=0, max_val=NOV)
                for par in range(2):
                    pool.wait_ge(y_stored[par], 16 * (NE // 2) * (layer + 1))
                with pool.If(n_ov > 0):
                    with pool.Fori(0, n_ov) as j:
                        off = pool.value_load(tabi[0:1, bass.ds(NE + NOV + j, 1)], min_val=0, max_val=NASSIGN)
                        g.dma_start(xg[:, 0, :], xs_d[bass.ds(off, P), :]).then_inc(ov_x[layer], 16)
                        pool.wait_ge(ov_act[layer], 4 * j + 4)
                        pool.wait_ge(ov_dve[layer], 3 * j + 3)
                        g.dma_start(ys_d[bass.ds(j * P + NE * P, P), :], ysb[:, 0, :]).then_inc(ov_y[layer], 16)
                        pool.wait_ge(ov_y[layer], 16 * j + 16)
                for t in range(NT):
                    for r in range(2):
                        g.indirect_dma_start(
                            out=yg[0:rows[t], t, r, :], out_offset=None, in_=ys_d[:, :],
                            in_offset=bass.IndirectOffsetOnAxis(ap=posi[0:rows[t], 1, r, t:t + 1], axis=0),
                        ).then_inc(yg_loaded[t], 16)

            dispatch(0)
            load_ab(2)
            load_ab(3)
            pool.wait_ge(f_stored, 32)
            pool.wait_ge(tr_done, 2 * NT * 5)
            pool.wait_ge(kv_out, 16 * 6)
            for t in range(TP):
                src = f_d[t * NH:(t + 1) * NH, :].unsqueeze(0).to_broadcast([P, NH, P])
                g.dma_start(nfb[:, :, t, :], src).then_inc(nfb_loaded, 16)
            ckv = cache_k[0].rearrange("(t p) (g h) d -> g p t (h d)", p=P, g=4)
            cvv = cache_v[0].rearrange("(t p) (g h) d -> g p t (h d)", p=P, g=4)
            fv = f_d.rearrange("(i g j) k -> g j i k", g=4, j=4)
            for gi in range(4):
                if gi == 1:
                    pool.wait_ge(at_o, TP * NH)
                if gi >= 2:
                    pool.wait_ge(sa_o, 2 * gi - 2)
                b = gi % 2
                g.dma_start(ck[b], ckv[gi]).then_inc(sa_loaded[b], 16)
                g.dma_start(cv[b], cvv[gi]).then_inc(sa_loaded[b], 16)
                for j in range(4):
                    src = fv[gi, j, TP:NF, :].unsqueeze(0)
                    g.dma_start(bias_s[b][32 * j:32 * j + 32, :].rearrange("p (i k) -> p i k", i=CT + 1),
                                src.to_broadcast([32, CT + 1, P])).then_inc(sa_loaded[b], 16)
            pool.wait_ge(sa_o, 8)
            load_g(2)
            load_ab(4)
            load_g(3)
            dispatch(1)

        @block.tensor
        def _(pe):
            T = nc.tensor

            def ada(grp, units=range(4)):
                bank = pb[grp % 2]
                if grp >= 2 and units[0] == 0:
                    pe.wait_ge(ada_staged, grp - 1)
                for u in units:
                    n = 4 * grp + u
                    pe.wait_ge(slot_loaded[ada_slot[n]], 16 * (n // 6 + 1))
                    w = ring[:, ada_slot[n], :].rearrange("p (k j n) -> p k j n", k=2, j=4)
                    for k in range(2):
                        for j in range(4):
                            last = T.matmul(bank[32 * j:32 * j + 32, :], cT[:, 2 * u + k, :], w[:, k, j, :],
                                            start=(u == 0 and k == 0), stop=(u == 3 and k == 1),
                                            tile_position=(0, 32 * j))
                    last.then_inc(unit_used, 1)

            def transposes(src, idx, srcready, half_cols):
                for t in range(NT):
                    srcready(t)
                    for b in range(2):
                        s = idx * NT + t
                        if s:
                            pe.wait_ge((tr_act, tr_dve)[b], s)
                        for c in range(4):
                            last = T.transpose(pb[2 + b][:, c * P:c * P + rows[t]], half_cols(src, t, 4 * b + c),
                                               ident[0:rows[t], 0:rows[t]])
                        last.then_inc(tr_done, 1)

            def by_stride(src, t, k):
                return src[0:rows[t], t, k:D:KC]

            def by_chunk(src, t, k):
                return src[0:rows[t], t, k * P:(k + 1) * P]

            def narrow_product(turn, banks, which, done):
                for bank, c0, n in ((pb[banks[0]], 0, SEQ), (pb[banks[1]], SEQ, DEC)):
                    for i in range(KC // 4):
                        for j in range(4):
                            k = j * KC // 4 + i
                            last = T.matmul(bank[32 * j:32 * j + 32, 0:n], wrf[:, k, :, :].rearrange("p a e -> p (a e)"),
                                            hT[:, k, c0:c0 + n], start=(i == 0), stop=(i == KC // 4 - 1),
                                            tile_position=(0, 32 * j))
                last.then_inc(part_done, 1)
                pe.wait_ge(part_copied, 2 * turn)
                for t in range(NT):
                    last = T.matmul(pb[6][0:rows[t], t * NE:(t + 1) * NE], partT[:, col[t]:col[t] + rows[t]],
                                    sel[:, which, :], start=True, stop=True)
                last.then_inc(done, 1)

            def route(layer):
                stage_no = 1 if layer == 0 else 4
                transposes(h, 6 * layer,
                           lambda t: pe.wait_ge(h_ready, NORM_DONE[stage_no] - NT + t + 1), by_stride)
                s = 6 * layer * NT
                pe.wait_ge(tr_act, s + NT)
                pe.wait_ge(tr_dve, s + NT)
                narrow_product((1, 3)[layer], (4, 5), 0, logits_done)

            def ranks(layer):
                pe.wait_ge(pick_ready, layer + 1)
                m = Mb[:, :, :].rearrange("p t e -> p (t e)")
                T.matmul(pb[6][:, 128:128 + NT * NE], tri_s[:, :], m, start=True, stop=True)
                T.matmul(pb[7][:, 128:128 + NT * NE], ones[:, :], m, start=True, stop=True).then_inc(rank_done, 1)

            def pe_tx(S, i, b, par):
                for half, done in enumerate((S.xt_act, S.xt_dve)):
                    if not (isinstance(i, int) and i + b == 0):
                        pe.wait_ge(done, i + b)
                    for c in range(4):
                        last = T.transpose(pb[half][:, c * P:(c + 1) * P], xg[:, par, 4 * half + c:D:KC], ident[:, :])
                    last.then_inc(S.tx, 1)

            def pe_gate(S, i, b, par, w, ks):
                for k in ks:
                    if k == 0:
                        pe.wait_ge(S.xt_act, i + (b + 1))
                        pe.wait_ge(S.xt_dve, i + (b + 1))
                        if not (isinstance(i, int) and i + b == 0):
                            pe.wait_ge(S.silu, i + b)
                    last = T.matmul(pb[3][:, :], xgT[:, par, k, :], w[:, k * DE:(k + 1) * DE],
                                    start=(k == 0), stop=(k == KC - 1))
                if ks[-1] == KC - 1:
                    last.then_inc(S.gate, 1)
                return last

            def pe_up(S, i, b, par, w):
                if not (isinstance(i, int) and i + b == 0):
                    pe.wait_ge(S.hact, i + b)
                for k in range(KC):
                    last = T.matmul(pb[4][:, :], xgT[:, par, k, :], w[:, k * DE:(k + 1) * DE],
                                    start=(k == 0), stop=(k == KC - 1))
                last.then_inc(S.up, 1)

            def pe_th(S, i, b):
                pe.wait_ge(S.hact, i + (b + 1))
                for c in range(KE):
                    last = T.transpose(pb[2][:, c * P:(c + 1) * P], hact[:, c:DE:KE], ident[:, :])
                last.then_inc(S.th, 1)

            def pe_down(S, i, b, w):
                pe.wait_ge(S.hactT, i + (b + 1))
                for half, done in enumerate((S.ys_act, S.ys_dve)):
                    if not (isinstance(i, int) and i + b == 0):
                        pe.wait_ge(done, i + b)
                    for k in range(KE):
                        last = T.matmul(pb[5 + half][:, :], hactT[:, k, :],
                                        w[:, k * D + 512 * half:k * D + 512 * half + 512],
                                        start=(k == 0), stop=(k == KE - 1))
                    last.then_inc(S.down, 1)

            def experts(layer):
                e0, before = layer * NE, MOE_BEFORE[layer]

                def unit(slot, i):
                    pe.wait_ge(slot_loaded[slot], 16 * i + 16 * (before[slot] + 1))
                    return ring[:, slot, :]

                def tokens(i, par):
                    pe.wait_ge(xg_loaded[par], 16 * i + 16 * (layer * NPE + 1))

                def step(i, par):
                    e = 2 * i + par
                    pe_up(E, e, e0, par, unit(U_SLOT + par, i))
                    tokens(i + par, 1 - par)
                    pe_tx(E, e + 1, e0, 1 - par)
                    w = unit(G_SLOT + 1 - par, i + par)
                    pe_gate(E, e + 1, e0, 1 - par, w, range(0, KC // 2))
                    pe_th(E, e, e0)
                    pe_gate(E, e + 1, e0, 1 - par, w, range(KC // 2, KC))
                    pe_down(E, e, e0, unit(D_SLOT + par, i))

                tokens(0, 0)
                pe_tx(E, 0, e0, 0)
                pe_gate(E, 0, e0, 0, unit(G_SLOT, 0), range(KC))
                step(0, 0)
                step(0, 1)
                with pe.Fori(1, NPE - 1) as i:
                    step(i, 0)
                    step(i, 1)
                step(NPE - 1, 0)
                pe_up(E, NE - 1, e0, 1, unit(U_SLOT + 1, NPE - 1))
                pe_th(E, NE - 1, e0)
                pe_down(E, NE - 1, e0, unit(D_SLOT + 1, NPE - 1))
                n_ov = pe.value_load(tabi[0:1, NE + 2 * NOV:NE + 2 * NOV + 1], min_val=0, max_val=NOV)
                with pe.If(n_ov > 0):
                    pe.wait_ge(E.ys_act, e0 + NE)
                    pe.wait_ge(E.ys_dve, e0 + NE)
                    with pe.Fori(0, n_ov) as j:
                        pe.wait_ge(ov_w[layer], 48 * j + 48)
                        pe.wait_ge(ov_x[layer], 16 * j + 16)
                        for half in range(2):
                            for c in range(4):
                                last = T.transpose(pb[half][:, c * P:(c + 1) * P], xg[:, 0, 4 * half + c:D:KC], ident[:, :])
                            last.then_inc(ov_pe[layer], 1)
                        pe.wait_ge(ov_act[layer], 4 * j + 1)
                        pe.wait_ge(ov_dve[layer], 3 * j + 1)
                        for bank, slot in ((3, G_SLOT), (4, U_SLOT)):
                            for k in range(KC):
                                last = T.matmul(pb[bank][:, :], xgT[:, 0, k, :], ring[:, slot, k * DE:(k + 1) * DE],
                                                start=(k == 0), stop=(k == KC - 1))
                            last.then_inc(ov_pe[layer], 1)
                        pe.wait_ge(ov_dve[layer], 3 * j + 2)
                        for c in range(KE):
                            last = T.transpose(pb[2][:, c * P:(c + 1) * P], hact[:, c:DE:KE], ident[:, :])
                        last.then_inc(ov_pe[layer], 1)
                        pe.wait_ge(ov_act[layer], 4 * j + 3)
                        for half in range(2):
                            for k in range(KE):
                                last = T.matmul(pb[5 + half][:, :], hactT[:, k, :],
                                                ring[:, D_SLOT, k * D + 512 * half:k * D + 512 * half + 512],
                                                start=(k == 0), stop=(k == KE - 1))
                            last.then_inc(ov_pe[layer], 1)
                        pe.wait_ge(ov_act[layer], 4 * j + 4)
                        pe.wait_ge(ov_dve[layer], 3 * j + 3)

            pe.wait_ge(c_ready, 1)
            for grp in range(3):
                ada(grp)
            pe.wait_ge(consts, 1)
            pe.wait_ge(bands_ready, 1)
            pe.wait_ge(small_loaded, SMALL)
            pe.wait_ge(cachep_loaded, 16)

            def differences(t):
                pe.wait_ge(h_ready, t + 1)
                r = rows[t]
                prev = None if t == 0 else (cachep if t == TS else h[:, t - 1, :])
                for b in range(2):
                    if t:
                        pe.wait_ge(mix_diffT, 2 * t - 1 + b)
                    for c in range(4 * b, 4 * b + 4):
                        grp = c * P // PGD
                        dst = pb[2 + b][:, (c % 4) * P:(c % 4) * P + r]
                        last = T.matmul(dst, h[0:r, t, c * P:(c + 1) * P], bands[0:r, 1 if t == 0 else 0, grp, 0:r],
                                        start=True, stop=prev is None)
                        if prev is not None:
                            last = T.matmul(dst, prev[:, c * P:(c + 1) * P], bands[:, 2, grp, 0:r],
                                            start=False, stop=True)
                    last.then_inc(mix_diff, 1)

            differences(0)
            for t in range(NT):
                r = rows[t]
                if t + 1 < NT:
                    differences(t + 1)
                for b in range(2):
                    pe.wait_ge(mix_diffT, 2 * t + 1 + b)
                    if t:
                        pe.wait_ge(mix_added, 2 * t - 1 + b)
                    for grp in range(2 * b, 2 * b + 2):
                        for k in range(2):
                            last = T.matmul(pb[4 + b][0:r, (grp % 2) * PGD:(grp % 2 + 1) * PGD],
                                            diffT[:, 2 * grp + k, 0:r], wpool[:, grp, k, :],
                                            start=(k == 0), stop=(k == 1))
                    last.then_inc(mix_y, 1)
                if t < 4:
                    ada(3, [t])
            ada(4)
            route(0)
            ada(5)
            ranks(0)
            ada(6)
            pe.wait_ge(ada_staged, 7)
            experts(0)

            def project(u0, n_units, ready_pass, stage_no, fpart):
                transposes(h, ready_pass, lambda t: pe.wait_ge(h_ready, NORM_DONE[stage_no] - NT + t + 1), by_stride)
                pe.wait_ge(tr_act, (ready_pass + 1) * NT)
                pe.wait_ge(tr_dve, (ready_pass + 1) * NT)
                c = u0 * NT
                for u in range(u0, u0 + n_units):
                    pe.wait_ge(slot_loaded[u % 2], 16 * (before_proj[u % 2] + u // 2 + 1))
                    w = ring[:, u % 2, :]
                    for t in range(NT):
                        if c >= 2:
                            pe.wait_ge((proj_act, proj_dve)[c % 2], c // 2)
                        for k in range(KC):
                            if t < TP:
                                last = T.matmul(pb[4 + c % 2][:, :], hT[:, k, col[t]:col[t] + P],
                                                w[:, k * 512:(k + 1) * 512], start=(k == 0), stop=(k == KC - 1))
                                continue
                            for j in range(4):
                                last = T.matmul(pb[4 + c % 2][32 * j:32 * j + DEC, 0:P], hT[:, k, SEQ:TOK],
                                                w[:, k * 512 + j * P:k * 512 + (j + 1) * P],
                                                start=(k == 0), stop=(k == KC - 1), tile_position=(0, 32 * j))
                        last.then_inc(proj_done, 1)
                        c += 1
                if fpart:
                    narrow_product(2, (0, 1), 1, f_done)

            project(0, 4, 1, 2, True)
            project(4, 2, 2, 3, False)
            pe.wait_ge(lf_ready, 1)
            lf = LF[:, :, :].rearrange("p t n -> p (t n)")
            T.matmul(pb[6][:, 0:NF * NH], tri_i[:, :], lf, start=True, stop=True)
            T.matmul(pb[7][:, 0:NF * NH], ones[:, :], lf, start=True, stop=True).then_inc(csum_done, 1)
            pe.wait_ge(F_ready, 1)
            ff = Fs[:, :, :].rearrange("p t n -> p (t n)")
            T.transpose(pb[0][:, 0:P], ff[:, 0:P], ident[:, :])
            T.transpose(pb[0][0:NF * NH - P, P:2 * P], ff[:, P:NF * NH], ident[:, :]).then_inc(fT_done, 1)
            transposes(kk, 3, lambda t: pe.wait_ge(qk_ready, t + 1), by_chunk)
            transposes(qq, 4, lambda t: pe.wait_ge(qk_ready, NT + t + 1), by_chunk)

            pe.wait_ge(tr_act, 5 * NT)
            pe.wait_ge(tr_dve, 5 * NT)
            NB = 2 * TP
            with pe.Fori(0, NPAIR) as j:
                def scores(n):
                    s, b = divmod(n, TP)
                    if n % TP == 0:
                        pe.wait_ge(at_q, 2 * j + s + 1)
                    bank = pb[n % 4]
                    if n >= 4:
                        pe.wait_ge(at_add, NB * j + n - 3)
                    if b:
                        T.matmul(bank[:, 0:b * P], qz[:, s, b * P:(b + 1) * P],
                                 kT[:, bass.ds(j, 1), 0:b * P].rearrange("p o t -> p (o t)"), start=True, stop=True)
                    T.matmul(bank[:, b * P:(b + 1) * P], qz[:, s, b * P:(b + 1) * P],
                             kT[:, bass.ds(j, 1), b * P:(b + 1) * P].rearrange("p o t -> p (o t)"), start=True, stop=False)
                    T.matmul(bank[:, b * P:(b + 1) * P], identb[:, :], causal[:, :],
                             start=False, stop=True).then_inc(at_s, 1)

                def turn(n):
                    s, b = divmod(n, TP)
                    pe.wait_ge(at_exp, NB * j + n + 1)
                    if n >= 2:
                        pe.wait_ge(at_pt, NB * j + n - 1)
                    for c in range(b + 1):
                        last = T.transpose(pb[4 + n % 2][:, c * P:(c + 1) * P], S_sb[:, n % 4, c * P:(c + 1) * P], ident[:, :])
                    last.then_inc(at_t, 1)

                def values(n):
                    s, b = divmod(n, TP)
                    pe.wait_ge(at_pt, NB * j + n + 1)
                    if n >= 2:
                        pe.wait_ge(at_o, NB * j + n - 1)
                    for c in range(b + 1):
                        last = T.matmul(pb[6 + n % 2][:, 0:HD], PT[:, n % 2, c * P:(c + 1) * P],
                                        vv[:, c, bass.ds(j * 2 * HD + s * HD, HD)], start=(c == 0), stop=(c == b))
                    last.then_inc(at_pv, 1)

                scores(0)
                scores(1)
                for n in range(NB):
                    if n + 2 < NB:
                        scores(n + 2)
                    turn(n)
                    if n:
                        values(n - 1)
                values(NB - 1)
                pe.wait_ge(at_o, NB * j + NB)
            with pe.Fori(0, 2) as gp:
                for par in range(2):
                    gi = gp * 2 + par
                    pe.wait_ge(sa_loaded[par], 96 * gp + 96)
                    for a in range(2):
                        for b in range(2):
                            bank = pb[2 * a + b]
                            for c in range(4):
                                last = T.transpose(bank[:, c * P:(c + 1) * P], ck[par][:, 4 * b + c, a * P:(a + 1) * P], ident[:, :])
                            last.then_inc(sa_kt, 1)
                    pe.wait_ge(sa_kte, 4 * gi + 4)
                    pe.wait_ge(sa_q, gi + 1)
                    for a in range(2):
                        for b in range(2):
                            T.matmul(pb[4 + b][64 * a:64 * a + 64, :], qbs[:, a, :], kTc[:, a, 512 * b:512 * b + 512],
                                     start=True, stop=True)
                        last = T.matmul(pb[6][64 * a:64 * a + 64, 0:DEC], qbs[:, a, :],
                                        kns[:, a, :], start=True, stop=True)
                    last.then_inc(sa_s, 1)
                    pe.wait_ge(sa_exp, gi + 1)
                    for c in range(CT):
                        last = T.transpose(pb[c // 4][:, (c % 4) * P:(c % 4 + 1) * P], Ss[:, c * P:(c + 1) * P], ident[:, :])
                    T.transpose(pb[2][0:DEC, 0:P], Ss[:, PAST:SK], ident[:, :]).then_inc(sa_t, 1)
                    pe.wait_ge(sa_pt, 3 * gi + 3)
                    for c in range(CT):
                        T.matmul(pb[7][:, 0:4 * HD], PTs[:, c, :], cv[par][:, c, :], start=(c == 0), stop=False)
                    T.matmul(pb[7][:, 0:4 * HD], PTs[0:DEC, CT, :], vv[0:DEC, TS, bass.ds(gi * 4 * HD, 4 * HD)],
                             start=False, stop=True).then_inc(sa_pv, 1)
                    pe.wait_ge(sa_o, 2 * gi + 2)
            transposes(oo, 5, lambda t: None, by_stride)
            pe.wait_ge(tr_act, 6 * NT)
            pe.wait_ge(tr_dve, 6 * NT)
            c = 0
            for u in range(2):
                if u == 0:
                    pe.wait_ge(wo_loaded, 16)
                else:
                    pe.wait_ge(slot_loaded[1], 16 * (before_proj[1] + 4))
                w = (wo_first, ring[:, 1, :])[u]
                for t in range(NT):
                    if c >= 2:
                        pe.wait_ge(o_added, c - 1)
                    for k in range(KC):
                        last = T.matmul(pb[4 + c % 2][0:rows[t], :], hT[:, k, col[t]:col[t] + rows[t]],
                                        w[:, k * 512:(k + 1) * 512], start=(k == 0), stop=(k == KC - 1))
                    last.then_inc(o_done, 1)
                    c += 1
            route(1)
            ranks(1)
            experts(1)

        @block.scalar
        def _(act):
            A = nc.scalar
            A.dma_start(wpool, w_pool[0].rearrange("g (k p) n -> p g k n", p=P)).then_inc(small_loaded, 16)
            A.dma_start(wrf[:, :, 0, :], w_router.rearrange("(p k) e -> p k e", k=KC)).then_inc(small_loaded, 16)
            A.dma_start(wrf[:, :, 1, :], kvf_v[:, :, 2 * D:2 * D + NH]).then_inc(small_loaded, 16)
            A.dma_start(brb[:, :], b_router.unsqueeze(0).to_broadcast([P, NE])).then_inc(small_loaded, 16)
            A.dma_start(bfb[:, :], b_f.unsqueeze(0).to_broadcast([P, NH])).then_inc(small_loaded, 16)
            A.dma_start(knb[:, :], k_norm.unsqueeze(0).to_broadcast([P, HD])).then_inc(small_loaded, 16)
            A.dma_start(qnb[:, :], q_norm[0:1, :].to_broadcast([P, HD])).then_inc(small_loaded, 16)
            act.wait_ge(cachep_zero, 1)
            A.dma_start(cachep[P - PBUF:P, :], cache_pool[0, 0]).then_inc(cachep_loaded, 16)

            def load_bias(grp):
                src = (ada_b[0], grp * 2048) if grp < 3 else (kv_ada_b, 0) if grp == 3 else (ada_b[1], (grp - 4) * 2048)
                if grp >= 2:
                    act.wait_ge(ada_staged, grp - 1)
                for s in range(2):
                    A.dma_start(adab[s:P:32, grp % 2, :],
                                src[0][src[1]:src[1] + 2048].rearrange("(j n) -> j n", j=4)).then_inc(bias_loaded[grp % 2], 16)

            def store_ada(grp):
                act.wait_ge(ada_staged, grp + 1)
                for s in range(2):
                    A.dma_start(ada_d[s, grp * 2048:(grp + 1) * 2048].rearrange("(j n) -> j n", j=4),
                                stage[s:P:32, grp % 2, :]).then_inc(ada_stored[grp], 16)

            act.wait_ge(c_loaded, 32)
            A.activation(csl[:, :, :], cs[:, :, :], ACT.Silu).then_inc(c_silu, 1)
            act.wait_ge(adab_zero, 1)
            load_bias(0)
            load_bias(1)

            def root_of_mean(m):
                act.wait_ge(ms_ready, m)
                A.activation(rstd[:, :], ssq[:, :], ACT.Sqrt).then_inc(root_ready, 1)

            def square_all(m, ready):
                for t in range(NT):
                    ready(t)
                    A.activation(h[0:rows[t], t, :], x[0:rows[t], t, :], ACT.Square,
                                 accum_out=ssq[0:rows[t], t:t + 1]).then_inc(squares, 1)
                if m > 1:
                    root_of_mean(m)

            def copy_transposed(idx, dst):
                for t in range(NT):
                    act.wait_ge(tr_done, 2 * (idx * NT + t) + 1)
                    A.activation(dst[:, 0:4, col[t]:col[t] + rows[t]],
                                 pb[2][:, :].rearrange("p (c t) -> p c t", c=4)[:, :, 0:rows[t]],
                                 ACT.Copy).then_inc(tr_act, 1)

            act.wait_ge(x_loaded, 16 * NT)
            act.wait_ge(c_ready, 1)
            square_all(1, lambda t: None)
            act.wait_ge(consts, 1)
            A.dma_start(LF[:, TP:TP + CT, :], cache_logf[0].rearrange("(t p) h -> p t h", p=P)).then_inc(clogf_loaded, 16)
            for grp in range(3):
                store_ada(grp)
                load_bias(grp + 2)
                if grp == 0:
                    root_of_mean(1)
            act.wait_ge(h_ready, NT)
            A.dma_start(pool_prompt[0, 0], h[P - PBUF:P, TP - 1, :]).then_inc(hist_stored, 16)
            A.dma_start(pool_sample[0, 0], h[DEC - PBUF:DEC, TS, :]).then_inc(hist_stored, 16)
            for t in range(NT):
                for b in range(2):
                    act.wait_ge(mix_diff, 2 * t + b + 1)
                    if t:
                        act.wait_ge(mix_y, 2 * t)
                    A.activation(diffT[:, 4 * b:4 * b + 4, 0:rows[t]],
                                 pb[2 + b][:, :].rearrange("p (c t) -> p c t", c=4)[:, :, 0:rows[t]],
                                 ACT.Copy).then_inc(mix_diffT, 1)
            store_ada(3)
            load_bias(5)
            act.wait_ge(hist_stored, 32)
            square_all(2, lambda t: act.wait_ge(mix_added, 2 * t + 2))
            store_ada(4)
            load_bias(6)

            def copy_partials(turn, banks):
                act.wait_ge(part_done, turn)
                A.activation(partT[:, 0:SEQ], pb[banks[0]][:, :], ACT.Copy).then_inc(part_copied, 1)
                A.activation(partT[:, SEQ:TOK], pb[banks[1]][:, 0:DEC], ACT.Copy).then_inc(part_copied, 1)

            def route(layer):
                copy_transposed(6 * layer, hT)
                copy_partials((1, 3)[layer], (4, 5))
                act.wait_ge(l_ready, layer + 1)
                A.activation(sc[:, :, :], L[:, :, :], ACT.Exp).then_inc(exp_ready, 1)

            def experts(layer):
                e0 = layer * NE

                def copy_x(S, i, b, par, with_wait=True):
                    act.wait_ge(S.tx, 2 * i + (2 * b + 1))
                    if with_wait:
                        act.wait_ge(S.up, i + (b - 1))
                    A.activation(xgT[:, par, 0:4, :], pb[0][:, :].rearrange("p (c t) -> p c t", c=4),
                                 ACT.Copy).then_inc(S.xt_act, 1)

                def silu(S, i, b):
                    act.wait_ge(S.gate, i + (b + 1))
                    if not (isinstance(i, int) and i + b == 0):
                        act.wait_ge(S.hact, i + b)
                    A.activation(sg, pb[3][:, :], ACT.Silu).then_inc(S.silu, 1)

                def copy_h(S, i, b):
                    act.wait_ge(S.th, i + (b + 1))
                    A.activation(hactT, pb[2][:, :].rearrange("p (c t) -> p c t", c=KE), ACT.Copy).then_inc(S.hactT, 1)

                def copy_y(S, i, b, par):
                    act.wait_ge(S.down, 2 * i + (2 * b + 1))
                    A.activation(ysb[:, par, 0:512], pb[5][:, :], ACT.Copy).then_inc(S.ys_act, 1)

                def step(i, par, pairs_stored, more=True):
                    e = 2 * i + par
                    silu(E, e, e0)
                    if more:
                        copy_x(E, e + 1, e0, 1 - par, not (isinstance(e, int) and e + e0 == 0))
                    copy_h(E, e, e0)
                    if pairs_stored is not None:
                        act.wait_ge(y_stored[par], pairs_stored)
                    copy_y(E, e, e0, par)

                copy_x(E, 0, e0, 0, layer > 0)
                for par in range(2):
                    step(0, par, 16 * NPE if layer else None)
                with act.Fori(1, NPE - 1) as i:
                    for par in range(2):
                        step(i, par, 16 * i + 16 * NPE * layer)
                step(NPE - 1, 0, 16 * (NPE - 1) + 16 * NPE * layer)
                step(NPE - 1, 1, 16 * (NPE - 1) + 16 * NPE * layer, more=False)
                n_ov = act.value_load(tabi[0:1, NE + 2 * NOV:NE + 2 * NOV + 1], min_val=0, max_val=NOV)
                with act.If(n_ov > 0):
                    with act.Fori(0, n_ov) as j:
                        act.wait_ge(ov_pe[layer], 7 * j + 1)
                        A.activation(xgT[:, 0, 0:4, :], pb[0][:, :].rearrange("p (c t) -> p c t", c=4),
                                     ACT.Copy).then_inc(ov_act[layer], 1)
                        act.wait_ge(ov_pe[layer], 7 * j + 3)
                        A.activation(sg, pb[3][:, :], ACT.Silu).then_inc(ov_act[layer], 1)
                        act.wait_ge(ov_pe[layer], 7 * j + 5)
                        A.activation(hactT, pb[2][:, :].rearrange("p (c t) -> p c t", c=KE),
                                     ACT.Copy).then_inc(ov_act[layer], 1)
                        act.wait_ge(ov_pe[layer], 7 * j + 6)
                        A.activation(ysb[:, 0, 0:512], pb[5][:, :], ACT.Copy).then_inc(ov_act[layer], 1)
                for t in range(NT):
                    act.wait_ge(yg_loaded[t], 32 * (layer + 1))
                    A.activation(yg[0:rows[t], t, 0, :], yg[0:rows[t], t, 0, :], ACT.Copy,
                                 scale=wts[0:rows[t], 0, t:t + 1]).then_inc(yg_scaled, 1)

            route(0)
            store_ada(5)
            store_ada(6)
            experts(0)
            square_all(3, lambda t: act.wait_ge(combined, t + 1))
            copy_transposed(1, hT)

            def copy_proj(c, dst):
                u, t = divmod(c, NT)
                act.wait_ge(proj_done, c + 1)
                if t < TP:
                    last = A.activation(dst[u // 2][:, t, 512 * (u % 2):512 * (u % 2) + 512], pb[4 + c % 2][:, :], ACT.Copy)
                else:
                    for j in range(4):
                        c0 = 512 * (u % 2) + j * P
                        last = A.activation(dst[u // 2][0:DEC, t, c0:c0 + P], pb[4 + c % 2][32 * j:32 * j + DEC, 0:P], ACT.Copy)
                last.then_inc(proj_act, 1)

            def squares_of(src, n0):
                for t in range(NT):
                    if n0 + t >= 2:
                        act.wait_ge(qk_ss, n0 + t - 1)
                    A.activation(mod[0:rows[t], 2, (n0 + t) % 2, :], src[0:rows[t], t, :], ACT.Square).then_inc(qk_sq, 1)

            def root(n):
                act.wait_ge(qk_ms, n)
                A.activation(ss[:, :, :], ss[:, :, :], ACT.Sqrt).then_inc(qk_root, 1)

            for c in range(0, 4 * NT, 2):
                copy_proj(c, (kk, vv, qq))
            copy_partials(2, (0, 1))
            act.wait_ge(f_abs, 1)
            A.activation(za[:, :, :], za[:, :, :], ACT.Exp, scale=-1.0).then_inc(f_exp, 1)
            act.wait_ge(f_1p, 1)
            A.activation(za[:, :, :], za[:, :, :], ACT.Ln).then_inc(f_ln, 1)
            copy_transposed(2, hT)
            act.wait_ge(proj_dve, 2 * NT)
            squares_of(kk, 0)
            root(1)
            for c in range(4 * NT, 6 * NT, 2):
                copy_proj(c, (kk, vv, qq))
            act.wait_ge(proj_dve, 3 * NT)
            act.wait_ge(fT_done, 1)
            A.activation(fT[:, 0, :], pb[0][:, 0:P], ACT.Copy, scale=-1.0).then_inc(fT_ready, 1)
            A.activation(fT[0:NF * NH - P, 1, :], pb[0][0:NF * NH - P, P:2 * P], ACT.Copy, scale=-1.0).then_inc(fT_ready, 1)
            act.wait_ge(fT_ready, 2)
            A.dma_start(f_d[0:P, :], fT[:, 0, :]).then_inc(f_stored, 16)
            A.dma_start(f_d[P:NF * NH, :], fT[0:NF * NH - P, 1, :]).then_inc(f_stored, 16)
            squares_of(qq, NT)
            root(2)
            copy_transposed(3, kT)
            copy_transposed(4, qT)

            act.wait_ge(nfb_loaded, 16 * TP)
            NB = 2 * TP
            with act.Fori(0, NPAIR) as j:
                for s in range(2):
                    A.activation(nfh[:, s, :], nfb[:, bass.ds(2 * j + s, 1), :, :].rearrange("p o t k -> p (o t k)"),
                                 ACT.Copy).then_inc(at_nf, 1)

                def expo(n):
                    w = (n % TP + 1) * P
                    act.wait_ge(at_nb, NB * j + n + 1)
                    A.activation(S_sb[:, n % 4, 0:w], S_sb[:, n % 4, 0:w], ACT.Exp, bias=mx[:, n, 2:3],
                                 accum_out=rs[:, n, 0:1]).then_inc(at_exp, 1)

                def out(n):
                    s, b = divmod(n, TP)
                    act.wait_ge(at_pv, NB * j + n + 1)
                    act.wait_ge(at_rinv, NB * j + n + 1)
                    A.activation(oo[:, b, bass.ds(j * 2 * HD + s * HD, HD)], pb[6 + n % 2][:, 0:HD], ACT.Copy,
                                 scale=rs[:, n, 1:2]).then_inc(at_o, 1)

                expo(0)
                expo(1)
                for n in range(NB):
                    if n + 2 < NB:
                        expo(n + 2)
                    if n:
                        out(n - 1)
                out(NB - 1)
            with act.Fori(0, 2) as gp:
                for par in range(2):
                    gi = gp * 2 + par
                    for b in range(2):
                        act.wait_ge(sa_kt, 4 * gi + b + 1)
                        A.activation(kTc[:, 0, 512 * b:512 * b + 512], pb[b][:, :], ACT.Copy).then_inc(sa_kte, 1)
                    act.wait_ge(sa_nb, gi + 1)
                    A.activation(Ss, Ss, ACT.Exp, bias=mx[:, 7, 2:3], accum_out=rs[:, 7, 0:1]).then_inc(sa_exp, 1)
                    act.wait_ge(sa_t, gi + 1)
                    A.activation(PTs[:, 0:4, :], pb[0][:, :].rearrange("p (c t) -> p c t", c=4), ACT.Copy).then_inc(sa_pt, 1)
                    act.wait_ge(sa_pv, gi + 1)
                    act.wait_ge(sa_rinv, gi + 1)
                    for jj in range(2):
                        last = A.activation(oo[0:DEC, TS, bass.ds(gi * 4 * HD + jj * HD, HD)],
                                            pb[7][32 * jj:32 * jj + 32, jj * HD:(jj + 1) * HD], ACT.Copy,
                                            scale=rs[32 * jj:32 * jj + 32, 7, 1:2])
                    last.then_inc(sa_o, 1)
            copy_transposed(5, hT)
            square_all(4, lambda t: act.wait_ge(o_added, NT + t + 1))
            route(1)
            experts(1)

        @block.vector
        def _(dve):
            V = nc.vector
            n_chain = [0]

            def link(ins):
                n_chain[0] += 1
                ins.then_inc(chain_v, 1)
                dve.wait_ge(chain_v, n_chain[0])

            link(V.memset(cT[:, :, :], 0.0))
            V.memset(adab[:, :, :], 0.0).then_inc(adab_zero, 1)
            V.memset(cachep, 0.0).then_inc(cachep_zero, 1)
            link(V.memset(ssq[:, :], float(D)))
            link(V.memset(L[:, :, :], 0.0))
            dve.wait_ge(c_silu, 1)
            V.tensor_copy(cT[:, :, 0:2].rearrange("p k s -> p s k"), csl[:, :, :]).then_inc(c_ready, 1)

            def stage_ada(grp):
                if grp >= 2:
                    dve.wait_ge(ada_stored[grp - 2], 32)
                dve.wait_ge(bias_loaded[grp % 2], 32 * (grp // 2 + 1))
                dve.wait_ge(unit_used, 4 * (grp + 1))
                V.tensor_tensor(stage[:, grp % 2, :], pb[grp % 2][:, :], adab[:, grp % 2, :], ALU.add).then_inc(ada_staged, 1)

            dve.wait_ge(consts, 1)
            link(V.tensor_copy(identb[:, :], ident[:, :]))
            link(V.tensor_reduce(sel[:, :, :], ident[:, :].rearrange("p (j w e) -> p w e j", j=4, w=2), axis=AX.X, op=ALU.add))
            for i, w in enumerate(WINDOWS):
                link(V.tensor_scalar(wtmp[:, :], cnti[:, :], float(w), None, ALU.min))
                link(V.reciprocal(wtmp[:, :], wtmp[:, :]))
                link(V.tensor_tensor(bands[:, 1, i, :], bands[:, 1, i, :], wtmp[:, :], ALU.mult))
                link(V.tensor_tensor(bands[:, 1, i, :], bands[:, 1, i, :], ident[:, :], ALU.subtract))
                ins = V.tensor_tensor(bands[:, 0, i, :], bands[:, 0, i, :], ident[:, :], ALU.subtract)
                if i + 1 < len(WINDOWS):
                    link(ins)
            ins.then_inc(bands_ready, 1)

            def norm(m, n_root, ready=None):
                if n_root:
                    dve.wait_ge(squares, NT * n_root)
                    V.tensor_scalar(ssq[:, :], ssq[:, :], 1.0 / D, EPS, ALU.mult, ALU.add).then_inc(ms_ready, 1)
                    dve.wait_ge(root_ready, n_root)
                    link(V.reciprocal(rstd[:, :], rstd[:, :]))
                dve.wait_ge(ab_loaded, 80 * (m + 1))
                V.scalar_tensor_tensor(out=mod[:, 0, 0, :], in0=mod[:, 0, 0, :], scalar=1.0, in1=gainb[:, :],
                                       op0=ALU.add, op1=ALU.mult)
                V.scalar_tensor_tensor(out=mod[0:DEC, 0, 1, :], in0=mod[0:DEC, 0, 1, :], scalar=1.0,
                                       in1=gainb[0:DEC, :], op0=ALU.add, op1=ALU.mult).then_inc(a_ready, 1)
                dve.wait_ge(a_ready, m + 1)
                if ready:
                    ready()
                for t in range(NT):
                    r, s = rows[t], t // TP
                    V.scalar_tensor_tensor(out=h[0:r, t, :], in0=x[0:r, t, :], scalar=rstd[0:r, t:t + 1],
                                           in1=mod[0:r, 0, s, :], op0=ALU.mult, op1=ALU.mult).then_inc(norm_mul, 1)
                    dve.wait_ge(norm_mul, NT * m + t + 1)
                    V.tensor_tensor(h[0:r, t, :], h[0:r, t, :], mod[0:r, 1, s, :], ALU.add).then_inc(h_ready, 1)

            def copy_transposed(idx, dst):
                for t in range(NT):
                    dve.wait_ge(tr_done, 2 * (idx * NT + t) + 2)
                    V.tensor_copy(dst[:, 4:8, col[t]:col[t] + rows[t]],
                                  pb[3][:, :].rearrange("p (c t) -> p c t", c=4)[:, :, 0:rows[t]]).then_inc(tr_dve, 1)

            stage_ada(0)
            stage_ada(1)
            norm(0, 1)
            stage_ada(2)
            dve.wait_ge(g_loaded, 48)
            V.tensor_tensor(mod[:, 2, 0, :], mod[:, 2, 0, :], gainb[:, :], ALU.mult)
            V.tensor_tensor(mod[0:DEC, 2, 1, :], mod[0:DEC, 2, 1, :], gainb[0:DEC, :], ALU.mult).then_inc(gp_ready, 1)
            dve.wait_ge(gp_ready, 1)

            def add_half(bank, t, half, done):
                r, s, c = rows[t], t // TP, slice(512 * half, 512 * half + 512)
                link(V.tensor_tensor(bank[0:r, :], bank[0:r, :], mod[0:r, 2, s, c], ALU.mult))
                return V.tensor_tensor(x[0:r, t, c], bank[0:r, :], x[0:r, t, c], ALU.add).then_inc(done, 1)

            for t in range(NT):
                for b in range(2):
                    dve.wait_ge(mix_y, 2 * t + b + 1)
                    add_half(pb[4 + b], t, b, mix_added)
            link(V.memset(t5[:, 0, :], 0.0))
            V.memset(t5[:, 1, :], 0.0).then_inc(g_free, 1)
            stage_ada(3)
            dve.wait_ge(hist_stored, 32)
            norm(1, 2)
            stage_ada(4)

            def tt(out, a, b, op):
                link(V.tensor_tensor(out, a, b, op))

            def red(out, a, op=ALU.max):
                link(V.tensor_reduce(out, a, axis=AX.X, op=op))

            def first_max(out, v, m, key, n):
                red(m, v)
                tt(out, v, bc(m, n, 2), ALU.is_equal)
                tt(key, out, bc(desc4[:, :], NT, 1), ALU.mult)
                red(m, key)
                tt(out, key, bc(m, n, 2), ALU.is_equal)

            def pick(layer):
                copy_transposed(6 * layer, hT)
                dve.wait_ge(logits_done, layer + 1)
                V.tensor_copy(L[:, 0:TP, :], pb[6][:, 0:TP * NE].rearrange("p (t e) -> p t e", t=TP))
                link(V.tensor_copy(L[0:DEC, TS, :], pb[6][0:DEC, TP * NE:NT * NE]))
                red(t5[:, 0, :], L[:, :, :])
                V.tensor_tensor(L[:, :, :], L[:, :, :], bc(t5[:, 0, :], NE, 2), ALU.subtract).then_inc(l_ready, 1)
                dve.wait_ge(exp_ready, layer + 1)
                red(t5[:, 1, :], sc[:, :, :], ALU.add)
                link(V.reciprocal(t5[:, 1, :], t5[:, 1, :]))
                tt(sc[:, :, :], sc[:, :, :], bc(t5[:, 1, :], NE, 2), ALU.mult)
                tt(selv[:, :, :], sc[:, :, :], bc(brb[:, :], NT, 1), ALU.add)
                sp4 = selv[:, :, :].rearrange("p t (g a b) -> p (t g) a b", g=NG, a=2)
                tt(pm[:, 0, :, :], sp4[:, :, :, 0], sp4[:, :, :, 1], ALU.max)
                tt(pm[:, 1, :, :], sp4[:, :, :, 0], sp4[:, :, :, 1], ALU.min)
                tt(pm[:, 2, :, 0], pm[:, 0, :, 0], pm[:, 0, :, 1], ALU.max)
                tt(pm[:, 2, :, 1], pm[:, 0, :, 0], pm[:, 0, :, 1], ALU.min)
                tt(pm[:, 3, :, 0], pm[:, 1, :, 0], pm[:, 1, :, 1], ALU.max)
                tt(pm[:, 3, :, 1], pm[:, 2, :, 1], pm[:, 3, :, 0], ALU.max)
                gs = m4[:, 0, :, :]
                tt(gs.rearrange("p t g -> p (t g)"), pm[:, 2, :, 0], pm[:, 3, :, 1], ALU.add)
                first_max(best[:, :, :], gs, t5[:, 2, :], m4[:, 1, :, :], NG)
                b4 = best[:, :, :].unsqueeze(3).to_broadcast([P, NT, NG, EPG])
                g44 = prod[:, :, :].rearrange("p t (g j) -> p t g j", g=NG)
                tt(g44, selv[:, :, :].rearrange("p t (g j) -> p t g j", g=NG), b4, ALU.mult)
                red(vj[:, :, :], prod[:, :, :].rearrange("p t (g j) -> p t j g", g=NG), ALU.add)
                for r in range(2):
                    first_max(one[:, r, :, :], vj[:, :, :], t5[:, 2, :], m4[:, 1, :, :], EPG)
                    if r == 0:
                        link(V.scalar_tensor_tensor(out=vj[:, :, :], in0=one[:, 0, :, :], scalar=-3e38,
                                                    in1=vj[:, :, :], op0=ALU.mult, op1=ALU.add))
                    o4 = oh[:, r, :, :].rearrange("p t (g j) -> p t g j", g=NG)
                    tt(o4, b4, one[:, r, :, :].unsqueeze(2).to_broadcast([P, NT, NG, EPG]), ALU.mult)
                    tt(prod[:, :, :], oh[:, r, :, :], sc[:, :, :], ALU.mult)
                    red(wts[:, r, :], prod[:, :, :], ALU.add)
                    tt(oh[:, r, :, :], oh[:, r, :, :], bc(valid[:, :], NE, 2), ALU.mult)
                V.tensor_tensor(Mb[:, :, :], oh[:, 0, :, :], oh[:, 1, :, :], ALU.add).then_inc(pick_ready, 1)
                tt(t5[:, 3, :], wts[:, 0, :], wts[:, 1, :], ALU.add)
                link(V.reciprocal(t5[:, 3, :], t5[:, 3, :]))
                for r in range(2):
                    tt(wts[:, r, :], wts[:, r, :], t5[:, 3, :], ALU.mult)

            def scan(out, counts):
                link(V.tensor_tensor_scan(out, onesr[:, :], counts, 0.0, ALU.mult, ALU.add))
                tt(out, out, counts, ALU.subtract)

            def places(layer):
                dve.wait_ge(rank_done, layer + 1)
                link(V.tensor_copy(tot[:, :, :], pb[7][:, 128:128 + NT * NE].rearrange("p (t e) -> p t e", t=NT)))
                for t in range(1, NT):
                    tt(tot[:, t, :], tot[:, t, :], tot[:, t - 1, :], ALU.add)
                link(V.tensor_copy(cnt[:, :], tot[:, NT - 1, :]))
                r6 = pb[6][:, 128:128 + NT * NE].rearrange("p (t e) -> p t e", t=NT)
                link(V.tensor_copy(rank[:, 0, :], r6[:, 0, :]))
                tt(rank[:, 1:NT, :], r6[:, 1:NT, :], tot[:, 0:NT - 1, :], ALU.add)
                scan(offs[:, :], cnt[:, :])
                link(V.tensor_scalar(ovc[:, :], cnt[:, :], float(P), None, ALU.is_gt))
                for m in range(2, -(-TOK // P)):
                    link(V.scalar_tensor_tensor(out=ovc[:, :], in0=cnt[:, :], scalar=float(m * P), in1=ovc[:, :],
                                                op0=ALU.is_gt, op1=ALU.add))
                scan(ovs[:, :], ovc[:, :])
                link(V.tensor_scalar(e16[:, 0, :], iotae[:, :], float(P), None, ALU.mult))
                link(V.tensor_scalar(e16[:, 1, :], ovs[:, :], float(P), float(NE * P - P), ALU.mult, ALU.add))
                tt(e16[:, 1, :], e16[:, 1, :], e16[:, 0, :], ALU.subtract)
                link(V.tensor_scalar(selv[:, :, :], rank[:, :, :], float(P), None, ALU.is_ge))
                tt(selv[:, :, :], selv[:, :, :], bc(e16[:, 1, :], NT, 1), ALU.mult)
                tt(selv[:, :, :], selv[:, :, :], bc(e16[:, 0, :], NT, 1), ALU.add)
                tt(selv[:, :, :], selv[:, :, :], rank[:, :, :], ALU.add)
                tt(rank[:, :, :], rank[:, :, :], bc(offs[:, :], NT, 1), ALU.add)
                for r in range(2):
                    for side, rowsof in enumerate((rank, selv)):
                        tt(prod[:, :, :], oh[:, r, :, :], rowsof[:, :, :], ALU.mult)
                        red(posf[:, side, r, :], prod[:, :, :], ALU.add)
                link(V.tensor_copy(posi[:, :, :, :], posf[:, :, :, :]))
                one_row = slice(0, 1)
                jj = iotaj[one_row, :].unsqueeze(2).to_broadcast([1, NOV, NE])
                ovs_b = ovs[one_row, :].unsqueeze(1).to_broadcast([1, NOV, NE])
                tt(ind[one_row, 0, :, :], jj, ovs_b, ALU.subtract)
                link(V.tensor_scalar(ind[one_row, 1, :, :], ind[one_row, 0, :, :], 0.0, None, ALU.is_ge))
                tt(ind[one_row, 2, :, :], ind[one_row, 0, :, :],
                   ovc[one_row, :].unsqueeze(1).to_broadcast([1, NOV, NE]), ALU.is_lt)
                tt(ind[one_row, 1, :, :], ind[one_row, 1, :, :], ind[one_row, 2, :, :], ALU.mult)
                link(V.tensor_scalar(ind[one_row, 0, :, :], ind[one_row, 0, :, :], float(P), float(P), ALU.mult, ALU.add))
                tt(ind[one_row, 0, :, :], ind[one_row, 0, :, :],
                   offs[one_row, :].unsqueeze(1).to_broadcast([1, NOV, NE]), ALU.add)
                tt(ind[one_row, 0, :, :], ind[one_row, 0, :, :], ind[one_row, 1, :, :], ALU.mult)
                tt(ind[one_row, 2, :, :], ind[one_row, 1, :, :],
                   iotae[one_row, :].unsqueeze(1).to_broadcast([1, NOV, NE]), ALU.mult)
                red(tabf[one_row, NE:NE + NOV], ind[one_row, 2, :, :], ALU.add)
                red(tabf[one_row, NE + NOV:NE + 2 * NOV], ind[one_row, 0, :, :], ALU.add)
                link(V.tensor_copy(tabf[one_row, 0:NE], offs[one_row, :]))
                red(tabf[one_row, NE + 2 * NOV:NE + 2 * NOV + 1], ovc[one_row, :], ALU.add)
                V.tensor_copy(tabi[one_row, :], tabf[one_row, :]).then_inc(pos_ready, 1)

            def experts(layer):
                e0 = layer * NE

                def copy_x(S, i, b, par, with_wait=True):
                    dve.wait_ge(S.tx, 2 * i + (2 * b + 2))
                    if with_wait:
                        dve.wait_ge(S.up, i + (b - 1))
                    V.tensor_copy(xgT[:, par, 4:8, :], pb[1][:, :].rearrange("p (c t) -> p c t", c=4)).then_inc(S.xt_dve, 1)

                def product(S, i, b):
                    dve.wait_ge(S.silu, i + (b + 1))
                    dve.wait_ge(S.up, i + (b + 1))
                    if not (isinstance(i, int) and i + b == 0):
                        dve.wait_ge(S.th, i + b)
                    V.tensor_tensor(hact, pb[4][:, :], sg, ALU.mult).then_inc(S.hact, 1)

                def copy_y(S, i, b, par):
                    dve.wait_ge(S.down, 2 * i + (2 * b + 2))
                    V.tensor_copy(ysb[:, par, 512:1024], pb[6][:, :]).then_inc(S.ys_dve, 1)

                def step(i, par, pairs_stored, more=True):
                    e = 2 * i + par
                    product(E, e, e0)
                    if more:
                        copy_x(E, e + 1, e0, 1 - par, not (isinstance(e, int) and e + e0 == 0))
                    if pairs_stored is not None:
                        dve.wait_ge(y_stored[par], pairs_stored)
                    copy_y(E, e, e0, par)

                copy_x(E, 0, e0, 0, layer > 0)
                for par in range(2):
                    step(0, par, 16 * NPE if layer else None)
                with dve.Fori(1, NPE - 1) as i:
                    for par in range(2):
                        step(i, par, 16 * i + 16 * NPE * layer)
                step(NPE - 1, 0, 16 * (NPE - 1) + 16 * NPE * layer)
                step(NPE - 1, 1, 16 * (NPE - 1) + 16 * NPE * layer, more=False)
                n_ov = dve.value_load(tabi[0:1, NE + 2 * NOV:NE + 2 * NOV + 1], min_val=0, max_val=NOV)
                with dve.If(n_ov > 0):
                    with dve.Fori(0, n_ov) as j:
                        dve.wait_ge(ov_pe[layer], 7 * j + 2)
                        V.tensor_copy(xgT[:, 0, 4:8, :], pb[1][:, :].rearrange("p (c t) -> p c t", c=4)).then_inc(
                            ov_dve[layer], 1)
                        dve.wait_ge(ov_act[layer], 4 * j + 2)
                        dve.wait_ge(ov_pe[layer], 7 * j + 4)
                        V.tensor_tensor(hact, pb[4][:, :], sg, ALU.mult).then_inc(ov_dve[layer], 1)
                        dve.wait_ge(ov_pe[layer], 7 * j + 7)
                        V.tensor_copy(ysb[:, 0, 512:1024], pb[6][:, :]).then_inc(ov_dve[layer], 1)
                dve.wait_ge(g_loaded, (80, 144)[layer])
                for t in range(NT):
                    r, s = rows[t], t // TP
                    dve.wait_ge(yg_scaled, NT * layer + t + 1)
                    y0, y1 = yg[0:r, t, 0, :], yg[0:r, t, 1, :]
                    link(V.scalar_tensor_tensor(out=y0, in0=y1, scalar=wts[0:r, 1, t:t + 1], in1=y0,
                                                op0=ALU.mult, op1=ALU.add))
                    link(V.tensor_tensor(y0, y0, mod[0:r, 2, s, :], ALU.mult))
                    V.tensor_tensor(x[0:r, t, :], x[0:r, t, :], y0, ALU.add).then_inc(combined, 1)

            pick(0)
            stage_ada(5)
            places(0)
            stage_ada(6)
            experts(0)
            link(V.memset(t5[:, 0, :], 0.0))
            V.memset(t5[:, 1, :], 0.0).then_inc(g_free, 1)

            norm(2, 3)
            copy_transposed(1, hT)

            def copy_proj(c):
                u, t = divmod(c, NT)
                dve.wait_ge(proj_done, c + 1)
                dst = (kk, vv, qq)[u // 2]
                if t < TP:
                    last = V.tensor_copy(dst[:, t, 512 * (u % 2):512 * (u % 2) + 512], pb[4 + c % 2][:, :])
                else:
                    for j in range(4):
                        c0 = 512 * (u % 2) + j * P
                        last = V.tensor_copy(dst[0:DEC, t, c0:c0 + P], pb[4 + c % 2][32 * j:32 * j + DEC, 0:P])
                last.then_inc(proj_dve, 1)

            def head_norm(src, gain, n0):
                for t in range(NT):
                    r = rows[t]
                    dve.wait_ge(qk_sq, n0 + t + 1)
                    V.tensor_reduce(ss[0:r, t, :], mod[0:r, 2, (n0 + t) % 2, :].rearrange("p (h d) -> p h d", h=NH),
                                    axis=AX.X, op=ALU.add).then_inc(qk_ss, 1)
                dve.wait_ge(qk_ss, n0 + NT)
                V.tensor_scalar(ss[:, :, :], ss[:, :, :], 1.0 / HD, EPS, ALU.mult, ALU.add).then_inc(qk_ms, 1)
                dve.wait_ge(qk_root, n0 // NT + 1)
                link(V.reciprocal(ss[:, :, :], ss[:, :, :]))
                for t in range(NT):
                    r = rows[t]
                    v = src[0:r, t, :].rearrange("p (h d) -> p h d", h=NH)
                    link(V.tensor_tensor(v, v, bc(ss[0:r, t, :], HD, 2), ALU.mult))
                    V.tensor_tensor(v, v, bc(gain[0:r, :], NH, 1), ALU.mult).then_inc(qk_ready, 1)

            for c in range(1, 4 * NT, 2):
                copy_proj(c)
            link(V.memset(ss[:, :, :], float(HD)))
            link(V.memset(z[:, :, :], 0.0))
            dve.wait_ge(f_done, 1)
            zp = pb[6][:, 0:NT * NH].rearrange("p (t e) -> p t e", t=NT)
            V.tensor_tensor(z[:, 0:TP, :], zp[:, 0:TP, :], bc(bfb[:, :], TP, 1), ALU.add)
            link(V.tensor_tensor(z[0:DEC, TS, :], zp[0:DEC, TS, :], bfb[0:DEC, :], ALU.add))
            V.scalar_tensor_tensor(out=za[:, :, :], in0=z[:, :, :], scalar=-1.0, in1=z[:, :, :],
                                   op0=ALU.mult, op1=ALU.max).then_inc(f_abs, 1)
            dve.wait_ge(f_exp, 1)
            V.tensor_scalar(za[:, :, :], za[:, :, :], 1.0, None, ALU.add).then_inc(f_1p, 1)
            dve.wait_ge(f_ln, 1)
            dve.wait_ge(clogf_loaded, 16)
            V.scalar_tensor_tensor(out=LF[0:DEC, NF - 1, :], in0=z[0:DEC, TS, :], scalar=0.0, in1=za[0:DEC, TS, :],
                                   op0=ALU.min, op1=ALU.subtract)
            V.scalar_tensor_tensor(out=LF[:, 0:TP, :], in0=z[:, 0:TP, :], scalar=0.0, in1=za[:, 0:TP, :],
                                   op0=ALU.min, op1=ALU.subtract).then_inc(lf_ready, 1)
            norm(3, 0)
            copy_transposed(2, hT)
            head_norm(kk, knb, 0)
            for c in range(4 * NT + 1, 6 * NT, 2):
                copy_proj(c)
            dve.wait_ge(csum_done, 1)
            link(V.tensor_copy(tF[:, :, :], pb[7][:, 0:NF * NH].rearrange("p (t n) -> p t n", t=NF)))
            for t in range(1, TP - 1):
                tt(tF[:, t, :], tF[:, t, :], tF[:, t - 1, :], ALU.add)
            for t in range(TP + 1, NF - 1):
                tt(tF[:, t, :], tF[:, t, :], tF[:, t - 1, :], ALU.add)
            c6 = pb[6][:, 0:NF * NH].rearrange("p (t n) -> p t n", t=NF)
            link(V.tensor_copy(Fs[:, 0, :], c6[:, 0, :]))
            link(V.tensor_copy(Fs[:, TP, :], c6[:, TP, :]))
            tt(Fs[:, 1:TP, :], c6[:, 1:TP, :], tF[:, 0:TP - 1, :], ALU.add)
            V.tensor_tensor(Fs[:, TP + 1:NF, :], c6[:, TP + 1:NF, :], tF[:, TP:NF - 1, :], ALU.add).then_inc(F_ready, 1)
            head_norm(qq, qnb, NT)
            copy_transposed(3, kT)
            copy_transposed(4, qT)
            dve.wait_ge(ada_stored[6], 32)
            link(V.memset(qz, 0.0))
            link(V.memset(qbd[:, :, :, :], 0.0))
            dve.wait_ge(tr_act, NT * 5)
            for s in range(2):
                link(V.tensor_scalar(qbd[64 * s:64 * s + 64, :, s, :], qT[64 * s:64 * s + 64, :, SEQ:TOK], SCALE, None, ALU.mult))
            for jj in range(4):
                link(V.tensor_copy(fqs[32 * jj:32 * jj + 32, :], Fs[0:DEC, NF - 1, jj:NH:4]))
            NB = 2 * TP
            K_AT = NB
            with dve.Fori(0, NPAIR) as j:
                k = [0]

                def step_link(ins):
                    k[0] += 1
                    ins.then_inc(at_chain, 1)
                    dve.wait_ge(at_chain, K_AT * j + k[0])

                for s in range(2):
                    q = slice(64 * s, 64 * s + 64)
                    V.tensor_scalar(qz[q, s, :], qT[q, bass.ds(j, 1), 0:SEQ].rearrange("p o t -> p (o t)"),
                                    SCALE, None, ALU.mult).then_inc(at_q, 1)

                def add(n):
                    s, b = divmod(n, TP)
                    w = (b + 1) * P
                    if n % TP == 0:
                        dve.wait_ge(at_nf, 2 * j + s + 1)
                    if n >= 4:
                        dve.wait_ge(at_t, NB * j + n - 3)
                    dve.wait_ge(at_s, NB * j + n + 1)
                    dve.sem_inc(passed_dve, 1)
                    V.tensor_tensor_reduce(out=S_sb[:, n % 4, 0:w], in0=pb[n % 4][:, 0:w], in1=nfh[:, s, 0:w], scale=1.0,
                                           scalar=-3e38, op0=ALU.add, op1=ALU.max,
                                           accum_out=mx[:, n, 0:1]).then_inc(at_add, 1)
                    dve.wait_ge(at_add, NB * j + n + 1)
                    fq = Fs[:, b, bass.ds(j * 2 + s, 1)]
                    step_link(V.tensor_tensor(mx[:, n, 1:2], mx[:, n, 0:1], fq, ALU.add))
                    V.tensor_tensor(mx[:, n, 2:3], fq, mx[:, n, 1:2], ALU.subtract).then_inc(at_nb, 1)

                def rest(n):
                    w = (n % TP + 1) * P
                    dve.wait_ge(at_exp, NB * j + n + 1)
                    V.reciprocal(rs[:, n, 1:2], rs[:, n, 0:1]).then_inc(at_rinv, 1)
                    dve.wait_ge(at_t, NB * j + n + 1)
                    if n >= 2:
                        dve.wait_ge(at_pv, NB * j + n - 1)
                    V.tensor_copy(PT[:, n % 2, 0:w], pb[4 + n % 2][:, 0:w]).then_inc(at_pt, 1)

                add(0)
                add(1)
                for n in range(NB):
                    if n + 2 < NB:
                        add(n + 2)
                    rest(n)
            with dve.Fori(0, 2) as gp:
                for par in range(2):
                    gi = gp * 2 + par
                    k = [0]

                    def link_s(ins):
                        k[0] += 1
                        ins.then_inc(sa_chain, 1)
                        dve.wait_ge(sa_chain, 4 * gi + k[0])

                    V.tensor_copy(kns, kT[:, bass.ds(2 * gi, 2), SEQ:TOK])
                    V.tensor_copy(qbs, qbd[:, bass.ds(2 * gi, 2), :, :].rearrange("p j a b -> p j (a b)")).then_inc(sa_q, 1)
                    for b in range(2):
                        dve.wait_ge(sa_kt, 4 * gi + 3 + b)
                        V.tensor_copy(kTc[:, 1, 512 * b:512 * b + 512], pb[2 + b][:, :]).then_inc(sa_kte, 1)
                    dve.wait_ge(sa_loaded[par], 96 * gp + 96)
                    link_s(V.tensor_tensor(bias_s[par][:, PAST:SK], bias_s[par][:, PAST:SK], smask[:, :], ALU.add))
                    dve.wait_ge(sa_s, gi + 1)
                    dve.sem_inc(passed_dve, 1)
                    for b, (c0, c1) in enumerate(((0, 512), (512, PAST), (PAST, SK))):
                        ins = V.tensor_tensor_reduce(out=Ss[:, c0:c1], in0=pb[4 + b][:, 0:c1 - c0], in1=bias_s[par][:, c0:c1],
                                                     scale=1.0, scalar=-3e38, op0=ALU.add, op1=ALU.max,
                                                     accum_out=mx[:, b, 0:1])
                    link_s(ins)
                    link_s(V.tensor_reduce(mx[:, 7, 0:1], mx[:, 0:3, 0], axis=AX.X, op=ALU.max))
                    fq = fqs[:, bass.ds(gi, 1)]
                    link_s(V.tensor_tensor(mx[:, 7, 1:2], mx[:, 7, 0:1], fq, ALU.add))
                    V.tensor_tensor(mx[:, 7, 2:3], fq, mx[:, 7, 1:2], ALU.subtract).then_inc(sa_nb, 1)
                    dve.wait_ge(sa_exp, gi + 1)
                    V.reciprocal(rs[:, 7, 1:2], rs[:, 7, 0:1]).then_inc(sa_rinv, 1)
                    dve.wait_ge(sa_t, gi + 1)
                    V.tensor_copy(PTs[:, 4:8, :], pb[1][:, :].rearrange("p (c t) -> p c t", c=4)).then_inc(sa_pt, 1)
                    V.tensor_copy(PTs[0:DEC, CT, :], pb[2][0:DEC, 0:P]).then_inc(sa_pt, 1)
                    dve.wait_ge(sa_pv, gi + 1)
                    dve.wait_ge(sa_rinv, gi + 1)
                    for jj in range(2, 4):
                        last = V.tensor_scalar(oo[0:DEC, TS, bass.ds(gi * 4 * HD + jj * HD, HD)],
                                               pb[7][32 * jj:32 * jj + 32, jj * HD:(jj + 1) * HD],
                                               rs[32 * jj:32 * jj + 32, 7, 1:2], None, ALU.mult)
                    last.then_inc(sa_o, 1)
            copy_transposed(5, hT)
            dve.wait_ge(g_loaded, 112)
            for c in range(2 * NT):
                u, t = divmod(c, NT)
                dve.wait_ge(o_done, c + 1)
                add_half(pb[4 + c % 2], t, u, o_added)
            link(V.memset(t5[:, 0, :], 0.0))
            V.memset(t5[:, 1, :], 0.0).then_inc(g_free, 1)
            norm(4, 4)
            pick(1)
            places(1)
            experts(1)


_INS = ['x_prompt', 'x_sample', 'cache_pool', 'cache_k', 'cache_v', 'cache_logf', 'c_prompt', 'c_sample',
        'ada_w', 'ada_b', 'norm_g', 'w_pool', 'pool_scale', 'kv_ada_w', 'kv_ada_b', 'kv_norm', 'w_kvf', 'b_f',
        'k_norm', 'w_q', 'q_norm', 'w_o', 'w_router', 'b_router', 'w_gate', 'w_up', 'w_down']


def kernel(**inputs):
    import numpy as _np
    import concourse.bacc as _bacc
    from concourse import mybir as _mybir
    from concourse.bass_utils import run_bass_kernel_spmd as _run

    nc = _bacc.Bacc("TRN2", target_bir_lowering=False, num_devices=1)
    arrays, args, shape = {}, [], {}
    for name in _INS:
        a = _np.ascontiguousarray(inputs[name])
        arrays[f"in_{name}_dram"] = a
        shape[name] = a.shape
        args.append(nc.dram_tensor(f"in_{name}_dram", a.shape, _mybir.dt.from_np(a.dtype), kind="ExternalInput").ap())
    B, S, D = shape['x_prompt']
    BD, SD, _ = shape['x_sample']
    LA, _, PB, _ = shape['cache_pool']
    H, HD = shape['cache_k'][2:]
    outs = [(B, S, D), (BD, SD, D), (LA, B, PB, D), (B, S, H, HD), (B, S, H, HD), (B, S, H),
            (LA, BD, PB, D), (BD, SD, H, HD), (BD, SD, H, HD), (BD, SD, H)]
    for i, s in enumerate(outs):
        args.append(nc.dram_tensor(f"out_{i}_dram", s, _mybir.dt.float32, kind="ExternalOutput").ap())
    bass_yoco_stream_step(nc, *args)
    r = _run(nc, [arrays], core_ids=[0])
    return tuple(r.results[0][f"out_{i}_dram"] for i in range(len(outs)))
```

```python
import concourse.bass as bass
from concourse import mybir
from contextlib import ExitStack



def bass_yoco_stream_step(
    nc, x_prompt, x_sample, cache_pool, cache_k, cache_v, cache_logf, c_prompt, c_sample,
    ada_w, ada_b, norm_g, w_pool, pool_scale, kv_ada_w, kv_ada_b, kv_norm, w_kvf, b_f,
    k_norm, w_q, q_norm, w_o, w_router, b_router, w_gate, w_up, w_down,
    y_prompt, y_sample, pool_prompt, k_prompt, v_prompt, logf_prompt,
    pool_sample, k_sample, v_sample, logf_sample,
):
    fp32, bf16, i32 = mybir.dt.float32, mybir.dt.bfloat16, mybir.dt.int32
    ALU, ACT, AX = mybir.AluOpType, mybir.ActivationFunctionType, mybir.AxisListType

    P = 128
    D = x_prompt.shape[2]
    SEQ, DEC = x_prompt.shape[1], x_sample.shape[1]
    PAST = cache_k.shape[1]
    NH, HD = cache_k.shape[2], cache_k.shape[3]
    NE = w_router.shape[1]
    NG, EPG = 4, 4
    DE = w_gate.shape[3]
    NPG = w_pool.shape[1]
    PGD = D // NPG
    WINDOWS = (2, 4, 8, 16)
    PBUF = cache_pool.shape[2]
    EPS, NEG = 1e-6, -1e30
    KC = D // P
    KE = DE // P
    TP = SEQ // P
    TS = TP
    NT = TP + 1
    TOK = SEQ + DEC
    NPAIR = NH // 2
    CT = PAST // P
    NF = TP + CT + 1
    SCALE = HD ** -0.5
    rows = [P] * TP + [DEC]
    col = [t * P for t in range(NT)]

    NASSIGN = 2 * TOK
    NOV = NASSIGN // P
    XROWS = NASSIGN + P
    YROWS = NE * P + NOV * P

    ada_d = nc.dram_tensor("ada_d", (2, 14 * D), fp32, kind="Internal").ap()
    xs_d = nc.dram_tensor("xs_d", (XROWS, D), fp32, kind="Internal").ap()
    ys_d = nc.dram_tensor("ys_d", (YROWS, D), fp32, kind="Internal").ap()
    f_d = nc.dram_tensor("f_d", (NF * NH, P), fp32, kind="Internal").ap()

    NADA = 28
    ada_src = []
    for grp in range(7):
        w, c0 = (ada_w[0], grp * 2048) if grp < 3 else (kv_ada_w, 0) if grp == 3 else (ada_w[1], (grp - 4) * 2048)
        v = w.rearrange("(p k) n -> p k n", k=KC)
        ada_src += [v[:, 2 * u:2 * u + 2, c0:c0 + 2048] for u in range(4)]
    kvf_v = w_kvf.rearrange("(p k) n -> p k n", k=KC)
    q_v = w_q[0].rearrange("(p k) n -> p k n", k=KC)
    o_v = w_o[0].rearrange("(p k) n -> p k n", k=KC)
    proj_src = ([kvf_v[:, :, 512 * c:512 * (c + 1)] for c in range(4)]
                + [q_v[:, :, 512 * c:512 * (c + 1)] for c in range(2)]
                + [o_v[:, :, 512 * c:512 * (c + 1)] for c in range(2)])
    wg_v = w_gate.rearrange("l e (p k) f -> (l e) p (k f)", k=KC)
    wu_v = w_up.rearrange("l e (p k) f -> (l e) p (k f)", k=KC)
    wd_v = w_down.rearrange("l e (p k) f -> (l e) p (k f)", k=KE)
    G_SLOT, U_SLOT, D_SLOT = 0, 2, 4
    NPE = NE // 2

    ada_slot = [n % 6 for n in range(NADA)]
    before0 = [ada_slot.count(s) for s in range(6)]
    before_proj = [n + NPE for n in before0]
    before1 = [n + (4, 4, 0, 0, 0, 0)[s] for s, n in enumerate(before_proj)]
    MOE_BEFORE = [before0, before1]

    ctx = ExitStack()
    with ctx:
        def sb(name, shape, dt=fp32):
            return ctx.enter_context(nc.sbuf_tensor(name, shape, dt))

        def sem(name):
            return ctx.enter_context(nc.semaphore(name))

        x = sb("x", [P, NT, D])
        h = sb("h", [P, NT, D])
        hT_raw = sb("hT_raw", [P, KC * TOK])
        ring = sb("ring", [P, 6, 4096])
        mod = sb("mod", [P, 3, 2, D])
        gainb = sb("gainb", [P, D])
        hT = hT_raw[:, :].rearrange("p (k t) -> p k t", k=KC)
        partT = hT_raw[:, 0:TOK]
        wpool = hT_raw[:, 0:2048].rearrange("p (g k n) -> p g k n", g=NPG, k=2)
        cachep = hT_raw[:, 2048:3072]
        diffT = hT_raw[:, 3072:4096].rearrange("p (c t) -> p c t", c=KC)
        cnti, wtmp = hT_raw[:, 4096:4224], hT_raw[:, 4224:4352]
        hf = h[:, :, :].rearrange("p t d -> p (t d)")
        xg = hf[:, 0:2048].rearrange("p (b n) -> p b n", b=2)
        xgT = hf[:, 2048:4096].rearrange("p (b k t) -> p b k t", b=2, k=KC)
        sg = hf[:, 4096:4608]
        hact = hf[:, 4608:5120]
        hactT = hT_raw[:, 0:512].rearrange("p (k t) -> p k t", k=KE)
        ysb = hT_raw[:, 512:2560].rearrange("p (b n) -> p b n", b=2)
        rf = ring[:, :, :].rearrange("p s n -> p (s n)")
        kk = rf[:, 8192:8192 + NT * D].rearrange("p (t d) -> p t d", t=NT)
        qq = rf[:, 13312:13312 + NT * D].rearrange("p (t d) -> p t d", t=NT)
        vv = rf[:, 18432:18432 + NT * D].rearrange("p (t d) -> p t d", t=NT)
        yg = rf[:, 8192:8192 + NT * 2 * D].rearrange("p (t r n) -> p t r n", t=NT, r=2)
        kT = hf[:, 0:KC * TOK].rearrange("p (k t) -> p k t", k=KC)
        qT = hT
        nfb = rf[:, 0:NH * SEQ].rearrange("p (h t k) -> p h t k", h=NH, t=TP)
        oo = rf[:, 8192:8192 + NT * D].rearrange("p (t d) -> p t d", t=NT)
        qz = rf[:, 13312:13312 + 2 * SEQ].rearrange("p (s t) -> p s t", s=2)
        S_sb = rf[:, 14336:16384].rearrange("p (b n) -> p b n", b=4)
        partT_f = rf[:, 13312:13312 + TOK]
        mf = mod[:, :, :, :].rearrange("p a s d -> p (a s d)")
        PT = rf[:, 23552:24576].rearrange("p (b n) -> p b n", b=2)
        ck = [v.rearrange("p (t n) -> p t n", t=CT) for v in (mf[:, 0:2048], rf[:, 16384:18432])]
        cv = [v.rearrange("p (t n) -> p t n", t=CT) for v in (mf[:, 2048:4096], hT_raw[:, 0:2048])]
        bias_s = [mf[:, 4096:4096 + (CT + 1) * P], hT_raw[:, 2048:2048 + (CT + 1) * P]]
        kTc = [rf[:, 23552:24576], rf[:, 13312:14336]]
        SK = PAST + DEC
        Ss = rf[:, 14336:14336 + SK]
        PTs = hT_raw[:, 3200:3200 + (CT + 1) * P].rearrange("p (t n) -> p t n", t=CT + 1)

        ident = sb("ident", [P, P])
        identb = sb("identb", [P, P], bf16)
        causal = sb("causal", [P, P], bf16)
        smask = sb("smask", [P, DEC])
        tri_s = sb("tri_s", [P, P])
        tri_i = sb("tri_i", [P, P])
        ones = sb("ones", [P, P])
        bands = sb("bands", [P, 3, NPG, P])
        wrf = sb("wrf", [P, KC, 2, NE])
        sel = sb("sel", [P, 2, NE])
        stage = sb("stage", [P, 2, 512])
        adab = sb("adab", [P, 2, 512])
        cs = sb("cs", [P, 2, KC])
        csl = sb("csl", [P, 2, KC])
        cT = sb("cT", [P, KC, 32])
        ssq = sb("ssq", [P, NT])
        eps = sb("eps", [P, 1])
        rstd = sb("rstd", [P, NT])
        brb = sb("brb", [P, NE])
        bfb = sb("bfb", [P, NH])
        knb = sb("knb", [P, HD])
        qnb = sb("qnb", [P, HD])
        valid = sb("valid", [P, NT])
        desc4 = sb("desc4", [P, 4])
        iotae = sb("iotae", [P, NE])
        iotaj = sb("iotaj", [P, NOV])
        L = sb("L", [P, NT, NE])
        sc = sb("sc", [P, NT, NE])
        selv = sb("selv", [P, NT, NE])
        pm = sb("pm", [P, 4, NT * NG, 2])
        m4 = sb("m4", [P, 4, NT, 4])
        best = sb("best", [P, NT, NG])
        vj = sb("vj", [P, NT, EPG])
        one = sb("one", [P, 2, NT, EPG])
        oh = sb("oh", [P, 2, NT, NE])
        Mb = sb("Mb", [P, NT, NE])
        t5 = sb("t5", [P, 8, NT])
        wts = sb("wts", [P, 2, NT])
        tot = sb("tot", [P, NT, NE])
        rank = sb("rank", [P, NT, NE])
        cnt = sb("cnt", [P, NE])
        offs = sb("offs", [P, NE])
        ovc = sb("ovc", [P, NE])
        ovs = sb("ovs", [P, NE])
        e16 = sb("e16", [P, 4, NE])
        nfh = gainb[:, :].rearrange("p (s k) -> p s k", s=2)
        o_s = gainb[0:DEC, :]
        onesr = sb("onesr", [P, NE])
        prod = sb("prod", [P, NT, NE])
        posf = sb("posf", [P, 2, 2, NT])
        posi = sb("posi", [P, 2, 2, NT], i32)
        tabf = sb("tabf", [P, NE + 2 * NOV + 1])
        tabi = sb("tabi", [P, NE + 2 * NOV + 1], i32)
        LF = sb("LF", [P, NF, NH])
        fqs = sb("fqs", [P, 4])
        mx = sb("mx", [P, 8, 4])
        rs = sb("rs", [P, 8, 2])
        bandf = bands[:, :, :, :].rearrange("p a g n -> p (a g n)")
        Fs = bandf[:, 0:NF * NH].rearrange("p (t n) -> p t n", t=NF)
        tF = bandf[:, 256:256 + NF * NH].rearrange("p (t n) -> p t n", t=NF)
        fT = bandf[:, 512:768].rearrange("p (a n) -> p a n", a=2)
        z = bandf[:, 768:768 + NT * NH].rearrange("p (t n) -> p t n", t=NT)
        za = bandf[:, 896:896 + NT * NH].rearrange("p (t n) -> p t n", t=NT)
        ss = bandf[:, 1024:1024 + NT * NH].rearrange("p (t n) -> p t n", t=NT)
        qbs = stage[:, 1, 0:128].rearrange("p (a q) -> p a q", a=2)
        kns = stage[:, 1, 128:192].rearrange("p (a t) -> p a t", a=2)
        ind = bandf[:, 1104:1104 + 3 * NOV * NE].rearrange("p (a j e) -> p a j e", a=3, j=NOV)
        qbd = stage[:, 0, :].rearrange("p (j a q) -> p j a q", j=NPAIR, a=2)
        pb = [ctx.enter_context(nc.psum_tensor(f"pb{i}", [P, 512], fp32)) for i in range(8)]

        consts = sem("consts")
        bands_ready = sem("bands_ready")
        cachep_zero = sem("cachep_zero")
        cachep_loaded = sem("cachep_loaded")
        slot_loaded = [sem(f"slot{i}_loaded") for i in range(6)]
        unit_used = sem("unit_used")
        x_loaded = sem("x_loaded")
        small_loaded = sem("small_loaded")
        tail_stored = sem("tail_stored")
        rows_filled = sem("rows_filled")
        c_loaded = sem("c_loaded")
        c_silu = sem("c_silu")
        c_ready = sem("c_ready")
        bias_loaded = [sem(f"adab{i}_loaded") for i in range(2)]
        ada_staged = sem("ada_staged")
        ada_stored = [sem(f"ada{i}_stored") for i in range(7)]
        ab_loaded = sem("ab_loaded")
        a_ready = sem("a_ready")
        g_loaded = sem("g_loaded")
        gp_ready = sem("gp_ready")
        adab_zero = sem("adab_zero")
        qk_sq = sem("qk_sq")
        at_nf = sem("at_nf")
        g_free = sem("g_free")
        squares = sem("squares")
        root_ready = sem("root_ready")
        h_ready = sem("h_ready")
        mix_diff = sem("mix_diff")
        mix_diffT = sem("mix_diffT")
        mix_y = sem("mix_y")
        mix_added = sem("mix_added")
        hist_stored = sem("hist_stored")
        tr_done = sem("tr_done")
        tr_act = sem("tr_act")
        tr_dve = sem("tr_dve")
        logits_done = sem("logits_done")
        l_ready = sem("l_ready")
        exp_ready = sem("exp_ready")
        pick_ready = sem("pick_ready")
        rank_done = sem("rank_done")
        rows_ready = sem("rows_ready")
        pos_ready = sem("pos_ready")
        scattered = sem("scattered")
        xg_loaded = [sem(f"xg{i}_loaded") for i in range(2)]
        y_stored = [sem(f"y{i}_stored") for i in range(2)]
        yg_loaded = [sem(f"yg{i}_loaded") for i in range(NT)]
        combined = sem("combined")
        yg_scaled = sem("yg_scaled")
        out_stored = sem("out_stored")
        chain_v = sem("chain_v")
        chain_p = sem("chain_p")
        proj_done = sem("proj_done")
        proj_act = sem("proj_act")
        proj_dve = sem("proj_dve")
        f_done = sem("f_done")
        o_sample = sem("o_sample")
        part_done = sem("part_done")
        part_copied = sem("part_copied")
        f_abs = sem("f_abs")
        f_exp = sem("f_exp")
        f_1p = sem("f_1p")
        f_ln = sem("f_ln")
        lf_ready = sem("lf_ready")
        clogf_loaded = sem("clogf_loaded")
        csum_done = sem("csum_done")
        F_ready = sem("F_ready")
        fT_done = sem("fT_done")
        fT_ready = sem("fT_ready")
        f_stored = sem("f_stored")
        nfb_loaded = sem("nfb_loaded")
        kv_out = sem("kv_out")
        qk_ss = sem("qk_ss")
        qk_root = sem("qk_root")
        qk_ready = sem("qk_ready")
        at_q = sem("at_q")
        at_s = sem("at_s")
        at_add = sem("at_add")
        at_nb = sem("at_nb")
        at_exp = sem("at_exp")
        at_rinv = sem("at_rinv")
        at_t = sem("at_t")
        at_pt = sem("at_pt")
        at_pv = sem("at_pv")
        at_o = sem("at_o")
        ck_loaded = [sem(f"ck{i}_loaded") for i in range(2)]
        sa_loaded = [sem(f"sa{i}_loaded") for i in range(2)]
        sa_q = sem("sa_q")
        sa_kt = sem("sa_kt")
        sa_kte = sem("sa_kte")
        sa_s = sem("sa_s")
        sa_nb = sem("sa_nb")
        sa_exp = sem("sa_exp")
        sa_rinv = sem("sa_rinv")
        sa_t = sem("sa_t")
        sa_pt = sem("sa_pt")
        sa_pv = sem("sa_pv")
        sa_o = sem("sa_o")
        sa_chain = sem("sa_chain")
        passed_sp = sem("passed_sp")
        passed_dve = sem("passed_dve")
        norm_mul = sem("norm_mul")
        o_done = sem("o_done")
        o_added = sem("o_added")

        class ExpertSems:

            def __init__(self, name):
                self.tx = sem(name + "_tx")
                self.xt_act = sem(name + "_xt_act")
                self.xt_dve = sem(name + "_xt_dve")
                self.gate = sem(name + "_gate")
                self.up = sem(name + "_up")
                self.silu = sem(name + "_silu")
                self.hact = sem(name + "_hact")
                self.th = sem(name + "_th")
                self.hactT = sem(name + "_hactT")
                self.down = sem(name + "_down")
                self.ys_act = sem(name + "_ys_act")
                self.ys_dve = sem(name + "_ys_dve")

        E = ExpertSems("ex")

        ov_w = [sem(f"ov{i}_w") for i in range(2)]
        ov_x = [sem(f"ov{i}_x") for i in range(2)]
        ov_y = [sem(f"ov{i}_y") for i in range(2)]
        ov_pe = [sem(f"ov{i}_pe") for i in range(2)]
        ov_act = [sem(f"ov{i}_act") for i in range(2)]
        ov_dve = [sem(f"ov{i}_dve") for i in range(2)]

        def bc(ap, n, axis):
            a = ap.unsqueeze(axis)
            shape = list(a.shape)
            shape[axis] = n
            return a.to_broadcast(shape)

        block = ctx.enter_context(nc.Block())

        STAGES = [(0, 1, norm_g[0, 0]), (3, 4, norm_g[0, 1]), (6, 7, kv_norm), (8, 9, norm_g[1, 0]),
                  (11, 12, norm_g[1, 1])]
        GATES = [2, 5, 10, 13]
        SMALL = 16 * 7
        NORM_DONE = [NT * (m + 1) for m in range(5)]
        TRN = 2 * NT

        @block.sync
        def _(sp):
            def load(slot, src):
                dst = ring[:, slot, :]
                if len(src.shape) == 3:
                    dst = dst.rearrange("p (k n) -> p k n", k=src.shape[1])
                sp.dma_start(dst, src).then_inc(slot_loaded[slot], 16)

            sp.dma_start(cs[:, 0, :], c_prompt[0].rearrange("(p k) -> p k", k=KC)).then_inc(c_loaded, 16)
            sp.dma_start(cs[:, 1, :], c_sample[0].rearrange("(p k) -> p k", k=KC)).then_inc(c_loaded, 16)
            load(0, ada_src[0])
            load(1, ada_src[1])
            for t in range(TP):
                sp.dma_start(x[:, t, :], x_prompt[0, t * P:(t + 1) * P, :]).then_inc(x_loaded, 16)
            sp.dma_start(x[0:DEC, TS, :], x_sample[0]).then_inc(x_loaded, 16)
            for n in range(2, NADA):
                if n >= 6:
                    sp.wait_ge(unit_used, n - 5)
                if n >= 4:
                    sp.wait_ge(slot_loaded[ada_slot[n - 2]], 16 * ((n - 2) // 6 + 1))
                load(ada_slot[n], ada_src[n])

            def experts(layer):
                e0 = layer * NE

                def w(view, e):
                    return view[e0 + e] if isinstance(e, int) else \
                        view[bass.ds(e + e0, 1), :, :].rearrange("o p n -> p (o n)")

                def first(kind, e):
                    view, slot = {"g": (wg_v, G_SLOT + e), "u": (wu_v, U_SLOT + e), "d": (wd_v, D_SLOT + e)}[kind]
                    if layer == 0:
                        last = max(n for n in range(NADA) if ada_slot[n] == slot)
                        sp.wait_ge(unit_used, last + 1)
                    elif kind == "g":
                        sp.wait_ge(o_done, 2 * NT)
                    else:
                        sp.wait_ge(tr_done, 2 * NT * 6)
                    load(slot, w(view, e))

                def turn(e, par):
                    sp.wait_ge(E.gate, e + (e0 - 1))
                    load(G_SLOT + par, w(wg_v, e))
                    sp.wait_ge(E.down, 2 * e + (2 * e0 - 4))
                    load(D_SLOT + 1 - par, w(wd_v, e - 1))
                    sp.wait_ge(E.up, e + (e0 - 1))
                    load(U_SLOT + par, w(wu_v, e))

                order = ["g0", "u0", "g1", "d0", "u1"] if layer == 0 else ["u0", "d0", "u1", "g0", "g1"]
                for n, (kind, e) in enumerate(order):
                    if layer == 0 and n == 2:
                        sp.wait_ge(xg_loaded[1], 16)
                    first(kind, int(e))
                sp.wait_ge(E.gate, e0 + 1)
                load(G_SLOT, w(wg_v, 2))
                first("d", 1)
                sp.wait_ge(E.up, e0 + 1)
                load(U_SLOT, w(wu_v, 2))
                turn(3, 1)
                with sp.Fori(2, NPE) as i:
                    turn(2 * i, 0)
                    turn(2 * i + 1, 1)
                sp.wait_ge(E.down, 2 * (e0 + NE - 2))
                load(D_SLOT + 1, w(wd_v, NE - 1))
                sp.wait_ge(pos_ready, layer + 1)
                n_ov = sp.value_load(tabi[0:1, NE + 2 * NOV:NE + 2 * NOV + 1], min_val=0, max_val=NOV)
                with sp.If(n_ov > 0):
                    sp.wait_ge(E.down, 2 * (e0 + NE))
                    with sp.Fori(0, n_ov) as j:
                        e = sp.value_load(tabi[0:1, bass.ds(j + NE, 1)], min_val=0, max_val=NE - 1)
                        for view, slot in ((wg_v, G_SLOT), (wu_v, U_SLOT), (wd_v, D_SLOT)):
                            sp.dma_start(ring[:, slot, :], w(view, e)).then_inc(ov_w[layer], 16)
                        sp.wait_ge(ov_y[layer], 16 * j + 16)
                        sp.sem_inc(passed_sp, 1)

            experts(0)
            for n in range(6):
                if n < 2:
                    sp.wait_ge(E.gate, NE - 1 + n)
                else:
                    sp.wait_ge(proj_done, NT * (n - 1))
                load(n % 2, proj_src[n])
            sp.wait_ge(proj_act, 2 * NT)
            sp.wait_ge(proj_dve, 2 * NT)
            sp.dma_start(v_prompt[0].rearrange("(t p) h d -> p t (h d)", p=P), vv[:, 0:TP, :]).then_inc(kv_out, 16)
            sp.dma_start(v_sample[0].rearrange("p h d -> p (h d)"), vv[0:DEC, TS, :]).then_inc(kv_out, 16)
            sp.wait_ge(lf_ready, 1)
            sp.dma_start(logf_prompt[0].rearrange("(t p) h -> p t h", p=P), LF[:, 0:TP, :]).then_inc(kv_out, 16)
            sp.dma_start(logf_sample[0], LF[0:DEC, NF - 1, :]).then_inc(kv_out, 16)
            sp.wait_ge(qk_ready, NT)
            sp.dma_start(k_prompt[0].rearrange("(t p) h d -> p t (h d)", p=P), kk[:, 0:TP, :]).then_inc(kv_out, 16)
            sp.dma_start(k_sample[0].rearrange("p h d -> p (h d)"), kk[0:DEC, TS, :]).then_inc(kv_out, 16)
            sp.wait_ge(at_o, TP * NH + 1)
            for n in range(6, 8):
                load(n % 2, proj_src[n])
            experts(1)
            for t in range(NT):
                sp.wait_ge(combined, NT + t + 1)
                dst = y_prompt[0, t * P:(t + 1) * P, :] if t < TP else y_sample[0]
                sp.dma_start(dst, x[0:rows[t], t, :]).then_inc(out_stored, 16)
            sp.wait_ge(kv_out, 16 * 6)
            sp.wait_ge(hist_stored, 32)
            sp.wait_ge(out_stored, 16 * NT)

        @block.gpsimd
        def _(pool):
            g = nc.gpsimd
            count = [0]

            def link(ins):
                count[0] += 1
                ins.then_inc(chain_p, 1)
                pool.wait_ge(chain_p, count[0])

            def fill_where(m, cmp, fill, base, pattern, cm):
                return g.affine_select(out=m, in_=m, compare_op=cmp, fill=fill, base=base,
                                       pattern=pattern, channel_multiplier=cm)

            link(g.memset(ident[:, :], 0.0))
            link(fill_where(ident[:, :], ALU.not_equal, 1.0, 0, [[-1, P]], 1))
            link(g.memset(bands[:, :, :, :], 0.0))
            for i, w in enumerate(WINDOWS):
                link(g.memset(bands[:, 0, i, :], 1.0 / w))
                link(fill_where(bands[:, 0, i, :], ALU.is_ge, 0.0, 0, [[1, P]], -1))
                link(fill_where(bands[:, 0, i, :], ALU.is_ge, 0.0, w - 1, [[-1, P]], 1))
                link(g.memset(bands[:, 2, i, :], 1.0 / w))
                link(fill_where(bands[:, 2, i, :], ALU.is_ge, 0.0, w - 1 - P, [[-1, P]], 1))
                link(g.memset(bands[:, 1, i, :], 1.0))
                link(fill_where(bands[:, 1, i, :], ALU.is_ge, 0.0, 0, [[1, P]], -1))
                link(fill_where(bands[:, 1, i, :], ALU.is_ge, 0.0, w - 1, [[-1, P]], 1))
            link(g.iota(cnti[:, :], pattern=[[1, P]], base=1, channel_multiplier=0,
                        allow_small_or_imprecise_dtypes=True))
            link(g.memset(tri_s[:, :], 1.0))
            link(g.memset(tri_i[:, :], 1.0))
            link(fill_where(tri_s[:, :], ALU.is_gt, 0.0, 0, [[1, P]], -1))
            link(fill_where(tri_i[:, :], ALU.is_ge, 0.0, 0, [[1, P]], -1))
            link(g.memset(ones[:, :], 1.0))
            link(g.memset(causal[:, :], 0.0))
            link(fill_where(causal[:, :], ALU.is_ge, NEG, 0, [[-1, P]], 1))
            link(g.memset(smask[:, :], 0.0))
            for j in range(4):
                part = smask[32 * j:32 * j + 32, :]
                link(fill_where(part, ALU.is_ge, NEG, 0, [[-1, DEC]], 1))
            link(g.memset(valid[:, :], 1.0))
            link(fill_where(valid[:, TS:TS + 1], ALU.is_ge, 0.0, DEC - 1, [[0, 1]], -1))
            link(g.iota(iotae[:, :], pattern=[[1, NE]], base=0, channel_multiplier=0,
                        allow_small_or_imprecise_dtypes=True))
            link(g.iota(iotaj[:, :], pattern=[[1, NOV]], base=0, channel_multiplier=0,
                        allow_small_or_imprecise_dtypes=True))
            link(g.iota(desc4[:, :], pattern=[[-1, 4]], base=4, channel_multiplier=0,
                        allow_small_or_imprecise_dtypes=True))
            link(g.memset(onesr[:, :], 1.0))
            g.memset(LF[:, :, :], 0.0).then_inc(consts, 1)

            def load_ab(m):
                shift, scale, gain = STAGES[m]
                if m:
                    pool.wait_ge(h_ready, NORM_DONE[m - 1])
                for v in (shift, scale):
                    pool.wait_ge(ada_stored[v // 2], 32)
                for v, a in ((scale, 0), (shift, 1)):
                    g.dma_start(mod[:, a, 0, :], ada_d[0:1, v * D:(v + 1) * D].to_broadcast([P, D])).then_inc(ab_loaded, 16)
                    g.dma_start(mod[0:DEC, a, 1, :], ada_d[1:2, v * D:(v + 1) * D].to_broadcast([DEC, D])).then_inc(ab_loaded, 16)
                if m:
                    pool.wait_ge(a_ready, m)
                if m == 1:
                    pool.wait_ge(gp_ready, 1)
                g.dma_start(gainb[:, :], gain.unsqueeze(0).to_broadcast([P, D])).then_inc(ab_loaded, 16)

            def load_g(i):
                v = GATES[i]
                pool.wait_ge(ada_stored[v // 2], 32)
                if i:
                    pool.wait_ge(g_free, i)
                g.dma_start(mod[:, 2, 0, :], ada_d[0:1, v * D:(v + 1) * D].to_broadcast([P, D])).then_inc(g_loaded, 16)
                g.dma_start(mod[0:DEC, 2, 1, :], ada_d[1:2, v * D:(v + 1) * D].to_broadcast([DEC, D])).then_inc(g_loaded, 16)

            load_ab(0)
            load_g(0)
            pool.wait_ge(a_ready, 1)
            g.dma_start(gainb[:, :], pool_scale[0:1, :].to_broadcast([P, D])).then_inc(g_loaded, 16)
            load_ab(1)
            g.dma_start(xs_d[NASSIGN:XROWS, :], x_prompt[0, 0:P, :]).then_inc(tail_stored, 16)
            load_g(1)

            def dispatch(layer):
                pool.wait_ge(rows_ready, layer + 1)
                pool.wait_ge(tail_stored, 16)
                for t in range(NT):
                    for r in range(2):
                        g.indirect_dma_start(
                            out=xs_d[:, :], out_offset=bass.IndirectOffsetOnAxis(ap=posi[0:rows[t], 0, r, t:t + 1], axis=0),
                            in_=h[0:rows[t], t, :], in_offset=None).then_inc(scattered, 16)

                def load_x(i, par, e):
                    off = pool.value_load(tabi[0:1, bass.ds(e, 1)] if not isinstance(e, int) else tabi[0:1, e:e + 1],
                                          min_val=0, max_val=NASSIGN)
                    g.dma_start(xg[:, par, :], xs_d[bass.ds(off, P), :]).then_inc(xg_loaded[par], 16)

                pool.wait_ge(scattered, 16 * 2 * NT * (layer + 1))
                pool.wait_ge(pos_ready, layer + 1)
                b = layer * NE
                load_x(0, 0, 0)
                load_x(1, 1, 1)
                if layer == 0:
                    load_ab(2)

                def step(e, par, more):
                    if more:
                        pool.wait_ge(E.tx, 2 * e + (2 * b + 2))
                        load_x(None, par, e + 2)
                    pool.wait_ge(E.ys_act, e + (b + 1))
                    pool.wait_ge(E.ys_dve, e + (b + 1))
                    row = e * P
                    dst = ys_d[row:row + P, :] if isinstance(e, int) else ys_d[bass.ds(row, P), :]
                    g.dma_start(dst, ysb[:, par, :]).then_inc(y_stored[par], 16)

                with pool.Fori(0, NE // 2 - 1) as i:
                    for par in range(2):
                        step(2 * i + par, par, True)
                if layer == 0:
                    for j in range(0, NOV, TP):
                        n = min(TP, NOV - j) * P
                        g.dma_start(ys_d[(NE + j) * P:(NE + j) * P + n, :], x_prompt[0, 0:n, :]).then_inc(rows_filled, 16)
                step(NE - 2, 0, False)
                step(NE - 1, 1, False)
                n_ov = pool.value_load(tabi[0:1, NE + 2 * NOV:NE + 2 * NOV + 1], min_val=0, max_val=NOV)
                for par in range(2):
                    pool.wait_ge(y_stored[par], 16 * (NE // 2) * (layer + 1))
                pool.wait_ge(rows_filled, 16 * ((NOV + TP - 1) // TP))
                with pool.If(n_ov > 0):
                    with pool.Fori(0, n_ov) as j:
                        off = pool.value_load(tabi[0:1, bass.ds(NE + NOV + j, 1)], min_val=0, max_val=NASSIGN)
                        g.dma_start(xg[:, 0, :], xs_d[bass.ds(off, P), :]).then_inc(ov_x[layer], 16)
                        pool.wait_ge(ov_act[layer], 4 * j + 4)
                        pool.wait_ge(ov_dve[layer], 3 * j + 3)
                        g.dma_start(ys_d[bass.ds(j * P + NE * P, P), :], ysb[:, 0, :]).then_inc(ov_y[layer], 16)
                        pool.wait_ge(ov_y[layer], 16 * j + 16)
                for t in range(NT):
                    for r in range(2):
                        g.indirect_dma_start(
                            out=yg[0:rows[t], t, r, :], out_offset=None, in_=ys_d[:, :],
                            in_offset=bass.IndirectOffsetOnAxis(ap=posi[0:rows[t], 1, r, t:t + 1], axis=0),
                        ).then_inc(yg_loaded[t], 16)

            dispatch(0)
            load_ab(3)
            pool.wait_ge(f_stored, 32)
            for half in range(2):
                pool.wait_ge(proj_done, NT * (5 + half))
                for t in range(TP):
                    h0, n = half * NH // 2, NH // 2
                    src = f_d[t * NH + h0:t * NH + h0 + n, :].unsqueeze(0).to_broadcast([P, n, P])
                    g.dma_start(nfb[:, h0:h0 + n, t, :], src).then_inc(nfb_loaded, 16)
            pool.wait_ge(tr_done, 2 * NT * 5)
            ckv = cache_k[0].rearrange("(t p) (g h) d -> g p t (h d)", p=P, g=4)
            cvv = cache_v[0].rearrange("(t p) (g h) d -> g p t (h d)", p=P, g=4)
            fv = f_d.rearrange("(i g j) k -> g j i k", g=4, j=4)

            def load_keys(gi):
                g.dma_start(ck[gi % 2], ckv[gi]).then_inc(ck_loaded[gi % 2], 16)

            def load_values(gi):
                b = gi % 2
                g.dma_start(cv[b], cvv[gi]).then_inc(sa_loaded[b], 16)
                for j in range(4):
                    src = fv[gi, j, TP:NF, :].unsqueeze(0)
                    g.dma_start(bias_s[b][32 * j:32 * j + 32, :].rearrange("p (i k) -> p i k", i=CT + 1),
                                src.to_broadcast([32, CT + 1, P])).then_inc(sa_loaded[b], 16)

            load_keys(0)
            load_values(0)
            load_keys(1)
            pool.wait_ge(nfb_loaded, 2 * 16 * TP)
            for s in range(2):
                g.tensor_copy(nfh[:, s, :], nfb[:, s, :, :].rearrange("p t k -> p (t k)")).then_inc(at_nf, 1)
            with pool.Fori(1, NPAIR) as j:
                for s in range(2):
                    pool.wait_ge(at_add, 2 * TP * j + TP * (s - 1))
                    g.tensor_copy(nfh[:, s, :], nfb[:, bass.ds(2 * j + s, 1), :, :].rearrange(
                        "p o t k -> p (o t k)")).then_inc(at_nf, 1)
            pool.wait_ge(at_o, TP * NH + 1)
            load_values(1)
            for gi in range(2, 4):
                pool.wait_ge(sa_kt, 4 * gi - 4)
                load_keys(gi)
                pool.wait_ge(sa_o, 2 * gi - 2)
                load_values(gi)
            pool.wait_ge(sa_o, 8)
            load_g(2)
            load_ab(4)
            load_g(3)
            dispatch(1)

        @block.tensor
        def _(pe):
            T = nc.tensor

            def ada(grp, units=range(4)):
                bank = pb[grp % 2]
                if grp >= 2 and units[0] == 0:
                    pe.wait_ge(ada_staged, grp - 1)
                for u in units:
                    n = 4 * grp + u
                    pe.wait_ge(slot_loaded[ada_slot[n]], 16 * (n // 6 + 1))
                    w = ring[:, ada_slot[n], :].rearrange("p (k j n) -> p k j n", k=2, j=4)
                    for k in range(2):
                        for j in range(4):
                            last = T.matmul(bank[32 * j:32 * j + 32, :], cT[:, 2 * u + k, :], w[:, k, j, :],
                                            start=(u == 0 and k == 0), stop=(u == 3 and k == 1),
                                            tile_position=(0, 32 * j))
                    last.then_inc(unit_used, 1)

            def transposes(src, idx, srcready, half_cols, tiles=range(NT)):
                for t in tiles:
                    srcready(t)
                    for b in range(2):
                        s = idx * NT + t
                        if s:
                            pe.wait_ge((tr_act, tr_dve)[b], s)
                        for c in range(4):
                            last = T.transpose(pb[2 + b][:, c * P:c * P + rows[t]], half_cols(src, t, 4 * b + c),
                                               ident[0:rows[t], 0:rows[t]])
                        last.then_inc(tr_done, 1)

            def by_stride(src, t, k):
                return src[0:rows[t], t, k:D:KC]

            def by_chunk(src, t, k):
                return src[0:rows[t], t, k * P:(k + 1) * P]

            def h_transposed(idx, stage_no, t):
                transposes(h, idx, lambda t: pe.wait_ge(h_ready, NORM_DONE[stage_no] - NT + t + 1), by_stride, [t])

            def narrow_product(turn, banks, which, part, done):
                for bank, c0, n in ((pb[banks[0]], 0, SEQ), (pb[banks[1]], SEQ, DEC)):
                    for i in range(KC // 4):
                        for j in range(4):
                            k = j * KC // 4 + i
                            last = T.matmul(bank[32 * j:32 * j + 32, 0:n], wrf[:, k, :, :].rearrange("p a e -> p (a e)"),
                                            hT[:, k, c0:c0 + n], start=(i == 0), stop=(i == KC // 4 - 1),
                                            tile_position=(0, 32 * j))
                last.then_inc(part_done, 1)
                pe.wait_ge(part_copied, 2 * turn)
                for t in range(NT):
                    last = T.matmul(pb[6][0:rows[t], t * NE:(t + 1) * NE], part[:, col[t]:col[t] + rows[t]],
                                    sel[:, which, :], start=True, stop=True)
                last.then_inc(done, 1)

            def route(layer):
                for t in range(NT) if layer == 0 else range(TP - 1, NT):
                    h_transposed(6 * layer, 4 * layer or 1, t)
                s = 6 * layer * NT
                pe.wait_ge(tr_act, s + NT)
                pe.wait_ge(tr_dve, s + NT)
                narrow_product((1, 3)[layer], (4, 5), 0, partT, logits_done)

            def ranks(layer):
                pe.wait_ge(pick_ready, layer + 1)
                m = Mb[:, :, :].rearrange("p t e -> p (t e)")
                T.matmul(pb[6][:, 128:128 + NT * NE], tri_s[:, :], m, start=True, stop=True)
                T.matmul(pb[7][:, 128:128 + NT * NE], ones[:, :], m, start=True, stop=True).then_inc(rank_done, 1)

            def pe_tx(S, i, b, par):
                for half, done in enumerate((S.xt_act, S.xt_dve)):
                    if not (isinstance(i, int) and i + b == 0):
                        pe.wait_ge(done, i + b)
                    for c in range(4):
                        last = T.transpose(pb[half][:, c * P:(c + 1) * P], xg[:, par, 4 * half + c:D:KC], ident[:, :])
                    last.then_inc(S.tx, 1)

            def pe_gate(S, i, b, par, w, ks):
                for k in ks:
                    if k == 0:
                        pe.wait_ge(S.xt_act, i + (b + 1))
                        pe.wait_ge(S.xt_dve, i + (b + 1))
                        if not (isinstance(i, int) and i + b == 0):
                            pe.wait_ge(S.silu, i + b)
                    last = T.matmul(pb[3][:, :], xgT[:, par, k, :], w[:, k * DE:(k + 1) * DE],
                                    start=(k == 0), stop=(k == KC - 1))
                if ks[-1] == KC - 1:
                    last.then_inc(S.gate, 1)
                return last

            def pe_up(S, i, b, par, w):
                if not (isinstance(i, int) and i + b == 0):
                    pe.wait_ge(S.hact, i + b)
                for k in range(KC):
                    last = T.matmul(pb[4][:, :], xgT[:, par, k, :], w[:, k * DE:(k + 1) * DE],
                                    start=(k == 0), stop=(k == KC - 1))
                last.then_inc(S.up, 1)

            def pe_th(S, i, b):
                pe.wait_ge(S.hact, i + (b + 1))
                for c in range(KE):
                    last = T.transpose(pb[2][:, c * P:(c + 1) * P], hact[:, c:DE:KE], ident[:, :])
                last.then_inc(S.th, 1)

            def pe_down(S, i, b, w):
                pe.wait_ge(S.hactT, i + (b + 1))
                for half, done in enumerate((S.ys_act, S.ys_dve)):
                    if not (isinstance(i, int) and i + b == 0):
                        pe.wait_ge(done, i + b)
                    for k in range(KE):
                        last = T.matmul(pb[5 + half][:, :], hactT[:, k, :],
                                        w[:, k * D + 512 * half:k * D + 512 * half + 512],
                                        start=(k == 0), stop=(k == KE - 1))
                    last.then_inc(S.down, 1)

            def experts(layer):
                e0, before = layer * NE, MOE_BEFORE[layer]

                def unit(slot, i):
                    pe.wait_ge(slot_loaded[slot], 16 * i + 16 * (before[slot] + 1))
                    return ring[:, slot, :]

                def tokens(i, par):
                    pe.wait_ge(xg_loaded[par], 16 * i + 16 * (layer * NPE + 1))

                def step(i, par):
                    e = 2 * i + par
                    pe_up(E, e, e0, par, unit(U_SLOT + par, i))
                    tokens(i + par, 1 - par)
                    pe_tx(E, e + 1, e0, 1 - par)
                    w = unit(G_SLOT + 1 - par, i + par)
                    pe_gate(E, e + 1, e0, 1 - par, w, range(0, KC // 2))
                    pe_th(E, e, e0)
                    pe_gate(E, e + 1, e0, 1 - par, w, range(KC // 2, KC))
                    pe_down(E, e, e0, unit(D_SLOT + par, i))

                tokens(0, 0)
                pe_tx(E, 0, e0, 0)
                pe_gate(E, 0, e0, 0, unit(G_SLOT, 0), range(KC))
                step(0, 0)
                step(0, 1)
                with pe.Fori(1, NPE - 1) as i:
                    step(i, 0)
                    step(i, 1)
                step(NPE - 1, 0)
                pe_up(E, NE - 1, e0, 1, unit(U_SLOT + 1, NPE - 1))
                pe_th(E, NE - 1, e0)
                pe_down(E, NE - 1, e0, unit(D_SLOT + 1, NPE - 1))
                n_ov = pe.value_load(tabi[0:1, NE + 2 * NOV:NE + 2 * NOV + 1], min_val=0, max_val=NOV)
                with pe.If(n_ov > 0):
                    pe.wait_ge(E.ys_act, e0 + NE)
                    pe.wait_ge(E.ys_dve, e0 + NE)
                    with pe.Fori(0, n_ov) as j:
                        pe.wait_ge(ov_w[layer], 48 * j + 48)
                        pe.wait_ge(ov_x[layer], 16 * j + 16)
                        for half in range(2):
                            for c in range(4):
                                last = T.transpose(pb[half][:, c * P:(c + 1) * P], xg[:, 0, 4 * half + c:D:KC], ident[:, :])
                            last.then_inc(ov_pe[layer], 1)
                        pe.wait_ge(ov_act[layer], 4 * j + 1)
                        pe.wait_ge(ov_dve[layer], 3 * j + 1)
                        for bank, slot in ((3, G_SLOT), (4, U_SLOT)):
                            for k in range(KC):
                                last = T.matmul(pb[bank][:, :], xgT[:, 0, k, :], ring[:, slot, k * DE:(k + 1) * DE],
                                                start=(k == 0), stop=(k == KC - 1))
                            last.then_inc(ov_pe[layer], 1)
                        pe.wait_ge(ov_dve[layer], 3 * j + 2)
                        for c in range(KE):
                            last = T.transpose(pb[2][:, c * P:(c + 1) * P], hact[:, c:DE:KE], ident[:, :])
                        last.then_inc(ov_pe[layer], 1)
                        pe.wait_ge(ov_act[layer], 4 * j + 3)
                        for half in range(2):
                            for k in range(KE):
                                last = T.matmul(pb[5 + half][:, :], hactT[:, k, :],
                                                ring[:, D_SLOT, k * D + 512 * half:k * D + 512 * half + 512],
                                                start=(k == 0), stop=(k == KE - 1))
                            last.then_inc(ov_pe[layer], 1)
                        pe.wait_ge(ov_act[layer], 4 * j + 4)
                        pe.wait_ge(ov_dve[layer], 3 * j + 3)

            pe.wait_ge(c_ready, 1)
            for grp in range(3):
                ada(grp)
            pe.wait_ge(consts, 1)
            pe.wait_ge(bands_ready, 1)
            pe.wait_ge(small_loaded, SMALL)
            pe.wait_ge(cachep_loaded, 16)

            def differences(t):
                pe.wait_ge(h_ready, t + 1)
                r = rows[t]
                prev = None if t == 0 else (cachep if t == TS else h[:, t - 1, :])
                for b in range(2):
                    if t:
                        pe.wait_ge(mix_diffT, 2 * t - 1 + b)
                    for c in range(4 * b, 4 * b + 4):
                        grp = c * P // PGD
                        dst = pb[2 + b][:, (c % 4) * P:(c % 4) * P + r]
                        last = T.matmul(dst, h[0:r, t, c * P:(c + 1) * P], bands[0:r, 1 if t == 0 else 0, grp, 0:r],
                                        start=True, stop=prev is None)
                        if prev is not None:
                            last = T.matmul(dst, prev[:, c * P:(c + 1) * P], bands[:, 2, grp, 0:r],
                                            start=False, stop=True)
                    last.then_inc(mix_diff, 1)

            differences(0)
            for t in range(NT):
                r = rows[t]
                if t + 1 < NT:
                    differences(t + 1)
                for b in range(2):
                    pe.wait_ge(mix_diffT, 2 * t + 1 + b)
                    if t:
                        pe.wait_ge(mix_added, 2 * t - 1 + b)
                    for grp in range(2 * b, 2 * b + 2):
                        for k in range(2):
                            last = T.matmul(pb[4 + b][0:r, (grp % 2) * PGD:(grp % 2 + 1) * PGD],
                                            diffT[:, 2 * grp + k, 0:r], wpool[:, grp, k, :],
                                            start=(k == 0), stop=(k == 1))
                    last.then_inc(mix_y, 1)
                if t < 4:
                    ada(3, [t])
            ada(4, [0, 1])
            route(0)
            ada(4, [2, 3])
            ada(5, [0, 1])
            ranks(0)
            ada(5, [2, 3])
            ada(6)
            pe.wait_ge(ada_staged, 7)
            experts(0)

            def tile_times_unit(bank, t, w):
                for k in range(KC):
                    if t < TP:
                        last = T.matmul(bank[:, :], hT[:, k, col[t]:col[t] + P], w[:, k * 512:(k + 1) * 512],
                                        start=(k == 0), stop=(k == KC - 1))
                        continue
                    for j in range(4):
                        last = T.matmul(bank[32 * j:32 * j + DEC, 0:P], hT[:, k, SEQ:TOK],
                                        w[:, k * 512 + j * P:k * 512 + (j + 1) * P],
                                        start=(k == 0), stop=(k == KC - 1), tile_position=(0, 32 * j))
                return last

            def project(c):
                u, t = divmod(c, NT)
                w = ring[:, u % 2, :]
                if t == 0:
                    pe.wait_ge(slot_loaded[u % 2], 16 * (before_proj[u % 2] + u // 2 + 1))
                if u in (0, 4):
                    turn = (1 if u == 0 else 2) * NT + t + 1
                    pe.wait_ge(tr_act, turn)
                    pe.wait_ge(tr_dve, turn)
                if c >= 2:
                    pe.wait_ge((proj_act, proj_dve)[c % 2], c // 2)
                tile_times_unit(pb[4 + c % 2], t, w).then_inc(proj_done, 1)

            h_transposed(1, 2, 0)
            for t in range(NT):
                if t + 1 < NT:
                    h_transposed(1, 2, t + 1)
                project(t)
            narrow_product(2, (0, 1), 1, partT_f, f_done)
            for c in range(NT, 2 * NT):
                project(c)
            pe.wait_ge(lf_ready, 1)
            lf = LF[:, :, :].rearrange("p t n -> p (t n)")
            T.matmul(pb[6][:, 0:NF * NH], tri_i[:, :], lf, start=True, stop=True)
            T.matmul(pb[7][:, 0:NF * NH], ones[:, :], lf, start=True, stop=True).then_inc(csum_done, 1)
            for c in range(2 * NT, 3 * NT):
                project(c)
            pe.wait_ge(F_ready, 1)
            ff = Fs[:, :, :].rearrange("p t n -> p (t n)")
            T.transpose(pb[0][:, 0:P], ff[:, 0:P], ident[:, :])
            T.transpose(pb[0][0:NF * NH - P, P:2 * P], ff[:, P:NF * NH], ident[:, :]).then_inc(fT_done, 1)
            for t in range(NT):
                project(3 * NT + t)
                if t:
                    h_transposed(2, 3, t - 1)
            h_transposed(2, 3, TS)
            for t in range(NT):
                project(4 * NT + t)
                transposes(kk, 3, lambda t: pe.wait_ge(qk_ready, t + 1), by_chunk, [t])
            for t in range(NT):
                project(5 * NT + t)
                if t:
                    transposes(qq, 4, lambda t: pe.wait_ge(qk_ready, NT + t + 1), by_chunk, [t - 1])
            transposes(qq, 4, lambda t: pe.wait_ge(qk_ready, NT + t + 1), by_chunk, [TS])

            pe.wait_ge(tr_act, 5 * NT)
            pe.wait_ge(tr_dve, 5 * NT)
            NB = 2 * TP
            with pe.Fori(0, NPAIR) as j:
                def scores(n):
                    s, b = divmod(n, TP)
                    if n % TP == 0:
                        pe.wait_ge(at_q, 2 * j + s + 1)
                    bank = pb[n % 4]
                    if n >= 4:
                        pe.wait_ge(at_add, NB * j + n - 3)
                    if b:
                        T.matmul(bank[:, 0:b * P], qz[:, s, b * P:(b + 1) * P],
                                 kT[:, bass.ds(j, 1), 0:b * P].rearrange("p o t -> p (o t)"), start=True, stop=True)
                    T.matmul(bank[:, b * P:(b + 1) * P], qz[:, s, b * P:(b + 1) * P],
                             kT[:, bass.ds(j, 1), b * P:(b + 1) * P].rearrange("p o t -> p (o t)"), start=True, stop=False)
                    T.matmul(bank[:, b * P:(b + 1) * P], identb[:, :], causal[:, :],
                             start=False, stop=True).then_inc(at_s, 1)

                def turn(n):
                    s, b = divmod(n, TP)
                    pe.wait_ge(at_exp, NB * j + n + 1)
                    if n >= 2:
                        pe.wait_ge(at_pt, NB * j + n - 1)
                    for c in range(b + 1):
                        last = T.transpose(pb[4 + n % 2][:, c * P:(c + 1) * P], S_sb[:, n % 4, c * P:(c + 1) * P], ident[:, :])
                    last.then_inc(at_t, 1)

                def values(n):
                    s, b = divmod(n, TP)
                    pe.wait_ge(at_pt, NB * j + n + 1)
                    pe.wait_ge(at_o, NB * j + max(n, 1))
                    for c in range(b + 1):
                        last = T.matmul(pb[6 + n % 2][:, 0:HD], PT[:, n % 2, c * P:(c + 1) * P],
                                        vv[:, c, bass.ds(j * 2 * HD + s * HD, HD)], start=(c == 0), stop=(c == b))
                    last.then_inc(at_pv, 1)

                scores(0)
                scores(1)
                for n in range(NB):
                    if n + 2 < NB:
                        scores(n + 2)
                    turn(n)
                    if n:
                        values(n - 1)
                values(NB - 1)
            def keys_transposed(gi):
                par, gp = gi % 2, gi // 2
                pe.wait_ge(ck_loaded[par], 16 * gp + 16)
                for a in range(2):
                    for b in range(2):
                        bank = pb[2 * a + b]
                        for c in range(4):
                            last = T.transpose(bank[:, c * P:(c + 1) * P], ck[par][:, 4 * b + c, a * P:(a + 1) * P], ident[:, :])
                        last.then_inc(sa_kt, 1)

            keys_transposed(0)
            for gi in range(4):
                par = gi % 2
                pe.wait_ge(sa_kte, 4 * gi + 4)
                pe.wait_ge(sa_q, gi + 1)
                for a in range(2):
                    for b in range(2):
                        T.matmul(pb[4 + b][64 * a:64 * a + 64, :], qbs[:, a, :], kTc[a][:, 512 * b:512 * b + 512],
                                 start=True, stop=True)
                    last = T.matmul(pb[6][64 * a:64 * a + 64, 0:DEC], qbs[:, a, :],
                                    kns[:, a, :], start=True, stop=True)
                last.then_inc(sa_s, 1)
                pe.wait_ge(sa_exp, gi + 1)
                for c in range(CT):
                    last = T.transpose(pb[c // 4][:, (c % 4) * P:(c % 4 + 1) * P], Ss[:, c * P:(c + 1) * P], ident[:, :])
                T.transpose(pb[2][0:DEC, 0:P], Ss[:, PAST:SK], ident[:, :]).then_inc(sa_t, 1)
                pe.wait_ge(sa_pt, 3 * gi + 3)
                if gi < 3:
                    keys_transposed(gi + 1)
                pe.wait_ge(sa_loaded[par], 80 * (gi // 2 + 1))
                for c in range(CT):
                    T.matmul(pb[7][:, 0:4 * HD], PTs[:, c, :], cv[par][:, c, :], start=(c == 0), stop=False)
                T.matmul(pb[7][:, 0:4 * HD], PTs[0:DEC, CT, :], vv[0:DEC, TS, bass.ds(gi * 4 * HD, 4 * HD)],
                         start=False, stop=True).then_inc(sa_pv, 1)
                pe.wait_ge(sa_o, 2 * gi + 2)
            transposes(oo, 5, lambda t: None, by_stride)
            pe.wait_ge(tr_act, 6 * NT)
            pe.wait_ge(tr_dve, 6 * NT)
            for u in range(2):
                pe.wait_ge(slot_loaded[u], 16 * (before_proj[u] + 4))
            for c in range(2 * NT):
                t, u = divmod(c, 2)
                if c >= 2:
                    pe.wait_ge(o_added, c - 1)
                tile_times_unit(pb[4 + u], t, ring[:, u, :]).then_inc(o_done, 1)
                if u and t >= 2:
                    h_transposed(6, 4, t - 2)
            route(1)
            ranks(1)
            experts(1)

        @block.scalar
        def _(act):
            A = nc.scalar
            A.dma_start(wpool, w_pool[0].rearrange("g (k p) n -> p g k n", p=P)).then_inc(small_loaded, 16)
            A.dma_start(wrf[:, :, 0, :], w_router.rearrange("(p k) e -> p k e", k=KC)).then_inc(small_loaded, 16)
            A.dma_start(wrf[:, :, 1, :], kvf_v[:, :, 2 * D:2 * D + NH]).then_inc(small_loaded, 16)
            A.dma_start(brb[:, :], b_router.unsqueeze(0).to_broadcast([P, NE])).then_inc(small_loaded, 16)
            A.dma_start(bfb[:, :], b_f.unsqueeze(0).to_broadcast([P, NH])).then_inc(small_loaded, 16)
            A.dma_start(knb[:, :], k_norm.unsqueeze(0).to_broadcast([P, HD])).then_inc(small_loaded, 16)
            A.dma_start(qnb[:, :], q_norm[0:1, :].to_broadcast([P, HD])).then_inc(small_loaded, 16)
            act.wait_ge(cachep_zero, 1)
            A.dma_start(cachep[P - PBUF:P, :], cache_pool[0, 0]).then_inc(cachep_loaded, 16)

            def load_bias(grp):
                src = (ada_b[0], grp * 2048) if grp < 3 else (kv_ada_b, 0) if grp == 3 else (ada_b[1], (grp - 4) * 2048)
                if grp >= 2:
                    act.wait_ge(ada_staged, grp - 1)
                for s in range(2):
                    A.dma_start(adab[s:P:32, grp % 2, :],
                                src[0][src[1]:src[1] + 2048].rearrange("(j n) -> j n", j=4)).then_inc(bias_loaded[grp % 2], 16)

            def store_ada(grp):
                act.wait_ge(ada_staged, grp + 1)
                for s in range(2):
                    A.dma_start(ada_d[s, grp * 2048:(grp + 1) * 2048].rearrange("(j n) -> j n", j=4),
                                stage[s:P:32, grp % 2, :]).then_inc(ada_stored[grp], 16)

            act.wait_ge(c_loaded, 32)
            A.activation(csl[:, :, :], cs[:, :, :], ACT.Silu).then_inc(c_silu, 1)
            act.wait_ge(adab_zero, 1)
            load_bias(0)
            load_bias(1)

            def square_root(n, t):
                r = rows[t]
                A.activation(h[0:r, t, :], x[0:r, t, :], ACT.Square, accum_out=ssq[0:r, t:t + 1]).then_inc(squares, 1)
                act.wait_ge(squares, NT * (n - 1) + t + 1)
                A.activation(rstd[0:r, t:t + 1], ssq[0:r, t:t + 1], ACT.Sqrt, scale=1.0 / D,
                             bias=eps[0:r, :]).then_inc(root_ready, 1)

            def copy_transposed(idx, dst, tiles=range(NT)):
                for t in tiles:
                    act.wait_ge(tr_done, 2 * (idx * NT + t) + 1)
                    A.activation(dst[:, 0:4, col[t]:col[t] + rows[t]],
                                 pb[2][:, :].rearrange("p (c t) -> p c t", c=4)[:, :, 0:rows[t]],
                                 ACT.Copy).then_inc(tr_act, 1)

            act.wait_ge(x_loaded, 16 * NT)
            act.wait_ge(c_ready, 1)
            for t in range(NT):
                square_root(1, t)
            act.wait_ge(consts, 1)
            A.dma_start(LF[:, TP:TP + CT, :], cache_logf[0].rearrange("(t p) h -> p t h", p=P)).then_inc(clogf_loaded, 16)
            for grp in range(3):
                store_ada(grp)
                load_bias(grp + 2)
            act.wait_ge(h_ready, NT)
            A.dma_start(pool_prompt[0, 0], h[P - PBUF:P, TP - 1, :]).then_inc(hist_stored, 16)
            A.dma_start(pool_sample[0, 0], h[DEC - PBUF:DEC, TS, :]).then_inc(hist_stored, 16)

            def root_of_mixed(t):
                act.wait_ge(mix_added, 2 * t + 2)
                if t == TP - 1:
                    act.wait_ge(hist_stored, 32)
                square_root(2, t)

            for t in range(NT):
                for b in range(2):
                    act.wait_ge(mix_diff, 2 * t + b + 1)
                    if t:
                        act.wait_ge(mix_y, 2 * t)
                    A.activation(diffT[:, 4 * b:4 * b + 4, 0:rows[t]],
                                 pb[2 + b][:, :].rearrange("p (c t) -> p c t", c=4)[:, :, 0:rows[t]],
                                 ACT.Copy).then_inc(mix_diffT, 1)
                if t:
                    root_of_mixed(t - 1)
            root_of_mixed(TS)
            store_ada(3)
            load_bias(5)

            def copy_partials(turn, banks, part):
                act.wait_ge(part_done, turn)
                A.activation(part[:, 0:SEQ], pb[banks[0]][:, :], ACT.Copy).then_inc(part_copied, 1)
                A.activation(part[:, SEQ:TOK], pb[banks[1]][:, 0:DEC], ACT.Copy).then_inc(part_copied, 1)

            def route(layer):
                copy_transposed(6 * layer, hT, (range(NT), range(TP - 1, NT))[layer])
                copy_partials((1, 3)[layer], (4, 5), partT)
                act.wait_ge(l_ready, layer + 1)
                A.activation(sc[:, :, :], L[:, :, :], ACT.Exp).then_inc(exp_ready, 1)

            def experts(layer):
                e0 = layer * NE

                def copy_x(S, i, b, par, with_wait=True):
                    act.wait_ge(S.tx, 2 * i + (2 * b + 1))
                    if with_wait:
                        act.wait_ge(S.up, i + (b - 1))
                    A.activation(xgT[:, par, 0:4, :], pb[0][:, :].rearrange("p (c t) -> p c t", c=4),
                                 ACT.Copy).then_inc(S.xt_act, 1)

                def silu(S, i, b):
                    act.wait_ge(S.gate, i + (b + 1))
                    if not (isinstance(i, int) and i + b == 0):
                        act.wait_ge(S.hact, i + b)
                    A.activation(sg, pb[3][:, :], ACT.Silu).then_inc(S.silu, 1)

                def copy_h(S, i, b):
                    act.wait_ge(S.th, i + (b + 1))
                    A.activation(hactT, pb[2][:, :].rearrange("p (c t) -> p c t", c=KE), ACT.Copy).then_inc(S.hactT, 1)

                def copy_y(S, i, b, par):
                    act.wait_ge(S.down, 2 * i + (2 * b + 1))
                    A.activation(ysb[:, par, 0:512], pb[5][:, :], ACT.Copy).then_inc(S.ys_act, 1)

                def step(i, par, pairs_stored, more=True):
                    e = 2 * i + par
                    silu(E, e, e0)
                    if more:
                        copy_x(E, e + 1, e0, 1 - par, not (isinstance(e, int) and e + e0 == 0))
                    copy_h(E, e, e0)
                    if pairs_stored is not None:
                        act.wait_ge(y_stored[par], pairs_stored)
                    copy_y(E, e, e0, par)

                copy_x(E, 0, e0, 0, layer > 0)
                for par in range(2):
                    step(0, par, 16 * NPE if layer else None)
                with act.Fori(1, NPE - 1) as i:
                    for par in range(2):
                        step(i, par, 16 * i + 16 * NPE * layer)
                step(NPE - 1, 0, 16 * (NPE - 1) + 16 * NPE * layer)
                step(NPE - 1, 1, 16 * (NPE - 1) + 16 * NPE * layer, more=False)
                n_ov = act.value_load(tabi[0:1, NE + 2 * NOV:NE + 2 * NOV + 1], min_val=0, max_val=NOV)
                with act.If(n_ov > 0):
                    with act.Fori(0, n_ov) as j:
                        act.wait_ge(ov_pe[layer], 7 * j + 1)
                        A.activation(xgT[:, 0, 0:4, :], pb[0][:, :].rearrange("p (c t) -> p c t", c=4),
                                     ACT.Copy).then_inc(ov_act[layer], 1)
                        act.wait_ge(ov_pe[layer], 7 * j + 3)
                        A.activation(sg, pb[3][:, :], ACT.Silu).then_inc(ov_act[layer], 1)
                        act.wait_ge(ov_pe[layer], 7 * j + 5)
                        A.activation(hactT, pb[2][:, :].rearrange("p (c t) -> p c t", c=KE),
                                     ACT.Copy).then_inc(ov_act[layer], 1)
                        act.wait_ge(ov_pe[layer], 7 * j + 6)
                        A.activation(ysb[:, 0, 0:512], pb[5][:, :], ACT.Copy).then_inc(ov_act[layer], 1)
                for t in range(NT):
                    act.wait_ge(yg_loaded[t], 32 * (layer + 1))
                    A.activation(yg[0:rows[t], t, 0, :], yg[0:rows[t], t, 0, :], ACT.Copy,
                                 scale=wts[0:rows[t], 0, t:t + 1]).then_inc(yg_scaled, 1)
                    if layer == 0:
                        if t >= 2:
                            copy_transposed(1, hT, [t - 2])
                        if t:
                            act.wait_ge(combined, t)
                            square_root(3, t - 1)

            route(0)
            store_ada(4)
            load_bias(6)
            store_ada(5)
            store_ada(6)
            experts(0)
            act.wait_ge(combined, NT)
            square_root(3, TS)
            copy_transposed(1, hT, [TP - 1])

            def copy_proj(c, dst):
                u, t = divmod(c, NT)
                act.wait_ge(proj_done, c + 1)
                if t < TP:
                    last = A.activation(dst[u // 2][:, t, 512 * (u % 2):512 * (u % 2) + 512], pb[4 + c % 2][:, :], ACT.Copy)
                else:
                    for j in range(4):
                        c0 = 512 * (u % 2) + j * P
                        last = A.activation(dst[u // 2][0:DEC, t, c0:c0 + P], pb[4 + c % 2][32 * j:32 * j + DEC, 0:P], ACT.Copy)
                last.then_inc(proj_act, 1)

            def head_root(src, n, t, last):
                r = rows[t]
                act.wait_ge(proj_act, last // 2 + 1)
                act.wait_ge(proj_dve, (last + 1) // 2)
                if n >= 2:
                    act.wait_ge(qk_ss, n - 1)
                A.activation(mod[0:r, 2, n % 2, :], src[0:r, t, :], ACT.Square).then_inc(qk_sq, 1)
                act.wait_ge(qk_ss, n + 1)
                A.activation(ss[0:r, t, :], ss[0:r, t, :], ACT.Sqrt, scale=1.0 / HD, bias=eps[0:r, :]).then_inc(qk_root, 1)

            def k_root(t):
                head_root(kk, t, t, NT + t)

            def q_root(t):
                head_root(qq, NT + t, t, 5 * NT + t)

            def proj(*cs):
                for c in cs:
                    copy_proj(c, (kk, vv, qq))

            def th(*tiles):
                copy_transposed(2, hT, tiles)

            def tk(*tiles):
                copy_transposed(3, kT, tiles)

            def tq(*tiles):
                copy_transposed(4, qT, tiles)

            proj(0)
            copy_transposed(1, hT, [TS])
            proj(2, 4)
            copy_partials(2, (0, 1), partT_f)
            act.wait_ge(f_abs, 1)
            A.activation(za[:, :, :], za[:, :, :], ACT.Exp, scale=-1.0).then_inc(f_exp, 1)
            act.wait_ge(f_1p, 1)
            A.activation(za[:, :, :], za[:, :, :], ACT.Ln).then_inc(f_ln, 1)
            proj(6, 8)
            k_root(0)
            proj(10)
            k_root(1)
            proj(12)
            k_root(2)
            proj(14)
            k_root(3)
            act.wait_ge(fT_done, 1)
            A.activation(fT[:, 0, :], pb[0][:, 0:P], ACT.Copy, scale=-1.0).then_inc(fT_ready, 1)
            A.activation(fT[0:NF * NH - P, 1, :], pb[0][0:NF * NH - P, P:2 * P], ACT.Copy, scale=-1.0).then_inc(fT_ready, 1)
            act.wait_ge(fT_ready, 2)
            A.dma_start(f_d[0:P, :], fT[:, 0, :]).then_inc(f_stored, 16)
            A.dma_start(f_d[P:NF * NH, :], fT[0:NF * NH - P, 1, :]).then_inc(f_stored, 16)
            k_root(4)
            proj(16)
            th(0, 1)
            proj(18)
            th(2, 3, 4)
            proj(20)
            tk(0, 1)
            proj(22)
            tk(2, 3)
            proj(24)
            tk(4)
            q_root(0)
            proj(26)
            tq(0)
            q_root(1)
            tq(1)
            q_root(2)
            proj(28)
            tq(2)
            q_root(3)
            q_root(4)
            tq(3, 4)

            act.wait_ge(kv_out, 16 * 6)
            NB = 2 * TP
            A.activation(rs[:, 0, 0:1], eps[:, :], ACT.Exp).then_inc(at_o, 1)
            act.wait_ge(at_o, 1)
            with act.Fori(0, NPAIR) as j:
                def expo(n):
                    w = (n % TP + 1) * P
                    act.wait_ge(at_nb, NB * j + n + 1)
                    A.activation(S_sb[:, n % 4, 0:w], S_sb[:, n % 4, 0:w], ACT.Exp, bias=mx[:, n, 2:3],
                                 accum_out=rs[:, n, 0:1]).then_inc(at_exp, 1)

                def out(n):
                    s, b = divmod(n, TP)
                    act.wait_ge(at_pv, NB * j + n + 1)
                    act.wait_ge(at_rinv, NB * j + n + 1)
                    A.activation(oo[:, b, bass.ds(j * 2 * HD + s * HD, HD)], pb[6 + n % 2][:, 0:HD], ACT.Copy,
                                 scale=rs[:, n, 1:2]).then_inc(at_o, 1)

                expo(0)
                expo(1)
                for n in range(NB):
                    if n + 2 < NB:
                        expo(n + 2)
                    if n:
                        out(n - 1)
                out(NB - 1)
            def keys_copied(gi):
                for b in range(2):
                    act.wait_ge(sa_kt, 4 * gi + b + 1)
                    A.activation(kTc[0][:, 512 * b:512 * b + 512], pb[b][:, :], ACT.Copy).then_inc(sa_kte, 1)

            keys_copied(0)
            for gi in range(4):
                act.wait_ge(sa_nb, gi + 1)
                A.activation(Ss, Ss, ACT.Exp, bias=mx[:, 7, 2:3], accum_out=rs[:, 7, 0:1]).then_inc(sa_exp, 1)
                act.wait_ge(sa_t, gi + 1)
                A.activation(PTs[:, 0:4, :], pb[0][:, :].rearrange("p (c t) -> p c t", c=4), ACT.Copy).then_inc(sa_pt, 1)
                if gi < 3:
                    keys_copied(gi + 1)
                act.wait_ge(sa_pv, gi + 1)
                act.wait_ge(sa_rinv, gi + 1)
                for jj in range(2):
                    last = A.activation(oo[0:DEC, TS, bass.ds(gi * 4 * HD + jj * HD, HD)],
                                        pb[7][32 * jj:32 * jj + 32, jj * HD:(jj + 1) * HD], ACT.Copy,
                                        scale=rs[32 * jj:32 * jj + 32, 7, 1:2])
                last.then_inc(sa_o, 1)
            copy_transposed(5, hT)
            for t in range(NT):
                if t >= 3:
                    copy_transposed(6, hT, [t - 3])
                if t == TS:
                    act.wait_ge(a_ready, 5)
                    for u in range(2):
                        act.wait_ge(o_done, 2 * TS + u + 1)
                        for j in range(4):
                            c0 = 512 * u + j * P
                            last = A.activation(o_s[:, c0:c0 + P], pb[4 + u][32 * j:32 * j + DEC, 0:P], ACT.Copy)
                        last.then_inc(o_sample, 1)
                act.wait_ge(o_added, 2 * t + 2)
                square_root(4, t)
            copy_transposed(6, hT, [2])
            route(1)
            experts(1)

        @block.vector
        def _(dve):
            V = nc.vector
            n_chain = [0]

            def link(ins):
                n_chain[0] += 1
                ins.then_inc(chain_v, 1)
                dve.wait_ge(chain_v, n_chain[0])

            link(V.memset(cT[:, :, :], 0.0))
            V.memset(adab[:, :, :], 0.0).then_inc(adab_zero, 1)
            V.memset(cachep, 0.0).then_inc(cachep_zero, 1)
            link(V.memset(eps[:, :], EPS))
            link(V.memset(L[:, :, :], 0.0))
            dve.wait_ge(c_silu, 1)
            V.tensor_copy(cT[:, :, 0:2].rearrange("p k s -> p s k"), csl[:, :, :]).then_inc(c_ready, 1)

            def stage_ada(grp):
                if grp >= 2:
                    dve.wait_ge(ada_stored[grp - 2], 32)
                dve.wait_ge(bias_loaded[grp % 2], 32 * (grp // 2 + 1))
                dve.wait_ge(unit_used, 4 * (grp + 1))
                V.tensor_tensor(stage[:, grp % 2, :], pb[grp % 2][:, :], adab[:, grp % 2, :], ALU.add).then_inc(ada_staged, 1)

            dve.wait_ge(consts, 1)
            link(V.tensor_copy(identb[:, :], ident[:, :]))
            link(V.tensor_reduce(sel[:, :, :], ident[:, :].rearrange("p (j w e) -> p w e j", j=4, w=2), axis=AX.X, op=ALU.add))
            for i, w in enumerate(WINDOWS):
                link(V.tensor_scalar(wtmp[:, :], cnti[:, :], float(w), None, ALU.min))
                link(V.reciprocal(wtmp[:, :], wtmp[:, :]))
                link(V.tensor_tensor(bands[:, 1, i, :], bands[:, 1, i, :], wtmp[:, :], ALU.mult))
                link(V.tensor_tensor(bands[:, 1, i, :], bands[:, 1, i, :], ident[:, :], ALU.subtract))
                ins = V.tensor_tensor(bands[:, 0, i, :], bands[:, 0, i, :], ident[:, :], ALU.subtract)
                if i + 1 < len(WINDOWS):
                    link(ins)
            ins.then_inc(bands_ready, 1)

            def scale_ready(m):
                dve.wait_ge(ab_loaded, 80 * (m + 1))
                V.scalar_tensor_tensor(out=mod[:, 0, 0, :], in0=mod[:, 0, 0, :], scalar=1.0, in1=gainb[:, :],
                                       op0=ALU.add, op1=ALU.mult)
                V.scalar_tensor_tensor(out=mod[0:DEC, 0, 1, :], in0=mod[0:DEC, 0, 1, :], scalar=1.0,
                                       in1=gainb[0:DEC, :], op0=ALU.add, op1=ALU.mult).then_inc(a_ready, 1)
                dve.wait_ge(a_ready, m + 1)

            def norm_tile(m, n_root, t):
                r, s = rows[t], t // TP
                if n_root:
                    dve.wait_ge(root_ready, NT * (n_root - 1) + t + 1)
                    link(V.reciprocal(rstd[0:r, t:t + 1], rstd[0:r, t:t + 1]))
                V.scalar_tensor_tensor(out=h[0:r, t, :], in0=x[0:r, t, :], scalar=rstd[0:r, t:t + 1],
                                       in1=mod[0:r, 0, s, :], op0=ALU.mult, op1=ALU.mult).then_inc(norm_mul, 1)
                dve.wait_ge(norm_mul, NT * m + t + 1)
                V.tensor_tensor(h[0:r, t, :], h[0:r, t, :], mod[0:r, 1, s, :], ALU.add).then_inc(h_ready, 1)

            def copy_transposed(idx, dst, tiles=range(NT)):
                for t in tiles:
                    dve.wait_ge(tr_done, 2 * (idx * NT + t) + 2)
                    V.tensor_copy(dst[:, 4:8, col[t]:col[t] + rows[t]],
                                  pb[3][:, :].rearrange("p (c t) -> p c t", c=4)[:, :, 0:rows[t]]).then_inc(tr_dve, 1)

            stage_ada(0)
            stage_ada(1)
            scale_ready(0)
            for t in range(NT):
                norm_tile(0, 1, t)
            stage_ada(2)
            dve.wait_ge(g_loaded, 48)
            V.tensor_tensor(mod[:, 2, 0, :], mod[:, 2, 0, :], gainb[:, :], ALU.mult)
            V.tensor_tensor(mod[0:DEC, 2, 1, :], mod[0:DEC, 2, 1, :], gainb[0:DEC, :], ALU.mult).then_inc(gp_ready, 1)
            dve.wait_ge(gp_ready, 1)

            def add_half(bank, t, half, done):
                r, s, c = rows[t], t // TP, slice(512 * half, 512 * half + 512)
                link(V.tensor_tensor(bank[0:r, :], bank[0:r, :], mod[0:r, 2, s, c], ALU.mult))
                return V.tensor_tensor(x[0:r, t, c], bank[0:r, :], x[0:r, t, c], ALU.add).then_inc(done, 1)

            for t in range(NT):
                for b in range(2):
                    dve.wait_ge(mix_y, 2 * t + b + 1)
                    add_half(pb[4 + b], t, b, mix_added)
                if t == 2:
                    scale_ready(1)
                if t >= 2:
                    norm_tile(1, 2, t - 2)
            link(V.memset(t5[:, 0, :], 0.0))
            V.memset(t5[:, 1, :], 0.0).then_inc(g_free, 1)
            stage_ada(3)
            for t in range(TP - 1, NT):
                norm_tile(1, 2, t)

            def tt(out, a, b, op):
                link(V.tensor_tensor(out, a, b, op))

            def red(out, a, op=ALU.max):
                link(V.tensor_reduce(out, a, axis=AX.X, op=op))

            def first_max(out, v, m, key, n):
                red(m, v)
                tt(out, v, bc(m, n, 2), ALU.is_equal)
                tt(key, out, bc(desc4[:, :], NT, 1), ALU.mult)
                red(m, key)
                tt(out, key, bc(m, n, 2), ALU.is_equal)

            def pick(layer):
                copy_transposed(6 * layer, hT, (range(NT), range(TP - 1, NT))[layer])
                dve.wait_ge(logits_done, layer + 1)
                V.tensor_copy(L[:, 0:TP, :], pb[6][:, 0:TP * NE].rearrange("p (t e) -> p t e", t=TP))
                link(V.tensor_copy(L[0:DEC, TS, :], pb[6][0:DEC, TP * NE:NT * NE]))
                red(t5[:, 0, :], L[:, :, :])
                V.tensor_tensor(L[:, :, :], L[:, :, :], bc(t5[:, 0, :], NE, 2), ALU.subtract).then_inc(l_ready, 1)
                dve.wait_ge(exp_ready, layer + 1)
                red(t5[:, 1, :], sc[:, :, :], ALU.add)
                link(V.reciprocal(t5[:, 1, :], t5[:, 1, :]))
                tt(sc[:, :, :], sc[:, :, :], bc(t5[:, 1, :], NE, 2), ALU.mult)
                tt(selv[:, :, :], sc[:, :, :], bc(brb[:, :], NT, 1), ALU.add)
                sp4 = selv[:, :, :].rearrange("p t (g a b) -> p (t g) a b", g=NG, a=2)
                tt(pm[:, 0, :, :], sp4[:, :, :, 0], sp4[:, :, :, 1], ALU.max)
                tt(pm[:, 1, :, :], sp4[:, :, :, 0], sp4[:, :, :, 1], ALU.min)
                tt(pm[:, 2, :, 0], pm[:, 0, :, 0], pm[:, 0, :, 1], ALU.max)
                tt(pm[:, 2, :, 1], pm[:, 0, :, 0], pm[:, 0, :, 1], ALU.min)
                tt(pm[:, 3, :, 0], pm[:, 1, :, 0], pm[:, 1, :, 1], ALU.max)
                tt(pm[:, 3, :, 1], pm[:, 2, :, 1], pm[:, 3, :, 0], ALU.max)
                gs = m4[:, 0, :, :]
                tt(gs.rearrange("p t g -> p (t g)"), pm[:, 2, :, 0], pm[:, 3, :, 1], ALU.add)
                first_max(best[:, :, :], gs, t5[:, 2, :], m4[:, 1, :, :], NG)
                b4 = best[:, :, :].unsqueeze(3).to_broadcast([P, NT, NG, EPG])
                g44 = prod[:, :, :].rearrange("p t (g j) -> p t g j", g=NG)
                tt(g44, selv[:, :, :].rearrange("p t (g j) -> p t g j", g=NG), b4, ALU.mult)
                red(vj[:, :, :], prod[:, :, :].rearrange("p t (g j) -> p t j g", g=NG), ALU.add)
                for r in range(2):
                    first_max(one[:, r, :, :], vj[:, :, :], t5[:, 2, :], m4[:, 1, :, :], EPG)
                    if r == 0:
                        link(V.scalar_tensor_tensor(out=vj[:, :, :], in0=one[:, 0, :, :], scalar=-3e38,
                                                    in1=vj[:, :, :], op0=ALU.mult, op1=ALU.add))
                    o4 = oh[:, r, :, :].rearrange("p t (g j) -> p t g j", g=NG)
                    tt(o4, b4, one[:, r, :, :].unsqueeze(2).to_broadcast([P, NT, NG, EPG]), ALU.mult)
                    tt(prod[:, :, :], oh[:, r, :, :], sc[:, :, :], ALU.mult)
                    red(wts[:, r, :], prod[:, :, :], ALU.add)
                    tt(oh[:, r, :, :], oh[:, r, :, :], bc(valid[:, :], NE, 2), ALU.mult)
                V.tensor_tensor(Mb[:, :, :], oh[:, 0, :, :], oh[:, 1, :, :], ALU.add).then_inc(pick_ready, 1)
                tt(t5[:, 3, :], wts[:, 0, :], wts[:, 1, :], ALU.add)
                link(V.reciprocal(t5[:, 3, :], t5[:, 3, :]))
                for r in range(2):
                    tt(wts[:, r, :], wts[:, r, :], t5[:, 3, :], ALU.mult)

            def scan(out, counts):
                link(V.tensor_tensor_scan(out, onesr[:, :], counts, 0.0, ALU.mult, ALU.add))
                tt(out, out, counts, ALU.subtract)

            def places(layer):
                dve.wait_ge(rank_done, layer + 1)
                link(V.tensor_copy(tot[:, :, :], pb[7][:, 128:128 + NT * NE].rearrange("p (t e) -> p t e", t=NT)))
                for t in range(1, NT):
                    tt(tot[:, t, :], tot[:, t, :], tot[:, t - 1, :], ALU.add)
                link(V.tensor_copy(cnt[:, :], tot[:, NT - 1, :]))
                r6 = pb[6][:, 128:128 + NT * NE].rearrange("p (t e) -> p t e", t=NT)
                link(V.tensor_copy(rank[:, 0, :], r6[:, 0, :]))
                tt(rank[:, 1:NT, :], r6[:, 1:NT, :], tot[:, 0:NT - 1, :], ALU.add)
                scan(offs[:, :], cnt[:, :])

                def picked(side, rowsof):
                    for r in range(2):
                        tt(prod[:, :, :], oh[:, r, :, :], rowsof[:, :, :], ALU.mult)
                        red(posf[:, side, r, :], prod[:, :, :], ALU.add)
                    return V.tensor_copy(posi[:, side, :, :], posf[:, side, :, :])

                tt(selv[:, :, :], rank[:, :, :], bc(offs[:, :], NT, 1), ALU.add)
                picked(0, selv).then_inc(rows_ready, 1)
                link(V.tensor_scalar(ovc[:, :], cnt[:, :], float(P), None, ALU.is_gt))
                for m in range(2, -(-TOK // P)):
                    link(V.scalar_tensor_tensor(out=ovc[:, :], in0=cnt[:, :], scalar=float(m * P), in1=ovc[:, :],
                                                op0=ALU.is_gt, op1=ALU.add))
                scan(ovs[:, :], ovc[:, :])
                link(V.tensor_scalar(e16[:, 0, :], iotae[:, :], float(P), None, ALU.mult))
                link(V.tensor_scalar(e16[:, 1, :], ovs[:, :], float(P), float(NE * P - P), ALU.mult, ALU.add))
                tt(e16[:, 1, :], e16[:, 1, :], e16[:, 0, :], ALU.subtract)
                link(V.tensor_scalar(selv[:, :, :], rank[:, :, :], float(P), None, ALU.is_ge))
                tt(selv[:, :, :], selv[:, :, :], bc(e16[:, 1, :], NT, 1), ALU.mult)
                tt(selv[:, :, :], selv[:, :, :], bc(e16[:, 0, :], NT, 1), ALU.add)
                tt(selv[:, :, :], selv[:, :, :], rank[:, :, :], ALU.add)
                link(picked(1, selv))
                one_row = slice(0, 1)
                jj = iotaj[one_row, :].unsqueeze(2).to_broadcast([1, NOV, NE])
                ovs_b = ovs[one_row, :].unsqueeze(1).to_broadcast([1, NOV, NE])
                tt(ind[one_row, 0, :, :], jj, ovs_b, ALU.subtract)
                link(V.tensor_scalar(ind[one_row, 1, :, :], ind[one_row, 0, :, :], 0.0, None, ALU.is_ge))
                tt(ind[one_row, 2, :, :], ind[one_row, 0, :, :],
                   ovc[one_row, :].unsqueeze(1).to_broadcast([1, NOV, NE]), ALU.is_lt)
                tt(ind[one_row, 1, :, :], ind[one_row, 1, :, :], ind[one_row, 2, :, :], ALU.mult)
                link(V.tensor_scalar(ind[one_row, 0, :, :], ind[one_row, 0, :, :], float(P), float(P), ALU.mult, ALU.add))
                tt(ind[one_row, 0, :, :], ind[one_row, 0, :, :],
                   offs[one_row, :].unsqueeze(1).to_broadcast([1, NOV, NE]), ALU.add)
                tt(ind[one_row, 0, :, :], ind[one_row, 0, :, :], ind[one_row, 1, :, :], ALU.mult)
                tt(ind[one_row, 2, :, :], ind[one_row, 1, :, :],
                   iotae[one_row, :].unsqueeze(1).to_broadcast([1, NOV, NE]), ALU.mult)
                red(tabf[one_row, NE:NE + NOV], ind[one_row, 2, :, :], ALU.add)
                red(tabf[one_row, NE + NOV:NE + 2 * NOV], ind[one_row, 0, :, :], ALU.add)
                link(V.tensor_copy(tabf[one_row, 0:NE], offs[one_row, :]))
                red(tabf[one_row, NE + 2 * NOV:NE + 2 * NOV + 1], ovc[one_row, :], ALU.add)
                V.tensor_copy(tabi[one_row, :], tabf[one_row, :]).then_inc(pos_ready, 1)

            def experts(layer):
                e0 = layer * NE

                def copy_x(S, i, b, par, with_wait=True):
                    dve.wait_ge(S.tx, 2 * i + (2 * b + 2))
                    if with_wait:
                        dve.wait_ge(S.up, i + (b - 1))
                    V.tensor_copy(xgT[:, par, 4:8, :], pb[1][:, :].rearrange("p (c t) -> p c t", c=4)).then_inc(S.xt_dve, 1)

                def product(S, i, b):
                    dve.wait_ge(S.silu, i + (b + 1))
                    dve.wait_ge(S.up, i + (b + 1))
                    if not (isinstance(i, int) and i + b == 0):
                        dve.wait_ge(S.th, i + b)
                    V.tensor_tensor(hact, pb[4][:, :], sg, ALU.mult).then_inc(S.hact, 1)

                def copy_y(S, i, b, par):
                    dve.wait_ge(S.down, 2 * i + (2 * b + 2))
                    V.tensor_copy(ysb[:, par, 512:1024], pb[6][:, :]).then_inc(S.ys_dve, 1)

                def step(i, par, pairs_stored, more=True):
                    e = 2 * i + par
                    product(E, e, e0)
                    if more:
                        copy_x(E, e + 1, e0, 1 - par, not (isinstance(e, int) and e + e0 == 0))
                    if pairs_stored is not None:
                        dve.wait_ge(y_stored[par], pairs_stored)
                    copy_y(E, e, e0, par)

                copy_x(E, 0, e0, 0, layer > 0)
                for par in range(2):
                    step(0, par, 16 * NPE if layer else None)
                with dve.Fori(1, NPE - 1) as i:
                    for par in range(2):
                        step(i, par, 16 * i + 16 * NPE * layer)
                step(NPE - 1, 0, 16 * (NPE - 1) + 16 * NPE * layer)
                step(NPE - 1, 1, 16 * (NPE - 1) + 16 * NPE * layer, more=False)
                n_ov = dve.value_load(tabi[0:1, NE + 2 * NOV:NE + 2 * NOV + 1], min_val=0, max_val=NOV)
                with dve.If(n_ov > 0):
                    with dve.Fori(0, n_ov) as j:
                        dve.wait_ge(ov_pe[layer], 7 * j + 2)
                        V.tensor_copy(xgT[:, 0, 4:8, :], pb[1][:, :].rearrange("p (c t) -> p c t", c=4)).then_inc(
                            ov_dve[layer], 1)
                        dve.wait_ge(ov_act[layer], 4 * j + 2)
                        dve.wait_ge(ov_pe[layer], 7 * j + 4)
                        V.tensor_tensor(hact, pb[4][:, :], sg, ALU.mult).then_inc(ov_dve[layer], 1)
                        dve.wait_ge(ov_pe[layer], 7 * j + 7)
                        V.tensor_copy(ysb[:, 0, 512:1024], pb[6][:, :]).then_inc(ov_dve[layer], 1)
                dve.wait_ge(g_loaded, (80, 144)[layer])
                if layer == 0:
                    scale_ready(2)
                for t in range(NT):
                    r, s = rows[t], t // TP
                    dve.wait_ge(yg_scaled, NT * layer + t + 1)
                    y0, y1 = yg[0:r, t, 0, :], yg[0:r, t, 1, :]
                    link(V.scalar_tensor_tensor(out=y0, in0=y1, scalar=wts[0:r, 1, t:t + 1], in1=y0,
                                                op0=ALU.mult, op1=ALU.add))
                    link(V.tensor_tensor(y0, y0, mod[0:r, 2, s, :], ALU.mult))
                    V.tensor_tensor(x[0:r, t, :], x[0:r, t, :], y0, ALU.add).then_inc(combined, 1)
                    if layer == 0 and t >= 2:
                        copy_transposed(1, hT, [t - 2])
                    if layer == 0 and t:
                        norm_tile(2, 3, t - 1)

            pick(0)
            places(0)
            stage_ada(4)
            stage_ada(5)
            stage_ada(6)
            experts(0)
            link(V.memset(t5[:, 0, :], 0.0))
            V.memset(t5[:, 1, :], 0.0).then_inc(g_free, 1)

            norm_tile(2, 3, TS)
            copy_transposed(1, hT, [TP - 1])

            def copy_proj(c):
                u, t = divmod(c, NT)
                dve.wait_ge(proj_done, c + 1)
                dst = (kk, vv, qq)[u // 2]
                if t < TP:
                    last = V.tensor_copy(dst[:, t, 512 * (u % 2):512 * (u % 2) + 512], pb[4 + c % 2][:, :])
                else:
                    for j in range(4):
                        c0 = 512 * (u % 2) + j * P
                        last = V.tensor_copy(dst[0:DEC, t, c0:c0 + P], pb[4 + c % 2][32 * j:32 * j + DEC, 0:P])
                last.then_inc(proj_dve, 1)

            def head_norm(src, gain, n, t):
                r = rows[t]
                dve.wait_ge(qk_sq, n + 1)
                V.tensor_reduce(ss[0:r, t, :], mod[0:r, 2, n % 2, :].rearrange("p (h d) -> p h d", h=NH),
                                axis=AX.X, op=ALU.add).then_inc(qk_ss, 1)
                dve.wait_ge(qk_root, n + 1)
                link(V.reciprocal(ss[0:r, t, :], ss[0:r, t, :]))
                v = src[0:r, t, :].rearrange("p (h d) -> p h d", h=NH)
                link(V.tensor_tensor(v, v, bc(ss[0:r, t, :], HD, 2), ALU.mult))
                V.tensor_tensor(v, v, bc(gain[0:r, :], NH, 1), ALU.mult).then_inc(qk_ready, 1)

            def proj(*cs):
                for c in cs:
                    copy_proj(c)

            def k_heads(t):
                head_norm(kk, knb, t, t)

            def q_heads(t):
                head_norm(qq, qnb, NT + t, t)

            def th(*tiles):
                copy_transposed(2, hT, tiles)

            def tk(*tiles):
                copy_transposed(3, kT, tiles)

            def tq(*tiles):
                copy_transposed(4, qT, tiles)

            proj(1)
            copy_transposed(1, hT, [TS])
            proj(3)
            link(V.memset(z[:, :, :], 0.0))
            dve.wait_ge(f_done, 1)
            zp = pb[6][:, 0:NT * NH].rearrange("p (t e) -> p t e", t=NT)
            V.tensor_tensor(z[:, 0:TP, :], zp[:, 0:TP, :], bc(bfb[:, :], TP, 1), ALU.add)
            link(V.tensor_tensor(z[0:DEC, TS, :], zp[0:DEC, TS, :], bfb[0:DEC, :], ALU.add))
            V.scalar_tensor_tensor(out=za[:, :, :], in0=z[:, :, :], scalar=-1.0, in1=z[:, :, :],
                                   op0=ALU.mult, op1=ALU.max).then_inc(f_abs, 1)
            dve.wait_ge(f_exp, 1)
            V.tensor_scalar(za[:, :, :], za[:, :, :], 1.0, None, ALU.add).then_inc(f_1p, 1)
            dve.wait_ge(f_ln, 1)
            dve.wait_ge(clogf_loaded, 16)
            V.scalar_tensor_tensor(out=LF[0:DEC, NF - 1, :], in0=z[0:DEC, TS, :], scalar=0.0, in1=za[0:DEC, TS, :],
                                   op0=ALU.min, op1=ALU.subtract)
            V.scalar_tensor_tensor(out=LF[:, 0:TP, :], in0=z[:, 0:TP, :], scalar=0.0, in1=za[:, 0:TP, :],
                                   op0=ALU.min, op1=ALU.subtract).then_inc(lf_ready, 1)
            proj(5)
            scale_ready(3)
            norm_tile(3, 0, 0)
            proj(7)
            norm_tile(3, 0, 1)
            norm_tile(3, 0, 2)
            proj(9)
            norm_tile(3, 0, 3)
            norm_tile(3, 0, 4)
            dve.wait_ge(csum_done, 1)
            link(V.tensor_copy(tF[:, :, :], pb[7][:, 0:NF * NH].rearrange("p (t n) -> p t n", t=NF)))
            for t in range(1, TP - 1):
                tt(tF[:, t, :], tF[:, t, :], tF[:, t - 1, :], ALU.add)
            for t in range(TP + 1, NF - 1):
                tt(tF[:, t, :], tF[:, t, :], tF[:, t - 1, :], ALU.add)
            c6 = pb[6][:, 0:NF * NH].rearrange("p (t n) -> p t n", t=NF)
            link(V.tensor_copy(Fs[:, 0, :], c6[:, 0, :]))
            link(V.tensor_copy(Fs[:, TP, :], c6[:, TP, :]))
            tt(Fs[:, 1:TP, :], c6[:, 1:TP, :], tF[:, 0:TP - 1, :], ALU.add)
            V.tensor_tensor(Fs[:, TP + 1:NF, :], c6[:, TP + 1:NF, :], tF[:, TP:NF - 1, :], ALU.add).then_inc(F_ready, 1)
            k_heads(0)
            k_heads(1)
            proj(11)
            k_heads(2)
            proj(13)
            k_heads(3)
            k_heads(4)
            proj(15)
            th(0)
            proj(17)
            th(1, 2)
            proj(19)
            th(3, 4)
            tk(0)
            proj(21)
            tk(1, 2)
            proj(23)
            tk(3, 4)
            proj(25)
            q_heads(0)
            tq(0)
            q_heads(1)
            proj(27)
            tq(1)
            q_heads(2)
            tq(2)
            q_heads(3)
            proj(29)
            q_heads(4)
            tq(3, 4)
            dve.wait_ge(ada_stored[6], 32)
            link(V.memset(qz, 0.0))
            link(V.memset(qbd[:, :, :, :], 0.0))
            dve.wait_ge(tr_act, NT * 5)
            for s in range(2):
                link(V.tensor_scalar(qbd[64 * s:64 * s + 64, :, s, :], qT[64 * s:64 * s + 64, :, SEQ:TOK], SCALE, None, ALU.mult))
            for jj in range(4):
                link(V.tensor_copy(fqs[32 * jj:32 * jj + 32, :], Fs[0:DEC, NF - 1, jj:NH:4]))
            NB = 2 * TP
            with dve.Fori(0, NPAIR) as j:
                for s in range(2):
                    q = slice(64 * s, 64 * s + 64)
                    V.tensor_scalar(qz[q, s, :], qT[q, bass.ds(j, 1), 0:SEQ].rearrange("p o t -> p (o t)"),
                                    SCALE, None, ALU.mult).then_inc(at_q, 1)

                def add(n):
                    s, b = divmod(n, TP)
                    w = (b + 1) * P
                    if n % TP == 0:
                        dve.wait_ge(at_nf, 2 * j + s + 1)
                    if n >= 4:
                        dve.wait_ge(at_t, NB * j + n - 3)
                    dve.wait_ge(at_s, NB * j + n + 1)
                    dve.sem_inc(passed_dve, 1)
                    V.tensor_tensor_reduce(out=S_sb[:, n % 4, 0:w], in0=pb[n % 4][:, 0:w], in1=nfh[:, s, 0:w], scale=1.0,
                                           scalar=-3e38, op0=ALU.add, op1=ALU.max,
                                           accum_out=mx[:, n, 0:1]).then_inc(at_add, 1)
                    dve.wait_ge(at_add, NB * j + n + 1)
                    fq = Fs[:, b, bass.ds(j * 2 + s, 1)]
                    V.scalar_tensor_tensor(out=mx[:, n, 2:3], in0=mx[:, n, 0:1], scalar=fq, in1=fq, op0=ALU.add,
                                           op1=ALU.subtract, reverse1=True).then_inc(at_nb, 1)

                def rest(n):
                    w = (n % TP + 1) * P
                    dve.wait_ge(at_exp, NB * j + n + 1)
                    V.reciprocal(rs[:, n, 1:2], rs[:, n, 0:1]).then_inc(at_rinv, 1)
                    dve.wait_ge(at_t, NB * j + n + 1)
                    if n >= 2:
                        dve.wait_ge(at_pv, NB * j + n - 1)
                    V.tensor_copy(PT[:, n % 2, 0:w], pb[4 + n % 2][:, 0:w]).then_inc(at_pt, 1)

                add(0)
                add(1)
                for n in range(NB):
                    if n + 2 < NB:
                        add(n + 2)
                    rest(n)
            def keys_copied(gi):
                V.tensor_copy(kns, kT[:, bass.ds(2 * gi, 2), SEQ:TOK])
                V.tensor_copy(qbs, qbd[:, bass.ds(2 * gi, 2), :, :].rearrange("p j a b -> p j (a b)")).then_inc(sa_q, 1)
                for b in range(2):
                    dve.wait_ge(sa_kt, 4 * gi + 3 + b)
                    V.tensor_copy(kTc[1][:, 512 * b:512 * b + 512], pb[2 + b][:, :]).then_inc(sa_kte, 1)

            keys_copied(0)
            for gi in range(4):
                par, gp = gi % 2, gi // 2
                k = [0]

                def link_s(ins):
                    k[0] += 1
                    ins.then_inc(sa_chain, 1)
                    dve.wait_ge(sa_chain, 4 * gi + k[0])

                dve.wait_ge(sa_loaded[par], 80 * gp + 80)
                link_s(V.tensor_tensor(bias_s[par][:, PAST:SK], bias_s[par][:, PAST:SK], smask[:, :], ALU.add))
                dve.wait_ge(sa_s, gi + 1)
                dve.sem_inc(passed_dve, 1)
                for b, (c0, c1) in enumerate(((0, 512), (512, PAST), (PAST, SK))):
                    ins = V.tensor_tensor_reduce(out=Ss[:, c0:c1], in0=pb[4 + b][:, 0:c1 - c0], in1=bias_s[par][:, c0:c1],
                                                 scale=1.0, scalar=-3e38, op0=ALU.add, op1=ALU.max,
                                                 accum_out=mx[:, b, 0:1])
                link_s(ins)
                link_s(V.tensor_reduce(mx[:, 7, 0:1], mx[:, 0:3, 0], axis=AX.X, op=ALU.max))
                fq = fqs[:, bass.ds(gi, 1)]
                link_s(V.tensor_tensor(mx[:, 7, 1:2], mx[:, 7, 0:1], fq, ALU.add))
                V.tensor_tensor(mx[:, 7, 2:3], fq, mx[:, 7, 1:2], ALU.subtract).then_inc(sa_nb, 1)
                dve.wait_ge(sa_exp, gi + 1)
                V.reciprocal(rs[:, 7, 1:2], rs[:, 7, 0:1]).then_inc(sa_rinv, 1)
                dve.wait_ge(sa_t, gi + 1)
                V.tensor_copy(PTs[:, 4:8, :], pb[1][:, :].rearrange("p (c t) -> p c t", c=4)).then_inc(sa_pt, 1)
                V.tensor_copy(PTs[0:DEC, CT, :], pb[2][0:DEC, 0:P]).then_inc(sa_pt, 1)
                if gi < 3:
                    keys_copied(gi + 1)
                dve.wait_ge(sa_pv, gi + 1)
                dve.wait_ge(sa_rinv, gi + 1)
                for jj in range(2, 4):
                    last = V.tensor_scalar(oo[0:DEC, TS, bass.ds(gi * 4 * HD + jj * HD, HD)],
                                           pb[7][32 * jj:32 * jj + 32, jj * HD:(jj + 1) * HD],
                                           rs[32 * jj:32 * jj + 32, 7, 1:2], None, ALU.mult)
                last.then_inc(sa_o, 1)
            copy_transposed(5, hT)
            dve.wait_ge(g_loaded, 112)
            scale_ready(4)
            for t in range(NT):
                for u in range(2):
                    if t < TS:
                        dve.wait_ge(o_done, 2 * t + u + 1)
                        add_half(pb[4 + u], t, u, o_added)
                        continue
                    dve.wait_ge(o_sample, u + 1)
                    c = slice(512 * u, 512 * u + 512)
                    link(V.tensor_tensor(o_s[:, c], o_s[:, c], mod[0:DEC, 2, 1, c], ALU.mult))
                    V.tensor_tensor(x[0:DEC, t, c], o_s[:, c], x[0:DEC, t, c], ALU.add).then_inc(o_added, 1)
                if t >= 3:
                    copy_transposed(6, hT, [t - 3])
                if t:
                    norm_tile(4, 4, t - 1)
            link(V.memset(t5[:, 0, :], 0.0))
            V.memset(t5[:, 1, :], 0.0).then_inc(g_free, 1)
            copy_transposed(6, hT, [2])
            norm_tile(4, 4, TS)
            pick(1)
            places(1)
            experts(1)


_INS = ['x_prompt', 'x_sample', 'cache_pool', 'cache_k', 'cache_v', 'cache_logf', 'c_prompt', 'c_sample',
        'ada_w', 'ada_b', 'norm_g', 'w_pool', 'pool_scale', 'kv_ada_w', 'kv_ada_b', 'kv_norm', 'w_kvf', 'b_f',
        'k_norm', 'w_q', 'q_norm', 'w_o', 'w_router', 'b_router', 'w_gate', 'w_up', 'w_down']


def kernel(**inputs):
    import numpy as _np
    import concourse.bacc as _bacc
    from concourse import mybir as _mybir
    from concourse.bass_utils import run_bass_kernel_spmd as _run

    nc = _bacc.Bacc("TRN2", target_bir_lowering=False, num_devices=1)
    arrays, args, shape = {}, [], {}
    for name in _INS:
        a = _np.ascontiguousarray(inputs[name])
        arrays[f"in_{name}_dram"] = a
        shape[name] = a.shape
        args.append(nc.dram_tensor(f"in_{name}_dram", a.shape, _mybir.dt.from_np(a.dtype), kind="ExternalInput").ap())
    B, S, D = shape['x_prompt']
    BD, SD, _ = shape['x_sample']
    LA, _, PB, _ = shape['cache_pool']
    H, HD = shape['cache_k'][2:]
    outs = [(B, S, D), (BD, SD, D), (LA, B, PB, D), (B, S, H, HD), (B, S, H, HD), (B, S, H),
            (LA, BD, PB, D), (BD, SD, H, HD), (BD, SD, H, HD), (BD, SD, H)]
    for i, s in enumerate(outs):
        args.append(nc.dram_tensor(f"out_{i}_dram", s, _mybir.dt.float32, kind="ExternalOutput").ap())
    bass_yoco_stream_step(nc, *args)
    r = _run(nc, [arrays], core_ids=[0])
    return tuple(r.results[0][f"out_{i}_dram"] for i in range(len(outs)))
```
